# Optimizing a Trainium2 kernel written in Bass

```python
import jax, jax.numpy as jnp
from jax import lax
import numpy as np

D_MODEL = 1024
BATCH = 1
SEQ = 512
DEPTH = 1

N_MEM = 256
EPS = 1e-6
D_RNN = D_MODEL
LRU_BLOCKS = 8
LRU_BLOCK = D_RNN // LRU_BLOCKS
LRU_C = 8.0
CONV_W = 4
FOX_HEADS = 8
FOX_HEAD_DIM = D_MODEL // FOX_HEADS
D_FOX = FOX_HEADS * FOX_HEAD_DIM
Q_BLOCK = 128
MEM_HEADS = 4
MEM_HEAD_DIM = D_MODEL // MEM_HEADS
D_MEMATT = MEM_HEADS * MEM_HEAD_DIM
N_BRANCH = 3
D_FF = 4 * D_MODEL
OFF_LRU = 0
OFF_Q = OFF_LRU + D_RNN
OFF_K = OFF_Q + D_FOX
OFF_V = OFF_K + D_FOX
OFF_MQ = OFF_V + D_FOX
OFF_GATE = OFF_MQ + D_MEMATT
OFF_F = OFF_GATE + N_BRANCH * D_MODEL
N_IN = OFF_F + FOX_HEADS

kernel_name = 'hybrid_rglru_fox_memory_block'

def rms_norm(x, g):
    xf = x.astype(jnp.float32)
    y = xf * lax.rsqrt(jnp.mean(xf * xf, axis=-1, keepdims=True) + EPS)
    return (y * g.astype(jnp.float32)).astype(x.dtype)

def causal_depthwise_conv(x, w, b):
    y = lax.conv_general_dilated(x, w[:, None, :].astype(x.dtype), window_strides=(1,),
                                 padding=[(CONV_W - 1, 0)], dimension_numbers=('NWC', 'WIO', 'NWC'),
                                 feature_group_count=x.shape[-1])
    return y + b.astype(x.dtype)

def _linear_recurrence_combine(left, right):
    a_l, b_l = left
    a_r, b_r = right
    return a_l * a_r, a_r * b_l + b_r

def rg_lru(x, w_r, b_r, w_i, b_i, lam):
    bsz, s, c = x.shape
    xb = x.reshape(bsz, s, LRU_BLOCKS, LRU_BLOCK)
    r = jax.nn.sigmoid((jnp.einsum('bshi,hij->bshj', xb, w_r) + b_r).astype(jnp.float32)).reshape(bsz, s, c)
    i = jax.nn.sigmoid((jnp.einsum('bshi,hij->bshj', xb, w_i) + b_i).astype(jnp.float32)).reshape(bsz, s, c)
    log_a = -LRU_C * r * jax.nn.softplus(-lam.astype(jnp.float32))
    a = jnp.exp(log_a)
    gated_x = jnp.sqrt(-jnp.expm1(2.0 * log_a)) * i * x.astype(jnp.float32)
    _, h = lax.associative_scan(_linear_recurrence_combine, (a, gated_x), axis=1)
    return h.astype(x.dtype)

def forgetting_attention(q, k, v, log_f):
    bsz, s, nh, dh = q.shape
    nb = s // Q_BLOCK
    c = jnp.cumsum(log_f, axis=1).transpose(0, 2, 1)
    q_blocks = q.reshape(bsz, nb, Q_BLOCK, nh, dh).transpose(1, 0, 2, 3, 4)
    c_blocks = c.reshape(bsz, nh, nb, Q_BLOCK).transpose(2, 0, 1, 3)
    k_pos = jnp.arange(s)
    scale = dh ** -0.5

    def one_block(args):
        q_blk, c_blk, blk_idx = args
        logits = jnp.einsum('bqhd,bkhd->bhqk', q_blk, k, preferred_element_type=jnp.float32) * scale
        logits = logits + c_blk[..., :, None] - c[:, :, None, :]
        q_pos = blk_idx * Q_BLOCK + jnp.arange(Q_BLOCK)
        logits = jnp.where(k_pos[None, :] <= q_pos[:, None], logits, -jnp.inf)
        p = jax.nn.softmax(logits, axis=-1)
        return jnp.einsum('bhqk,bkhd->bqhd', p.astype(v.dtype), v)

    out = lax.map(one_block, (q_blocks, c_blocks, jnp.arange(nb)))
    return out.transpose(1, 0, 2, 3, 4).reshape(bsz, s, nh, dh)

def memory_attention(q, mem_k, mem_v):
    scale = q.shape[-1] ** -0.5
    logits = jnp.einsum('bshd,bmhd->bhsm', q, mem_k, preferred_element_type=jnp.float32) * scale
    p = jax.nn.softmax(logits, axis=-1)
    return jnp.einsum('bhsm,bmhd->bshd', p.astype(mem_v.dtype), mem_v)

def mixer_sublayer(h, mem, g_pre, w_in, conv_w, conv_b, w_r, b_r, w_i, b_i, lam, b_f,
                   g_mem, w_mem_kv, b_gate, w_pa, w_pb, w_pc, w_o, g_post):
    bsz, s, _ = h.shape
    n_mem = mem.shape[1]
    u = rms_norm(h, g_pre)
    z = u @ w_in
    y_a = rg_lru(causal_depthwise_conv(z[..., OFF_LRU:OFF_LRU + D_RNN], conv_w, conv_b),
                 w_r, b_r, w_i, b_i, lam)
    q = z[..., OFF_Q:OFF_Q + D_FOX].reshape(bsz, s, FOX_HEADS, FOX_HEAD_DIM)
    k = z[..., OFF_K:OFF_K + D_FOX].reshape(bsz, s, FOX_HEADS, FOX_HEAD_DIM)
    v = z[..., OFF_V:OFF_V + D_FOX].reshape(bsz, s, FOX_HEADS, FOX_HEAD_DIM)
    log_f = jax.nn.log_sigmoid(z[..., OFF_F:OFF_F + FOX_HEADS].astype(jnp.float32) + b_f.astype(jnp.float32))
    y_b = forgetting_attention(q, k, v, log_f).reshape(bsz, s, D_FOX)
    kv = rms_norm(mem, g_mem) @ w_mem_kv
    mem_k = kv[..., :D_MEMATT].reshape(bsz, n_mem, MEM_HEADS, MEM_HEAD_DIM)
    mem_v = kv[..., D_MEMATT:].reshape(bsz, n_mem, MEM_HEADS, MEM_HEAD_DIM)
    mq = z[..., OFF_MQ:OFF_MQ + D_MEMATT].reshape(bsz, s, MEM_HEADS, MEM_HEAD_DIM)
    y_c = memory_attention(mq, mem_k, mem_v).reshape(bsz, s, D_MEMATT)
    gates = jax.nn.sigmoid(z[..., OFF_GATE:OFF_GATE + N_BRANCH * D_MODEL].reshape(bsz, s, N_BRANCH, D_MODEL) + b_gate)
    merged = (gates[:, :, 0] * (y_a @ w_pa) + gates[:, :, 1] * (y_b @ w_pb)
              + gates[:, :, 2] * (y_c @ w_pc))
    return h + rms_norm(merged @ w_o, g_post)

def mlp_sublayer(h, g_pre, w_up, w_down, g_post):
    u = rms_norm(h, g_pre)
    act = jnp.square(jax.nn.relu(u @ w_up))
    return h + rms_norm(act @ w_down, g_post)

def setup_inputs(seed: int = 0) -> dict:
    key = jax.random.key(seed)
    ks = jax.random.split(key, 26)
    f32 = jnp.float32

    def nrm(k, shape, fan_in):
        return jax.random.normal(k, shape, f32) * (fan_in ** -0.5)

    def gain(k):
        return 1.0 + 0.02 * jax.random.normal(k, (DEPTH, D_MODEL), f32)

    def small(k, shape):
        return 0.01 * jax.random.normal(k, shape, f32)

    a_c = jax.random.uniform(ks[8], (DEPTH, D_RNN), f32, minval=0.9, maxval=0.999)
    a0 = a_c ** (1.0 / LRU_C)
    lru_lambda = jnp.log(a0) - jnp.log1p(-a0)
    return {
        'x': jax.random.normal(ks[0], (BATCH, SEQ, D_MODEL), f32),
        'mem': jax.random.normal(ks[1], (BATCH, N_MEM, D_MODEL), f32),
        'g_mix_pre': gain(ks[2]),
        'w_in': nrm(ks[3], (DEPTH, D_MODEL, N_IN), D_MODEL),
        'conv_w': nrm(ks[4], (DEPTH, CONV_W, D_RNN), CONV_W),
        'conv_b': small(ks[5], (DEPTH, D_RNN)),
        'w_r': nrm(ks[6], (DEPTH, LRU_BLOCKS, LRU_BLOCK, LRU_BLOCK), LRU_BLOCK),
        'b_r': small(ks[7], (DEPTH, LRU_BLOCKS, LRU_BLOCK)),
        'w_i': nrm(ks[9], (DEPTH, LRU_BLOCKS, LRU_BLOCK, LRU_BLOCK), LRU_BLOCK),
        'b_i': small(ks[10], (DEPTH, LRU_BLOCKS, LRU_BLOCK)),
        'lru_lambda': lru_lambda,
        'b_f': jax.random.uniform(ks[11], (DEPTH, FOX_HEADS), f32, minval=1.0, maxval=6.0),
        'g_mem': gain(ks[12]),
        'w_mem_kv': nrm(ks[13], (DEPTH, D_MODEL, 2 * D_MEMATT), D_MODEL),
        'b_gate': small(ks[14], (DEPTH, N_BRANCH, D_MODEL)),
        'w_pa': nrm(ks[15], (DEPTH, D_RNN, D_MODEL), D_RNN),
        'w_pb': nrm(ks[16], (DEPTH, D_FOX, D_MODEL), D_FOX),
        'w_pc': nrm(ks[17], (DEPTH, D_MEMATT, D_MODEL), D_MEMATT),
        'w_o': nrm(ks[18], (DEPTH, D_MODEL, D_MODEL), D_MODEL),
        'g_mix_post': gain(ks[19]),
        'g_mlp_pre': gain(ks[20]),
        'w_up': nrm(ks[21], (DEPTH, D_MODEL, D_FF), D_MODEL),
        'w_down': nrm(ks[22], (DEPTH, D_FF, D_MODEL), D_FF),
        'g_mlp_post': gain(ks[23]),
    }

def reference(x, mem, g_mix_pre, w_in, conv_w, conv_b, w_r, b_r, w_i, b_i, lru_lambda, b_f,
              g_mem, w_mem_kv, b_gate, w_pa, w_pb, w_pc, w_o, g_mix_post,
              g_mlp_pre, w_up, w_down, g_mlp_post):
    h = x
    for l in range(DEPTH):
        h = mixer_sublayer(h, mem, g_mix_pre[l], w_in[l], conv_w[l], conv_b[l], w_r[l], b_r[l],
                           w_i[l], b_i[l], lru_lambda[l], b_f[l], g_mem[l], w_mem_kv[l], b_gate[l],
                           w_pa[l], w_pb[l], w_pc[l], w_o[l], g_mix_post[l])
        h = mlp_sublayer(h, g_mlp_pre[l], w_up[l], w_down[l], g_mlp_post[l])
    return h


_drawn_inputs = setup_inputs


def setup_inputs(seed=0):
    import zlib

    import numpy as np

    out = dict(_drawn_inputs(seed))
    spreads = {}
    factors = {'g_mix_pre': 3.254,
     'b_r': 64.0,
     'b_i': 64.0,
     'g_mem': 8.0,
     'b_gate': 24.585,
     'g_mix_post': 10.343,
     'g_mlp_pre': 43.203,
     'g_mlp_post': 61.891,
     'conv_b': 8.0}
    for name, (base, spread) in spreads.items():
        noise = np.random.default_rng([zlib.crc32(name.encode()), seed]).standard_normal(out[name].shape)
        drawn = base * np.exp(spread * noise) if base else spread * noise
        out[name] = __import__('jax').numpy.asarray(drawn.astype(out[name].dtype))
    for name, factor in factors.items():
        out[name] = (out[name] * factor).astype(out[name].dtype)
    return out
```

```python
from contextlib import ExitStack

import numpy as np
import concourse.bass as bass
from concourse import mybir

F32 = mybir.dt.float32
F32R = mybir.dt.float32r
ALU = mybir.AluOpType
ACT = mybir.ActivationFunctionType
AX = mybir.AxisListType

P = 128
T = 512
NT = T // P
D = 1024
KD = D // P
NM = 256
MT = NM // P
FOX_HEADS = 8
MEM_HEADS = 4
CONV_W = 4
EPS = 1e-6
LRU_C = 8.0
FF = 4 * D
OFF_Q, OFF_K, OFF_V, OFF_MQ = D, 2 * D, 3 * D, 4 * D
OFF_GATE = 5 * D
OFF_F = 8 * D
N_IN = OFF_F + FOX_HEADS
FOX_SCALE = float(D // FOX_HEADS) ** -0.5
MEM_SCALE = float(D // MEM_HEADS) ** -0.5
MASKED = -1e30
BIG = 3e38
F_ROW = P - FOX_HEADS
F_Q = 96
LOG1P_TERMS = (1 / 15, 1 / 13, 1 / 11, 1 / 9, 1 / 7, 1 / 5, 1 / 3)
SLOTS = 4

PHASES = {
    "mem_k": ((0, 1, 2, 3), 2),
    "mem_v": ((0, 1, 2, 3, 0, 1, 2, 3, 2), 1),
    "mem_att": ((0, 1, 2, 3), 2),
    "lru": ((0, 1, 2), 8),
    "merge_a": ((0, 1, 2, 3), 4),
    "fox": ((0, 1, 2, 0, 1, 2), 4),
    "merge_b": ((0, 1, 2, 3), 4),
    "w_o": ((0, 1, 2, 3, 0, 1, 2, 3), 1),
    "mlp": ((0, 1, 2, 3) * 4, 4),
}


class Units:

    def __init__(self):
        self.base, self.uses, self.first = {}, {}, {}
        n, use, last = 0, [0] * SLOTS, [None] * SLOTS
        for name, (slots, iters) in PHASES.items():
            self.base[name], self.uses[name] = n, list(use)
            self.first[name] = [None if x is None else x - n for x in last]
            for i in range(iters):
                for s, slot in enumerate(slots):
                    use[slot] += 1
                    last[slot] = n
                    n += 1

    def slot(self, phase, s):
        slots = PHASES[phase][0]
        return slots[s % len(slots)]

    def count(self, phase, i, s):
        return i * len(PHASES[phase][0]) + (self.base[phase] + s + 1)

    def loaded(self, phase, i, s):
        slots = PHASES[phase][0]
        s_in, more = s % len(slots), s // len(slots)
        per = slots.count(slots[s_in])
        nth = slots[:s_in].count(slots[s_in]) + 1
        return i * (16 * per) + 16 * (self.uses[phase][slots[s_in]] + more * per + nth)

    def before(self, phase, i, s):
        slots = PHASES[phase][0]
        size = len(slots)
        slot = slots[s % size]
        for back in range(s - 1, -1, -1):
            if slots[back % size] == slot:
                return i * size + (self.base[phase] + back + 1)
        earlier = self.first[phase][slot]
        if isinstance(i, int) and i == 0:
            return None if earlier is None else self.base[phase] + earlier + 1
        wrapped = s - 1
        while slots[wrapped % size] != slot:
            wrapped -= 1
        if earlier is not None:
            wrapped = max(wrapped, earlier)
        return i * size + (self.base[phase] + wrapped + 1)


class From1:

    def __init__(self, n):
        self.n = n

    def __mul__(self, m):
        return self.n * m + (-m)


class Chain:

    def __init__(self, eng, sem):
        self.eng, self.sem, self.n, self.i, self.per = eng, sem, 0, None, 0

    def __call__(self, ins):
        self.n += 1
        ins.then_inc(self.sem, 1)
        self.eng.wait_ge(self.sem, self.n if self.i is None else self.i * self.per + self.n)

    def enter(self, i, per):
        self.i, self.per, self.start = i, per, self.n

    def leave(self, iters):
        assert self.n - self.start == self.per, (self.n - self.start, self.per)
        self.n = self.start + self.per * iters
        self.i = None


def block_program(nc, x, mem, g_mix_pre, w_in, conv_w, conv_b, w_r, b_r, w_i, b_i, lru_lambda,
                  b_f, g_mem, w_mem_kv, b_gate, w_pa, w_pb, w_pc, w_o, g_mix_post, g_mlp_pre,
                  w_up, w_down, g_mlp_post, out):
    ctx = ExitStack()
    units = Units()
    KB = 1024
    with ctx:
        ctx.enter_context(nc.allow_non_contiguous_dma("small parameter columns"))
        base = -(-nc.sbuf_base // 32) * 32
        ctx.enter_context(nc.sbuf_tensor("arena", [P, 207 * 256], F32))

        def at(name, kib, shape, dt=F32):
            return nc.alloc_sbuf_tensor_at(name, [P] + shape, dt, offset=base + int(kib * KB))

        def sem(name):
            return ctx.enter_context(nc.semaphore(name))

        RING, RAW, UT, Y0, Y1, E, MG, TMP, CONST = 0, 32, 48, 80, 112, 144, 168, 184, 204
        ring = at("ring", RING, [SLOTS, 2, D], F32R)
        raw = at("raw", RAW, [SLOTS, D])
        uT = at("uT", UT, [2, KD, T], F32R)
        yc = at("yc", Y0, [2, KD, T], F32R)
        ya = at("ya", Y1, [2, KD, T], F32R)
        yb = at("yb", Y0, [2, KD, T], F32R)
        mgT = at("mgT", Y1, [2, KD, T], F32R)
        merged = at("merged", MG, [KD, T])
        x_in = at("x_in", MG, [NT, D])
        mem_in = at("mem_in", TMP, [MT, D])
        square_out = at("square_out", TMP + 8, [D])
        g_mem_all = at("g_mem_all", Y0, [D])
        g_mix_all = at("g_mix_all", Y0 + 4, [D])
        memT = at("memT", Y1, [2, KD, NM], F32R)
        mem_k = at("mem_k", Y1 + 16, [2, KD, NM], F32R)
        mem_v = at("mem_v", E, [2, MT, D], F32R)
        f_z = at("f_z", MG, [T])
        f_e = at("f_e", MG + 2, [T])
        f_s = at("f_s", MG + 4, [T])
        f_y = at("f_y", MG + 6, [T])
        f_p = at("f_p", MG + 8, [T])
        f_ones = at("f_ones", MG + 10, [T])
        f_neg_c = at("f_neg_c", MG + 12, [T])
        f_c = at("f_c", MG + 14, [T])
        mq = at("mq", Y1, [4, 2, T], F32R)
        mem_pT = at("mem_pT", E + 16, [2, MT, T], F32R)
        mem_p = at("mem_p", TMP, [2, NT, NM])
        mem_vh = at("mem_vh", TMP + 8, [2, 2, MT, NM], F32R)
        xcT = at("xcT", E, [2, T], F32R)
        w_ri = at("w_ri", E + 4, [2, 2, P], F32R)
        z_pad = at("z_pad", TMP, [T + 8])
        xc = at("xc", TMP + 2.5, [T])
        l_r = at("l_r", TMP + 4.5, [T])
        l_i = at("l_i", TMP + 6.5, [T])
        l_t = at("l_t", TMP + 8.5, [T])
        l_a = at("l_a", TMP + 10.5, [T])
        l_m = at("l_m", TMP + 12.5, [T])
        l_h = at("l_h", TMP + 14.5, [T])
        w_ri_raw = at("w_ri_raw", TMP + 16.5, [2, P])
        gate = at("gate", E + 12, [2, T])
        prod = at("prod", E + 16, [2, T])
        qk = at("qk", Y1, [4, 2, T], F32R)
        v_h = at("v_h", Y1 + 16, [2, NT, P], F32R)
        ROW = [P * t * (t + 1) // 2 for t in range(NT + 1)]
        COL = [P * (NT * j - j * (j - 1) // 2) for j in range(NT + 1)]
        fox_pT = at("fox_pT", E, [2, ROW[NT]], F32R)
        fox_p = at("fox_p", TMP, [2, ROW[NT]])
        v_f = at("v_f", TMP + 10, [T])
        c_all = at("c_all", TMP + 12, [2, T])
        h1 = at("h1", TMP, [NT, D])
        g_post_all = at("g_post_all", E, [D])
        g_pre2_all = at("g_pre2_all", E + 4, [D])
        g_post2_all = at("g_post2_all", E + 8, [D])
        normed = at("normed", E + 12, [D])
        square_out2 = at("square_out2", E + 20, [D])
        u2 = at("u2", Y0, [NT, D])
        u2T = at("u2T", UT, [2, KD, T], F32R)
        actT = at("actT", Y0, [2, KD, T], F32R)
        relu = at("relu", E + 12, [2, T])
        relu2 = at("relu2", E + 16, [2, T])
        down_sum = at("down_sum", MG, [NT, D])
        ident = at("ident", CONST, [P])
        identR = at("identR", CONST + 0.5, [P], F32R)
        mask = at("mask", CONST + 1, [P])
        maskR = at("maskR", CONST + 1.5, [P], F32R)
        col = at("col", CONST + 2, [27, 8])
        stat = at("stat", CONST + 2.875, [4, 8])
        f_col = at("f_col", TMP + 18, [8])
        CW, CB, BR, BI, LAM, BG, NQ, SP = 0, 4, 5, 6, 7, 8, 11, 15
        rows = at("rows", CONST + 3, [8, 4])

        ps = ctx.enter_context(nc.psum_tensor("ps", [P, 8, T], F32))
        c_dram = nc.dram_tensor("c_scratch", [2, FOX_HEADS, T], F32, kind="Internal").ap()

        slot_loaded = [sem(f"slot_loaded{s}") for s in range(SLOTS)]
        hi_done, lo_done, unit_used = sem("hi_done"), sem("lo_done"), sem("unit_used")
        act_link, dve_link, pool_link = sem("act_link"), sem("dve_link"), sem("pool_link")
        mem_landed = sem("mem_landed")
        x_landed = [sem(f"x_landed{t}") for t in range(NT)]
        g_mem_landed, g_mix_landed = sem("g_mem_landed"), sem("g_mix_landed")
        cols_landed, consts_ready = sem("cols_landed"), sem("consts_ready")
        consts_rounded = sem("consts_rounded")
        norm_sum, norm_var, norm_std = sem("norm_sum"), sem("norm_var"), sem("norm_std")
        normed_ready, turned, turned_hi, turned_lo = (
            sem("normed_ready"), sem("turned"), sem("turned_hi"), sem("turned_lo"))
        mem_k_hi, mem_k_lo = sem("mem_k_hi"), sem("mem_k_lo")
        mem_v_done, mem_v_hi, mem_v_lo = sem("mem_v_done"), sem("mem_v_hi"), sem("mem_v_lo")
        f_read, f_abs, f_exp, f_c_ready = sem("f_read"), sem("f_abs"), sem("f_exp"), sem("f_c_ready")
        c_stored, c_cols_landed = sem("c_stored"), sem("c_cols_landed")
        lam_abs, lam_exp, pads_zeroed = sem("lam_abs"), sem("lam_exp"), sem("pads_zeroed")
        mq_hi, mq_lo = sem("mq_hi"), sem("mq_lo")
        ms_done, ms_max, ms_exp, ms_p = sem("ms_done"), sem("ms_max"), sem("ms_exp"), sem("ms_p")
        mt_done, mt_hi, mt_lo, mem_vh_ready = (
            sem("mt_done"), sem("mt_hi"), sem("mt_lo"), sem("mem_vh_ready"))
        yc_done, yc_hi, yc_lo = sem("yc_done"), sem("yc_hi"), sem("yc_lo")
        wri_landed, wri_hi, wri_lo = sem("wri_landed"), sem("wri_hi"), sem("wri_lo")
        z_copied, xc_ready, xc_hi, xc_lo = (
            sem("z_copied"), sem("xc_ready"), sem("xc_hi"), sem("xc_lo"))
        ri_done, lru_tanh, lru_i, lru_a, lru_m2, lru_m, lru_h, ya_lo = (
            sem("ri_done"), sem("lru_tanh"), sem("lru_i"), sem("lru_a"), sem("lru_m2"),
            sem("lru_m"), sem("lru_h"), sem("ya_lo"))
        ya_hi = sem("ya_hi")
        br = {}
        for b in "cab":
            br[b] = {n: sem(f"{n}_{b}") for n in ("gate_ready", "merged_done")}
        mg_hi, mg_lo = sem("mg_hi"), sem("mg_lo")
        qk_hi, qk_lo = sem("qk_hi"), sem("qk_lo")
        v_copied, vt_done, vt_hi, vt_lo = (
            sem("v_copied"), sem("vt_done"), sem("vt_hi"), sem("vt_lo"))
        fs_done, fs_read, fs_min, fs_exp, fs_p = (
            sem("fs_done"), sem("fs_read"), sem("fs_min"), sem("fs_exp"), sem("fs_p"))
        ft_done, ft_hi, ft_lo = sem("ft_done"), sem("ft_hi"), sem("ft_lo")
        yb_done, yb_hi, yb_lo = sem("yb_done"), sem("yb_hi"), sem("yb_lo")
        c_landed = [sem("c_landed_a"), sem("c_landed_b")]
        gains2_landed, x2_landed = sem("gains2_landed"), sem("x2_landed")
        wo_done = sem("wo_done")
        n2_sum, n2_var, n2_std, h1_ready, n3_sum, n3_var, n3_std, u2_ready = (
            sem("n2_sum"), sem("n2_var"), sem("n2_std"), sem("h1_ready"), sem("n3_sum"),
            sem("n3_var"), sem("n3_std"), sem("u2_ready"))
        u2_turned, u2_hi, pair_free = sem("u2_turned"), sem("u2_hi"), sem("pair_free")
        sums_zeroed = sem("sums_zeroed")
        up_relu, up_sq, up_hi, act_ready, down_done = (
            sem("up_relu"), sem("up_sq"), sem("up_hi"), sem("act_ready"),
            sem("down_done"))
        n4_in, n4_sum, n4_var, n4_std, y_ready, stored = (
            sem("n4_in"), sem("n4_sum"), sem("n4_var"), sem("n4_std"), sem("y_ready"), sem("stored"))

        block = ctx.enter_context(nc.Block())

        w_in_v = w_in.rearrange("o (k p) n -> p (o k) n", p=P)
        w_kv_v = w_mem_kv.rearrange("o (k p) n -> p (o k) n", p=P)
        w_up_v = w_up.rearrange("o (k p) n -> p (o k) n", p=P)
        proj_v = {"a": w_pa.rearrange("o (k p) n -> p (o k) n", p=P),
                  "b": w_pb.rearrange("o (k p) n -> p (o k) n", p=P),
                  "c": w_pc.rearrange("o (k p) n -> p (o k) n", p=P)}
        w_o_v = w_o.rearrange("o (k p) n -> p (o k) n", p=P)
        w_down_v = w_down.rearrange("o (k p) n -> p (o k) n", p=P)
        x_v = x.rearrange("o (t p) d -> p (o t) d", p=P)
        out_v = out.rearrange("o (t p) d -> p (o t) d", p=P)
        GATE_OFF = {"a": OFF_GATE, "b": OFF_GATE + D, "c": OFF_GATE + 2 * D}

        @block.sync
        def _(sp):
            def cols(view, start):
                return view[:, :, bass.ds(start, P)]

            def load(phase, i, s, src):
                slot = units.slot(phase, s)
                used = units.before(phase, i, s)
                if used is not None:
                    sp.wait_ge(lo_done, used)
                dst = raw[:, slot]
                if len(src.shape) == 3 and src.shape[1] == KD:
                    dst = dst.rearrange("p (k n) -> p k n", k=KD)
                    return sp.dma_start(dst, src).then_inc(slot_loaded[slot], 16)
                return sp.dma_start(dst, src).then_inc(slot_loaded[slot], 16)

            sp.dma_start(mem_in[:], mem.rearrange("o (t p) d -> p (o t) d", p=P)).then_inc(mem_landed, 16)
            sp.dma_start(g_mem_all[:], g_mem.partition_broadcast(P)[:, 0]).then_inc(g_mem_landed, 16)
            for m in range(KD):
                load("mem_k", m // 4, m % 4, cols(w_kv_v, m * P))
                if m == 0:
                    for t in range(NT):
                        sp.dma_start(x_in[:, t], x_v[:, t]).then_inc(x_landed[t], 16)
            for k in range(KD):
                load("mem_v", 0, k, w_kv_v[:, k, D:2 * D])
            load("mem_v", 0, KD, cols(w_in_v, N_IN - P))
            with sp.Fori(0, 2) as i:
                for s in range(4):
                    load("mem_att", i, s, cols(w_in_v, i * (4 * P) + (OFF_MQ + s * P)))
            def lru_loads(i):
                load("lru", i, 0, cols(w_in_v, i * P))
                load("lru", i, 1, cols(w_in_v, i * P + GATE_OFF["c"]))
                load("lru", i, 2, cols(proj_v["c"], i * P))

            wri_v = [w.rearrange("o h i j -> i (o h) j") for w in (w_r, w_i)]
            lru_loads(0)
            sp.wait_ge(yc_lo, KD)
            for g in range(2):
                sp.dma_start(w_ri_raw[:, g], wri_v[g][:, 0]).then_inc(wri_landed, 16)
            with sp.Fori(1, KD) as i:
                lru_loads(i)
                sp.wait_ge(wri_lo, i)
                for g in range(2):
                    sp.dma_start(w_ri_raw[:, g], wri_v[g][:, bass.ds(i, 1)]).then_inc(wri_landed, 16)

            def merge_loads(phase, b):
                with sp.Fori(1, KD // 2 + 1) as n:
                    i = From1(n)
                    for s in range(2):
                        load(phase, i, 2 * s, cols(w_in_v, i * (2 * P) + (GATE_OFF[b] + s * P)))
                        load(phase, i, 2 * s + 1, cols(proj_v[b], i * (2 * P) + s * P))

            merge_loads("merge_a", "a")
            with sp.Fori(0, FOX_HEADS // 2) as i:
                for s, off in enumerate((OFF_Q, OFF_K, OFF_Q + P, OFF_K + P, OFF_V, OFF_V + P)):
                    load("fox", i, s, cols(w_in_v, i * (2 * P) + off))
            merge_loads("merge_b", "b")
            for k in range(KD):
                load("w_o", 0, k, w_o_v[:, k])
            with sp.Fori(1, 5) as n:
                i = From1(n)
                for s in range(8):
                    load("mlp", i, s, cols(w_up_v, i * D + s * P))
                for s in range(8):
                    load("mlp", i, 8 + s, w_down_v[:, bass.ds(i * KD + s, 1)])
            for t in range(NT):
                sp.wait_ge(y_ready, t + 1)
                sp.dma_start(out_v[:, t], down_sum[:, t]).then_inc(stored, 16)
            sp.wait_ge(stored, 16 * NT)

        @block.gpsimd
        def _(pool):
            link = Chain(pool, pool_link)
            link(nc.gpsimd.memset(ident[:], 0.0))
            link(nc.gpsimd.memset(mask[:], 0.0))
            nc.gpsimd.affine_select(out=ident[:], in_=ident[:], compare_op=ALU.not_equal, fill=1.0,
                                    base=0, pattern=[[-1, P]], channel_multiplier=1).then_inc(consts_ready, 1)
            nc.gpsimd.affine_select(out=mask[:], in_=mask[:], compare_op=ALU.is_ge, fill=MASKED,
                                    base=0, pattern=[[-1, P]], channel_multiplier=1).then_inc(consts_ready, 1)
            pool.dma_start(g_mix_all[:], g_mix_pre.partition_broadcast(P)[:, 0]).then_inc(g_mix_landed, 16)
            link(nc.gpsimd.memset(f_col[:], 0.0))
            for w in range(CONV_W):
                pool.dma_start(col[:, CW + w], conv_w[0, w].rearrange("(j p) -> p j", p=P)).then_inc(cols_landed, 16)
            pool.dma_start(col[:, CB], conv_b[0].rearrange("(j p) -> p j", p=P)).then_inc(cols_landed, 16)
            pool.dma_start(col[:, BR], b_r[0].rearrange("j p -> p j")).then_inc(cols_landed, 16)
            pool.dma_start(col[:, BI], b_i[0].rearrange("j p -> p j")).then_inc(cols_landed, 16)
            pool.dma_start(col[:, LAM], lru_lambda[0].rearrange("(j p) -> p j", p=P)).then_inc(cols_landed, 16)
            for b in range(3):
                pool.dma_start(col[:, BG + b], b_gate[0, b].rearrange("(j p) -> p j", p=P)).then_inc(cols_landed, 16)
            pool.dma_start(f_col[F_ROW:P, 0:1], b_f.rearrange("o h -> h o")).then_inc(cols_landed, 16)
            pool.wait_ge(f_c_ready, 1)
            pool.dma_start(c_dram[0], f_neg_c[F_ROW:P, :]).then_inc(c_stored, 16)
            pool.dma_start(c_dram[1], f_c[F_ROW:P, :]).then_inc(c_stored, 16)
            pool.wait_ge(c_stored, 32)
            for t in range(NT):
                pool.dma_start(col[:, NQ + t], c_dram[0, :, t * P:(t + 1) * P].rearrange("h p -> p h")).then_inc(c_cols_landed, 16)
            pool.wait_ge(br["a"]["merged_done"], KD)
            for n in range(2):
                pool.dma_start(c_all[:, n], c_dram[1, n:n + 1].partition_broadcast(P)[:, 0]).then_inc(c_landed[n], 16)
            with pool.Fori(0, FOX_HEADS // 2 - 1) as i:
                for n in range(2):
                    pool.wait_ge(fs_min, i * 8 + 4 * (n + 1))
                    pool.dma_start(c_all[:, n], c_dram[1, bass.ds(i * 2 + (n + 2), 1)].partition_broadcast(P)[:, 0]).then_inc(c_landed[n], 16)
            pool.wait_ge(yb_lo, FOX_HEADS)
            for g, dst in ((g_mix_post, g_post_all), (g_mlp_pre, g_pre2_all), (g_mlp_post, g_post2_all)):
                pool.dma_start(dst[:], g.partition_broadcast(P)[:, 0]).then_inc(gains2_landed, 16)
            pool.dma_start(h1[:], x_v).then_inc(x2_landed, 16)
            pool.wait_ge(mg_lo, KD)
            nc.gpsimd.memset(down_sum[:], 0.0).then_inc(sums_zeroed, 1)

        @block.scalar
        def _(act):
            A = nc.scalar.activation

            def split(phase, i, s):
                slot = units.slot(phase, s)
                act.wait_ge(slot_loaded[slot], units.loaded(phase, i, s))
                used = units.before(phase, i, s)
                if used is not None:
                    act.wait_ge(unit_used, used)
                A(ring[:, slot, 0], raw[:, slot], ACT.Copy).then_inc(hi_done, 1)

            def evac(ready, value, dst, src, done):
                act.wait_ge(ready, value)
                A(dst, src, ACT.Copy).then_inc(done, 1)

            act.wait_ge(mem_landed, 16)
            for t in range(MT):
                if t:
                    act.wait_ge(norm_sum, t)
                A(square_out[:], mem_in[:, t], ACT.Square, accum_out=stat[:, 0, t:t + 1]).then_inc(norm_sum, 1)
            act.wait_ge(norm_var, 1)
            A(stat[:, 2, 0:MT], stat[:, 1, 0:MT], ACT.Sqrt).then_inc(norm_std, 1)
            split("mem_k", 0, 0)
            split("mem_k", 0, 1)
            for t in range(MT):
                evac(turned, t + 1, memT[:, 0, :, t * P:(t + 1) * P],
                     ps[:, 2 * t:2 * t + 2].rearrange("p b (k n) -> p (b k) n", n=P), turned_hi)
            for t in range(NT):
                act.wait_ge(x_landed[t], 16)
                act.wait_ge(norm_sum, MT + t)
                A(square_out[:], x_in[:, t], ACT.Square, accum_out=stat[:, 0, MT + t:MT + t + 1]).then_inc(norm_sum, 1)
            act.wait_ge(norm_var, 2)
            A(stat[:, 2, MT:MT + NT], stat[:, 1, MT:MT + NT], ACT.Sqrt).then_inc(norm_std, 1)
            for m in range(KD):
                split("mem_k", 0, m + 2)
                evac(unit_used, units.count("mem_k", 0, m), mem_k[:, 0, m], ps[:, 4 + m % 4, 0:NM], mem_k_hi)

            def x_turned(t):
                evac(turned, MT + t + 1, uT[:, 0, :, t * P:(t + 1) * P],
                     ps[:, 2 * (t % 2):2 * (t % 2) + 2].rearrange("p b (k n) -> p (b k) n", n=P), turned_hi)

            for s in range(KD + 1):
                if s == 0:
                    x_turned(0)
                split("mem_v", 0, s + 2)
                if s == 0:
                    x_turned(1)
                if s == 3:
                    x_turned(2)
                if s == 5:
                    x_turned(3)
                if s == KD - 1:
                    for j in range(MT):
                        evac(*((mem_v_done, 1) if j == 0 else (unit_used, units.count("mem_v", 0, KD - 1))), mem_v[:, 0, j],
                             ps[:, 4 + 2 * j:6 + 2 * j].rearrange("p b n -> p (b n)"), mem_v_hi)
            act.wait_ge(lam_abs, 1)
            A(col[:, SP + 2], col[:, SP + 1], ACT.Exp, scale=-1.0).then_inc(lam_exp, 1)
            act.wait_ge(unit_used, units.count("mem_v", 0, KD))
            A(f_z[F_Q:P], ps[F_Q:P, 0], ACT.Identity, bias=f_col[F_Q:P, 0:1]).then_inc(f_read, 1)
            act.wait_ge(f_abs, 1)
            A(f_e[F_Q:P], f_e[F_Q:P], ACT.Exp, scale=-1.0).then_inc(f_exp, 1)

            with act.Fori(0, 2) as i:
                def mem_exp(n):
                    act.wait_ge(ms_max, i * 2 + n + 1)
                    for t in range(NT):
                        A(mem_p[:, n, t], ps[:, 2 * n + t // 2, (t % 2) * NM:(t % 2 + 1) * NM], ACT.Exp,
                          bias=rows[:, 4 * n + 1, t:t + 1], scale=MEM_SCALE,
                          accum_out=rows[:, 4 * n + 2, t:t + 1]).then_inc(ms_exp, 1)

                def mem_turned(n):
                    for j in range(MT):
                        evac(mt_done, i * 4 + 2 * n + j + 1, mem_pT[:, 0, j], ps[:, 4 + 2 * n + j], mt_hi)

                def mem_out(n):
                    for f in range(2):
                        evac(yc_done, i * 4 + 2 * n + f + 1, yc[:, 0, bass.ds(i * 4 + (2 * n + f), 1)],
                             ps[:, 2 * n + f:2 * n + f + 1], yc_hi)

                for s in range(4):
                    split("mem_att", i, s + 2)
                    evac(unit_used, units.count("mem_att", i, s), mq[:, s, 0], ps[:, 4 + s], mq_hi)
                    if s == 2:
                        mem_exp(0)
                mem_turned(0)
                mem_exp(1)
                mem_out(0)
                mem_turned(1)
                mem_out(1)

            with act.Fori(0, KD) as i:
                one = bass.ds(i, 1)
                split("lru", i, 2)
                act.wait_ge(unit_used, units.count("lru", i, 0))
                A(z_pad[:, CONV_W - 1:CONV_W - 1 + T], ps[:, 0], ACT.Copy).then_inc(z_copied, 1)
                split("lru", i, 3)
                act.wait_ge(wri_landed, i * 32 + 32)
                A(w_ri[:, 0], w_ri_raw[:], ACT.Copy).then_inc(wri_hi, 1)
                act.wait_ge(xc_ready, i + 1)
                A(xcT[:, 0], xc[:], ACT.Copy).then_inc(xc_hi, 1)
                act.wait_ge(unit_used, units.count("lru", i, 1))
                A(gate[:, 0], ps[:, 1], ACT.Sigmoid, bias=col[:, BG + 2, one]).then_inc(br["c"]["gate_ready"], 1)
                split("lru", i, 4)
                act.wait_ge(ri_done, i * 2 + 1)
                A(l_r[:], ps[:, 2], ACT.Sigmoid, bias=col[:, BR, one]).then_inc(act_link, 1)
                act.wait_ge(ri_done, i * 2 + 2)
                A(l_i[:], ps[:, 3], ACT.Sigmoid, bias=col[:, BI, one]).then_inc(lru_i, 1)
                act.wait_ge(act_link, i + 1)
                A(l_t[:], l_r[:], ACT.Tanh, scale=col[:, SP, one]).then_inc(lru_tanh, 1)
                A(l_a[:], l_r[:], ACT.Exp, scale=col[:, SP + 7, one]).then_inc(lru_a, 1)
                act.wait_ge(lru_m2, i + 1)
                A(l_m[:], l_m[:], ACT.Sqrt).then_inc(lru_m, 1)
                evac(lru_h, i + 1, ya[:, 0, one], l_h[:].rearrange("p (o t) -> p o t", o=1), ya_hi)

            def merge(phase, b, banks, last):
                with act.Fori(0, KD // 2) as i:
                    for s in range(2):
                        split(phase, i, 2 * s + 2)
                        act.wait_ge(unit_used, units.count(phase, i, 2 * s))
                        A(gate[:, s], ps[:, banks[2 * s]], ACT.Sigmoid,
                          bias=col[:, BG + "abc".index(b), bass.ds(i * 2 + s, 1)]).then_inc(br[b]["gate_ready"], 1)
                        split(phase, i, 2 * s + 3)
                        if last:
                            evac(br[b]["merged_done"], i * 2 + s + 1, mgT[:, 0, bass.ds(i * 2 + s, 1)],
                                 merged[:, bass.ds(i * 2 + s, 1)], mg_hi)

            act.wait_ge(br["c"]["merged_done"], KD)
            merge("merge_a", "a", (5, 6, 7, 0), False)

            act.wait_ge(c_cols_landed, 16 * NT)
            with act.Fori(0, FOX_HEADS // 2) as i:
                def scores(n):
                    for t in range(NT):
                        act.wait_ge(fs_done, i * 8 + 4 * n + t + 1)
                        A(fox_p[:, n, ROW[t]:ROW[t + 1]], ps[:, 2 + t, 0:(t + 1) * P], ACT.Identity,
                          bias=col[:, NQ + t, bass.ds(i * 2 + n, 1)], scale=-FOX_SCALE).then_inc(fs_read, 1)

                def exps(n):
                    for t in range(NT):
                        act.wait_ge(fs_min, i * 8 + 4 * n + t + 1)
                        p = fox_p[:, n, ROW[t]:ROW[t + 1]]
                        A(p, p, ACT.Exp, bias=rows[:, 4 * n, t:t + 1], scale=-1.0,
                          accum_out=rows[:, 4 * n + 2, t:t + 1]).then_inc(fs_exp, 1)

                def turned_p(n):
                    for j in range(NT):
                        evac(ft_done, i * 8 + 4 * n + j + 1, fox_pT[:, 0, COL[j]:COL[j + 1]],
                             ps[:, 6 + j % 2, 0:(NT - j) * P], ft_hi)

                def value(n, bank):
                    act.wait_ge(unit_used, units.count("fox", i, 4 + n))
                    A(v_f[:], ps[:, bank], ACT.Copy).then_inc(v_copied, 1)

                for s in range(4):
                    split("fox", i, s + 2)
                    evac(unit_used, units.count("fox", i, s), qk[:, s, 0], ps[:, s % 2], qk_hi)
                scores(0)
                exps(0)
                split("fox", i, 6)
                value(0, 0)
                scores(1)
                evac(vt_done, i * 2 + 1, v_h[:, 0], ps[:, 1].rearrange("p (j n) -> p j n", n=P), vt_hi)
                turned_p(0)
                exps(1)
                split("fox", i, 7)
                evac(yb_done, i * 2 + 1, yb[:, 0, bass.ds(i * 2, 1)], ps[:, 0:1], yb_hi)
                value(1, 1)
                evac(vt_done, i * 2 + 2, v_h[:, 0], ps[:, 0].rearrange("p (j n) -> p j n", n=P), vt_hi)
                turned_p(1)
                evac(yb_done, i * 2 + 2, yb[:, 0, bass.ds(i * 2 + 1, 1)], ps[:, 2:3], yb_hi)

            merge("merge_b", "b", (2, 3, 4, 5), True)

            for s in range(KD):
                split("w_o", 0, s + 2)
            for t in range(NT):
                if t < NT - 1:
                    act.wait_ge(wo_done, t + 1)
                else:
                    act.wait_ge(unit_used, units.count("w_o", 0, KD - 1))
                if t:
                    act.wait_ge(n3_sum, t)
                A(square_out2[:], ps[:, 2 * t:2 * t + 2].rearrange("p b n -> p (b n)"), ACT.Square,
                  accum_out=stat[:, 0, t:t + 1]).then_inc(n2_sum, 1)
                act.wait_ge(n2_var, t + 1)
                A(stat[:, 2, t:t + 1], stat[:, 1, t:t + 1], ACT.Sqrt).then_inc(n2_std, 1)
                act.wait_ge(h1_ready, t + 1)
                act.wait_ge(n2_sum, t + 1)
                A(square_out2[:], h1[:, t], ACT.Square, accum_out=stat[:, 0, 4 + t:5 + t]).then_inc(n3_sum, 1)
                act.wait_ge(n3_var, t + 1)
                A(stat[:, 2, 4 + t:5 + t], stat[:, 1, 4 + t:5 + t], ACT.Sqrt).then_inc(n3_std, 1)
                evac(u2_turned, t + 1, u2T[:, 0, :, t * P:(t + 1) * P],
                     ps[:, 2 * t:2 * t + 2].rearrange("p b (k n) -> p (b k) n", n=P), u2_hi)

            def mlp(i, final):
                for s in range(8):
                    split("mlp", i, s + 2)
                    act.wait_ge(unit_used, units.count("mlp", i, s))
                    A(relu[:, s % 2], ps[:, s], ACT.Relu).then_inc(up_relu, 1)
                    evac(up_sq, i * 8 + s + 1, actT[:, 0, s], relu2[:, s % 2], up_hi)
                for s in range(8, 16):
                    if not (final and s >= 14):
                        split("mlp", i, s + 2)

            with act.Fori(0, 3) as i:
                mlp(i, False)
            mlp(3, True)
            for t in range(NT):
                act.wait_ge(n4_in, t + 1)
                if t:
                    act.wait_ge(n4_sum, t)
                A(square_out2[:], down_sum[:, t], ACT.Square, accum_out=stat[:, 0, t:t + 1]).then_inc(n4_sum, 1)
                act.wait_ge(n4_var, t + 1)
                A(stat[:, 2, t:t + 1], stat[:, 1, t:t + 1], ACT.Sqrt).then_inc(n4_std, 1)

        @block.vector
        def _(dve):
            V = nc.vector
            link = Chain(dve, dve_link)

            def split(phase, i, s):
                slot = units.slot(phase, s)
                dve.wait_ge(hi_done, units.count(phase, i, s))
                V.tensor_tensor(ring[:, slot, 1], raw[:, slot], ring[:, slot, 0].bitcast(F32),
                                ALU.subtract).then_inc(lo_done, 1)

            def evac(hi_sem, value, dst, src, hi, done):
                dve.wait_ge(hi_sem, value)
                V.tensor_tensor(dst, src, hi.bitcast(F32), ALU.subtract).then_inc(done, 1)

            def log1p(e, s, y, p):
                link(V.tensor_scalar_add(s, e, 2.0))
                link(V.reciprocal(y, s))
                link(V.tensor_tensor(s, e, y, ALU.mult))
                link(V.tensor_tensor(y, s, s, ALU.mult))
                link(V.tensor_scalar(p, y, LOG1P_TERMS[0], None, ALU.mult))
                for term in LOG1P_TERMS[1:]:
                    link(V.scalar_tensor_tensor(out=p, in0=p, scalar=term, in1=y, op0=ALU.add, op1=ALU.mult))
                link(V.scalar_tensor_tensor(out=p, in0=p, scalar=1.0, in1=s, op0=ALU.add, op1=ALU.mult))
                link(V.tensor_scalar(p, p, 2.0, None, ALU.mult))

            def variance(sums, value, lo, hi, done):
                dve.wait_ge(sums, value)
                V.tensor_scalar(stat[:, 1, lo:hi], stat[:, 0, lo:hi], 1.0 / D, EPS, ALU.mult, ALU.add).then_inc(done, 1)

            def rstd(stds, value, lo, hi):
                dve.wait_ge(stds, value)
                link(V.reciprocal(stat[:, 3, lo:hi], stat[:, 2, lo:hi]))

            variance(norm_sum, MT, 0, MT, norm_var)
            rstd(norm_std, 1, 0, MT)
            dve.wait_ge(g_mem_landed, 16)
            for t in range(MT):
                V.scalar_tensor_tensor(out=mem_in[:, t], in0=mem_in[:, t], scalar=stat[:, 3, t:t + 1],
                                       in1=g_mem_all[:], op0=ALU.mult, op1=ALU.mult).then_inc(normed_ready, 1)
            dve.wait_ge(consts_ready, 2)
            V.tensor_copy(identR[:], ident[:]).then_inc(consts_rounded, 1)
            V.tensor_copy(maskR[:], mask[:]).then_inc(consts_rounded, 1)
            split("mem_k", 0, 0)
            split("mem_k", 0, 1)

            def turned_to(dst, n, t, bank):
                evac(turned_hi, n + 1, dst[:, 1, :, t * P:(t + 1) * P],
                     ps[:, bank:bank + 2].rearrange("p b (k n) -> p (b k) n", n=P),
                     dst[:, 0, :, t * P:(t + 1) * P], turned_lo)

            for t in range(MT):
                turned_to(memT, t, t, 2 * t)
            variance(norm_sum, MT + NT, MT, MT + NT, norm_var)
            rstd(norm_std, 2, MT, MT + NT)
            dve.wait_ge(g_mix_landed, 16)
            for t in range(NT):
                V.scalar_tensor_tensor(out=x_in[:, t], in0=x_in[:, t], scalar=stat[:, 3, MT + t:MT + t + 1],
                                       in1=g_mix_all[:], op0=ALU.mult, op1=ALU.mult).then_inc(normed_ready, 1)
            for m in range(KD):
                split("mem_k", 0, m + 2)
                evac(mem_k_hi, m + 1, mem_k[:, 1, m], ps[:, 4 + m % 4, 0:NM], mem_k[:, 0, m], mem_k_lo)
            for s in range(KD + 1):
                if s == 0:
                    turned_to(uT, MT, 0, 0)
                split("mem_v", 0, s + 2)
                if s == 0:
                    turned_to(uT, MT + 1, 1, 2)
                if s == 3:
                    turned_to(uT, MT + 2, 2, 0)
                if s == 5:
                    turned_to(uT, MT + 3, 3, 2)
                if s == KD - 1:
                    for j in range(MT):
                        evac(mem_v_hi, j + 1, mem_v[:, 1, j],
                             ps[:, 4 + 2 * j:6 + 2 * j].rearrange("p b n -> p (b n)"), mem_v[:, 0, j], mem_v_lo)
            dve.wait_ge(cols_landed, 16 * 12)
            V.scalar_tensor_tensor(out=col[:, SP + 1], in0=col[:, LAM], scalar=-1.0, in1=col[:, LAM],
                                   op0=ALU.mult, op1=ALU.max).then_inc(lam_abs, 1)
            dve.wait_ge(lam_exp, 1)
            log1p(col[:, SP + 2], col[:, SP + 3], col[:, SP + 4], col[:, SP + 5])
            link(V.tensor_scalar(col[:, SP + 6], col[:, LAM], -1.0, 0.0, ALU.mult, ALU.max))
            link(V.tensor_tensor(col[:, SP + 6], col[:, SP + 6], col[:, SP + 5], ALU.add))
            link(V.tensor_scalar(col[:, SP], col[:, SP + 6], LRU_C, None, ALU.mult))
            link(V.tensor_scalar(col[:, SP + 7], col[:, SP + 6], -LRU_C, None, ALU.mult))
            q = slice(F_Q, P)
            dve.wait_ge(f_read, 1)
            V.scalar_tensor_tensor(out=f_e[q], in0=f_z[q], scalar=-1.0, in1=f_z[q], op0=ALU.mult,
                                   op1=ALU.max).then_inc(f_abs, 1)
            V.memset(f_ones[q], 1.0)
            dve.wait_ge(f_exp, 1)
            log1p(f_e[q], f_s[q], f_y[q], f_p[q])
            link(V.tensor_scalar(f_z[q], f_z[q], -1.0, 0.0, ALU.mult, ALU.max))
            link(V.tensor_tensor(f_z[q], f_z[q], f_p[q], ALU.add))
            link(V.tensor_tensor_scan(f_neg_c[q], f_ones[q], f_z[q], 0.0, ALU.mult, ALU.add))
            V.tensor_scalar(f_c[q], f_neg_c[q], -1.0, None, ALU.mult).then_inc(f_c_ready, 1)

            with dve.Fori(0, 2) as i:
                link.enter(i, 4)

                def mem_max(n):
                    dve.wait_ge(ms_done, i * 2 + n + 1)
                    for h in range(2):
                        ins = V.reduce_max(rows[:, 4 * n, 2 * h:2 * h + 2],
                                           ps[:, 2 * n + h].rearrange("p (t m) -> p t m", m=NM), axis=AX.X)
                    link(ins)
                    V.tensor_scalar(rows[:, 4 * n + 1], rows[:, 4 * n], -MEM_SCALE, None, ALU.mult).then_inc(ms_max, 1)

                def mem_norm(n):
                    dve.wait_ge(ms_exp, i * 8 + 4 * n + 4)
                    link(V.reciprocal(rows[:, 4 * n + 3], rows[:, 4 * n + 2]))
                    for t in range(NT):
                        V.tensor_scalar(mem_p[:, n, t], mem_p[:, n, t], rows[:, 4 * n + 3, t:t + 1], None,
                                        ALU.mult).then_inc(ms_p, 1)

                def mem_turned(n):
                    for j in range(MT):
                        evac(mt_hi, i * 4 + 2 * n + j + 1, mem_pT[:, 1, j], ps[:, 4 + 2 * n + j],
                             mem_pT[:, 0, j], mt_lo)

                def mem_out(n):
                    for f in range(2):
                        one = bass.ds(i * 4 + (2 * n + f), 1)
                        evac(yc_hi, i * 4 + 2 * n + f + 1, yc[:, 1, one], ps[:, 2 * n + f:2 * n + f + 1],
                             yc[:, 0, one], yc_lo)

                for s in range(4):
                    split("mem_att", i, s + 2)
                    evac(mq_hi, i * 4 + s + 1, mq[:, s, 1], ps[:, 4 + s], mq[:, s, 0], mq_lo)
                    if s == 1:
                        for n in range(2):
                            V.tensor_copy(mem_vh[:, n], mem_v[:, :, :, bass.ds(i * (4 * P) + n * NM, NM)]).then_inc(mem_vh_ready, 1)
                    if s == 2:
                        mem_max(0)
                    if s == 3:
                        mem_norm(0)
                mem_turned(0)
                mem_max(1)
                mem_norm(1)
                mem_out(0)
                mem_turned(1)
                mem_out(1)
            link.leave(2)

            dve.wait_ge(c_stored, 32)
            link(V.memset(z_pad[:, 0:CONV_W - 1], 0.0))
            with dve.Fori(0, KD) as i:
                link.enter(i, 6)
                one = bass.ds(i, 1)
                split("lru", i, 2)
                dve.wait_ge(z_copied, i + 1)
                link(V.tensor_scalar(xc[:], z_pad[:, 0:T], col[:, CW, one], col[:, CB, one], ALU.mult, ALU.add))
                for w in range(1, CONV_W):
                    ins = V.scalar_tensor_tensor(out=xc[:], in0=z_pad[:, w:w + T], scalar=col[:, CW + w, one],
                                                 in1=xc[:], op0=ALU.mult, op1=ALU.add)
                    if w < CONV_W - 1:
                        link(ins)
                    else:
                        ins.then_inc(xc_ready, 1)
                split("lru", i, 3)
                dve.wait_ge(wri_hi, i + 1)
                V.tensor_tensor(w_ri[:, 1], w_ri_raw[:], w_ri[:, 0].bitcast(F32), ALU.subtract).then_inc(wri_lo, 1)
                evac(xc_hi, i + 1, xcT[:, 1], xc[:], xcT[:, 0], xc_lo)
                split("lru", i, 4)
                dve.wait_ge(lru_tanh, i + 1)
                link(V.tensor_scalar_add(l_h[:], l_t[:], 1.0))
                link(V.reciprocal(l_m[:], l_h[:]))
                V.scalar_tensor_tensor(out=l_m[:], in0=l_t[:], scalar=2.0, in1=l_m[:], op0=ALU.mult,
                                       op1=ALU.mult).then_inc(lru_m2, 1)
                dve.wait_ge(lru_i, i + 1)
                link(V.tensor_tensor(l_i[:], l_i[:], xc[:], ALU.mult))
                dve.wait_ge(lru_m, i + 1)
                V.tensor_tensor(l_t[:], l_i[:], l_m[:], ALU.mult).then_inc(pads_zeroed, 1)
                dve.wait_ge(pads_zeroed, i + 1)
                dve.wait_ge(lru_a, i + 1)
                V.tensor_tensor_scan(l_h[:], l_a[:], l_t[:], 0.0, ALU.mult, ALU.add).then_inc(lru_h, 1)
                evac(ya_hi, i + 1, ya[:, 1, one], l_h[:].rearrange("p (o t) -> p o t", o=1), ya[:, 0, one], ya_lo)
                dve.wait_ge(br["c"]["gate_ready"], i + 1)
                dve.wait_ge(unit_used, units.count("lru", i, 2))
                V.tensor_tensor(merged[:, one], gate[:, 0:1], ps[:, 4:5], ALU.mult).then_inc(br["c"]["merged_done"], 1)
                link.n += 0
            link.leave(KD)

            def merge(phase, b, banks, last):
                with dve.Fori(0, KD // 2) as i:
                    link.enter(i, 2)
                    for s in range(2):
                        one = bass.ds(i * 2 + s, 1)
                        split(phase, i, 2 * s + 2)
                        split(phase, i, 2 * s + 3)
                        dve.wait_ge(br[b]["gate_ready"], i * 2 + s + 1)
                        dve.wait_ge(unit_used, units.count(phase, i, 2 * s + 1))
                        link(V.tensor_tensor(prod[:, s], gate[:, s], ps[:, banks[2 * s + 1]], ALU.mult))
                        V.tensor_tensor(merged[:, one], merged[:, one], prod[:, s:s + 1], ALU.add).then_inc(br[b]["merged_done"], 1)
                        if last:
                            evac(mg_hi, i * 2 + s + 1, mgT[:, 1, one], merged[:, one], mgT[:, 0, one], mg_lo)
                link.leave(KD // 2)

            merge("merge_a", "a", (5, 6, 7, 0), False)

            with dve.Fori(0, FOX_HEADS // 2) as i:
                link.enter(i, 2)

                def mins(n):
                    dve.wait_ge(c_landed[n], i * 16 + 16)
                    for t in range(NT):
                        dve.wait_ge(fs_read, i * 8 + 4 * n + t + 1)
                        V.memset(rows[:, 4 * n + 1, t:t + 1], 0.0)
                        p = fox_p[:, n, ROW[t]:ROW[t + 1]]
                        V.tensor_tensor_reduce(out=p, in0=p, in1=c_all[:, n, 0:(t + 1) * P], scale=1.0, scalar=BIG,
                                               op0=ALU.add, op1=ALU.min,
                                               accum_out=rows[:, 4 * n, t:t + 1]).then_inc(fs_min, 1)

                def norm(n):
                    dve.wait_ge(fs_exp, i * 8 + 4 * n + 4)
                    link(V.reciprocal(rows[:, 4 * n + 3], rows[:, 4 * n + 2]))
                    for t in range(NT):
                        p = fox_p[:, n, ROW[t]:ROW[t + 1]]
                        V.tensor_scalar(p, p, rows[:, 4 * n + 3, t:t + 1], None, ALU.mult).then_inc(fs_p, 1)

                def turned_p(n):
                    for j in range(NT):
                        c = slice(COL[j], COL[j + 1])
                        evac(ft_hi, i * 8 + 4 * n + j + 1, fox_pT[:, 1, c], ps[:, 6 + j % 2, 0:(NT - j) * P],
                             fox_pT[:, 0, c], ft_lo)

                def value(n, bank):
                    evac(vt_hi, i * 2 + n + 1, v_h[:, 1], ps[:, bank].rearrange("p (j n) -> p j n", n=P),
                         v_h[:, 0], vt_lo)

                def out_b(n, bank):
                    one = bass.ds(i * 2 + n, 1)
                    evac(yb_hi, i * 2 + n + 1, yb[:, 1, one], ps[:, bank:bank + 1], yb[:, 0, one], yb_lo)

                for s in range(4):
                    split("fox", i, s + 2)
                    evac(qk_hi, i * 4 + s + 1, qk[:, s, 1], ps[:, s % 2], qk[:, s, 0], qk_lo)
                mins(0)
                norm(0)
                split("fox", i, 6)
                mins(1)
                value(0, 1)
                turned_p(0)
                split("fox", i, 7)
                norm(1)
                out_b(0, 0)
                value(1, 0)
                turned_p(1)
                out_b(1, 2)
            link.leave(FOX_HEADS // 2)

            merge("merge_b", "b", (2, 3, 4, 5), True)

            for s in range(KD):
                split("w_o", 0, s + 2)
            dve.wait_ge(gains2_landed, 48)
            dve.wait_ge(x2_landed, 16)
            for t in range(NT):
                two = ps[:, 2 * t:2 * t + 2].rearrange("p b n -> p (b n)")
                variance(n2_sum, t + 1, t, t + 1, n2_var)
                rstd(n2_std, t + 1, t, t + 1)
                link(V.scalar_tensor_tensor(out=normed[:], in0=two, scalar=stat[:, 3, t:t + 1],
                                            in1=g_post_all[:], op0=ALU.mult, op1=ALU.mult))
                V.tensor_tensor(h1[:, t], h1[:, t], normed[:], ALU.add).then_inc(h1_ready, 1)
                variance(n3_sum, t + 1, 4 + t, 5 + t, n3_var)
                rstd(n3_std, t + 1, 4 + t, 5 + t)
                V.scalar_tensor_tensor(out=u2[:, t], in0=h1[:, t], scalar=stat[:, 3, 4 + t:5 + t],
                                       in1=g_pre2_all[:], op0=ALU.mult, op1=ALU.mult).then_inc(u2_ready, 1)
                evac(u2_hi, t + 1, u2T[:, 1, :, t * P:(t + 1) * P],
                     ps[:, 2 * t:2 * t + 2].rearrange("p b (k n) -> p (b k) n", n=P),
                     u2T[:, 0, :, t * P:(t + 1) * P], pair_free)

            def mlp(i, final):
                for s in range(8):
                    split("mlp", i, s + 2)
                    dve.wait_ge(up_relu, i * 8 + s + 1)
                    V.scalar_tensor_tensor(out=relu2[:, s % 2], in0=ps[:, s], scalar=0.0, in1=relu[:, s % 2],
                                           op0=ALU.max, op1=ALU.mult).then_inc(up_sq, 1)
                    evac(up_hi, i * 8 + s + 1, actT[:, 1, s], relu2[:, s % 2], actT[:, 0, s], act_ready)
                for s in range(8, 16):
                    if not (final and s >= 14):
                        split("mlp", i, s + 2)
                for t in range(NT):
                    if t < NT - 1:
                        dve.wait_ge(down_done, i * (NT - 1) + t + 1)
                    else:
                        dve.wait_ge(unit_used, units.count("mlp", i, 15))
                    V.tensor_tensor(down_sum[:, t], down_sum[:, t],
                                    ps[:, 2 * t:2 * t + 2].rearrange("p b n -> p (b n)"),
                                    ALU.add).then_inc(n4_in if final else pair_free, 1)

            dve.wait_ge(sums_zeroed, 1)
            with dve.Fori(0, 3) as i:
                mlp(i, False)
            mlp(3, True)
            for t in range(NT):
                variance(n4_sum, t + 1, t, t + 1, n4_var)
                rstd(n4_std, t + 1, t, t + 1)
                link(V.scalar_tensor_tensor(out=down_sum[:, t], in0=down_sum[:, t], scalar=stat[:, 3, t:t + 1],
                                            in1=g_post2_all[:], op0=ALU.mult, op1=ALU.mult))
                V.tensor_tensor(down_sum[:, t], down_sum[:, t], h1[:, t], ALU.add).then_inc(y_ready, 1)

        @block.tensor
        def _(pe):
            def product(dst, lhs, rhs, start, stop):
                nc.tensor.matmul(dst, lhs(0), rhs(0), start=start, stop=False)
                nc.tensor.matmul(dst, lhs(0), rhs(1), start=False, stop=False)
                return nc.tensor.matmul(dst, lhs(1), rhs(0), start=False, stop=stop)

            def unit_ready(phase, i, s):
                pe.wait_ge(lo_done, units.count(phase, i, s))

            def columns(phase, i, s, dst, moving):
                unit_ready(phase, i, s)
                slot = units.slot(phase, s)
                for k in range(KD):
                    last = product(dst, lambda h: ring[:, slot, h, k * P:(k + 1) * P],
                                   lambda h: moving(h, k), k == 0, k == KD - 1)
                last.then_inc(unit_used, 1)

            def turn(t, src, bank):
                for k in range(KD):
                    last = nc.tensor.transpose(ps[:, bank + k // 4, (k % 4) * P:(k % 4 + 1) * P],
                                               src[:, k * P:(k + 1) * P], ident[:])
                return last

            from_u = lambda h, k: uT[:, h, k]

            pe.wait_ge(consts_ready, 2)
            for t in range(MT):
                pe.wait_ge(normed_ready, t + 1)
                turn(t, mem_in[:, t], 2 * t).then_inc(turned, 1)
            pe.wait_ge(turned_lo, MT)
            with pe.Fori(0, 2) as i:
                for s in range(4):
                    columns("mem_k", i, s, ps[:, 4 + s, 0:NM], lambda h, k: memT[:, h, k])

            def turn_x(t):
                pe.wait_ge(normed_ready, MT + t + 1)
                if t >= 2:
                    pe.wait_ge(turned_lo, MT + t - 1)
                turn(t, x_in[:, t], 2 * (t % 2)).then_inc(turned, 1)

            turn_x(0)
            turn_x(1)
            pe.wait_ge(mem_k_lo, KD)
            for k in range(KD):
                unit_ready("mem_v", 0, k)
                slot = units.slot("mem_v", k)
                for j in range(MT):
                    for h in range(2):
                        last = product(ps[:, 4 + 2 * j + h], lambda w: memT[:, w, k, j * P:(j + 1) * P],
                                       lambda w: ring[:, slot, w, h * T:(h + 1) * T], k == 0, k == KD - 1)
                    if k == KD - 1 and j == 0:
                        last.then_inc(mem_v_done, 1)
                last.then_inc(unit_used, 1)
                if k == 3:
                    turn_x(2)
                if k == 5:
                    turn_x(3)
            pe.wait_ge(turned_lo, MT + NT)
            columns("mem_v", 0, KD, ps[:, 0], from_u)

            pe.wait_ge(mem_v_lo, MT)
            pe.wait_ge(f_read, 1)
            with pe.Fori(0, 2) as i:
                def query(s):
                    columns("mem_att", i, s, ps[:, 4 + s], from_u)

                def scores(n):
                    pe.wait_ge(mq_lo, i * 4 + 2 * n + 2)
                    for t in range(NT):
                        dst = ps[:, 2 * n + t // 2, (t % 2) * NM:(t % 2 + 1) * NM]
                        for d in range(2):
                            last = product(dst, lambda w: mq[:, 2 * n + d, w, t * P:(t + 1) * P],
                                           lambda w: mem_k[:, w, bass.ds(i * 4 + (2 * n + d), 1)],
                                           d == 0, d == 1)
                    last.then_inc(ms_done, 1)

                def turn_p(n):
                    pe.wait_ge(ms_p, i * 8 + 4 * n + 4)
                    if n:
                        pe.wait_ge(mq_lo, i * 4 + 4)
                    for j in range(MT):
                        for t in range(NT):
                            last = nc.tensor.transpose(ps[:, 4 + 2 * n + j, t * P:(t + 1) * P],
                                                       mem_p[:, n, t, j * P:(j + 1) * P], ident[:])
                        last.then_inc(mt_done, 1)

                def outputs(n):
                    pe.wait_ge(mt_lo, i * 4 + 2 * n + 2)
                    pe.wait_ge(mem_vh_ready, i * 2 + n + 1)
                    for f in range(2):
                        for j in range(MT):
                            last = product(ps[:, 2 * n + f], lambda w: mem_vh[:, n, w, j, f * P:(f + 1) * P],
                                           lambda w: mem_pT[:, w, j], j == 0, j == MT - 1)
                        last.then_inc(yc_done, 1)

                query(0)
                query(1)
                query(2)
                scores(0)
                query(3)
                turn_p(0)
                scores(1)
                outputs(0)
                turn_p(1)
                outputs(1)

            pe.wait_ge(yc_lo, KD)
            with pe.Fori(0, KD) as i:
                columns("lru", i, 0, ps[:, 0], from_u)
                columns("lru", i, 1, ps[:, 1], from_u)
                pe.wait_ge(xc_lo, i + 1)
                pe.wait_ge(wri_lo, i + 1)
                for n in range(2):
                    product(ps[:, 2 + n], lambda w: w_ri[:, w, n], lambda w: xcT[:, w], True, True).then_inc(ri_done, 1)
                columns("lru", i, 2, ps[:, 4], lambda h, k: yc[:, h, k])

            def merge(phase, b, banks, y):
                with pe.Fori(0, KD // 2) as i:
                    for s in range(2):
                        columns(phase, i, 2 * s, ps[:, banks[2 * s]], from_u)
                        columns(phase, i, 2 * s + 1, ps[:, banks[2 * s + 1]],
                                lambda h, k: y[:, h, k])

            pe.wait_ge(ya_lo, KD)
            merge("merge_a", "a", (5, 6, 7, 0), ya)

            pe.wait_ge(consts_rounded, 2)
            pe.wait_ge(br["a"]["merged_done"], KD)
            with pe.Fori(0, FOX_HEADS // 2) as i:
                def project(s, bank):
                    columns("fox", i, s, ps[:, bank], from_u)

                def scores(n):
                    for t in range(NT):
                        if n:
                            pe.wait_ge(fs_read, i * 8 + t + 1)
                        dst = ps[:, 2 + t, 0:(t + 1) * P]
                        product(dst, lambda w: qk[:, 2 * n, w, t * P:(t + 1) * P],
                                lambda w: qk[:, 2 * n + 1, w, 0:(t + 1) * P], True, False)
                        nc.tensor.matmul(ps[:, 2 + t, t * P:(t + 1) * P], identR[:], maskR[:],
                                         start=False, stop=True).then_inc(fs_done, 1)

                def turn_v(n, bank):
                    pe.wait_ge(v_copied, i * 2 + n + 1)
                    for j in range(NT):
                        last = nc.tensor.transpose(ps[:, bank, j * P:(j + 1) * P], v_f[:, j * P:(j + 1) * P], ident[:])
                    last.then_inc(vt_done, 1)

                def turn_p(n):
                    pe.wait_ge(fs_p, i * 8 + 4 * n + 4)
                    for j in range(NT):
                        if j >= 2 or n:
                            pe.wait_ge(ft_lo, i * 8 + 4 * n + j - 1)
                        for t in range(j, NT):
                            last = nc.tensor.transpose(ps[:, 6 + j % 2, (t - j) * P:(t - j + 1) * P],
                                                       fox_p[:, n, ROW[t] + j * P:ROW[t] + (j + 1) * P], ident[:])
                        last.then_inc(ft_done, 1)

                def outputs(n, bank):
                    pe.wait_ge(vt_lo, i * 2 + n + 1)
                    for j in range(NT):
                        pe.wait_ge(ft_lo, i * 8 + 4 * n + j + 1)
                        last = product(ps[:, bank, j * P:T], lambda w: v_h[:, w, j],
                                       lambda w: fox_pT[:, w, COL[j]:COL[j + 1]], j == 0, j == NT - 1)
                    last.then_inc(yb_done, 1)

                project(0, 0)
                project(1, 1)
                pe.wait_ge(qk_lo, i * 4 + 1)
                project(2, 0)
                pe.wait_ge(qk_lo, i * 4 + 2)
                project(3, 1)
                scores(0)
                pe.wait_ge(qk_lo, i * 4 + 3)
                project(4, 0)
                pe.wait_ge(qk_lo, i * 4 + 4)
                scores(1)
                turn_v(0, 1)
                turn_p(0)
                outputs(0, 0)
                project(5, 1)
                pe.wait_ge(yb_lo, i * 2 + 1)
                turn_v(1, 0)
                turn_p(1)
                outputs(1, 2)

            pe.wait_ge(yb_lo, FOX_HEADS)
            merge("merge_b", "b", (2, 3, 4, 5), yb)

            for k in range(KD):
                pe.wait_ge(mg_lo, k + 1)
                unit_ready("w_o", 0, k)
                slot = units.slot("w_o", k)
                for t in range(NT):
                    if k == 0 and t in (1, 2):
                        pe.wait_ge(mg_lo, KD - 2 + t)
                    for h in range(2):
                        last = product(ps[:, 2 * t + h], lambda w: mgT[:, w, k, t * P:(t + 1) * P],
                                       lambda w: ring[:, slot, w, h * T:(h + 1) * T], k == 0, k == KD - 1)
                    if k == KD - 1 and t < NT - 1:
                        last.then_inc(wo_done, 1)
                last.then_inc(unit_used, 1)
            for t in range(NT):
                pe.wait_ge(u2_ready, t + 1)
                turn(t, u2[:, t], 2 * t).then_inc(u2_turned, 1)

            pe.wait_ge(pair_free, NT)
            with pe.Fori(0, 4) as i:
                for s in range(8):
                    pe.wait_ge(pair_free, i * 4 + s // 2 + 1)
                    columns("mlp", i, s, ps[:, s], lambda h, k: u2T[:, h, k])
                for k in range(8):
                    pe.wait_ge(act_ready, i * 8 + k + 1)
                    unit_ready("mlp", i, 8 + k)
                    slot = units.slot("mlp", 8 + k)
                    for t in range(NT):
                        if k == 0:
                            pe.wait_ge(act_ready, i * 8 + 2 * t + 2)
                        for h in range(2):
                            last = product(ps[:, 2 * t + h], lambda w: actT[:, w, k, t * P:(t + 1) * P],
                                           lambda w: ring[:, slot, w, h * T:(h + 1) * T], k == 0, k == 7)
                        if k == 7 and t < NT - 1:
                            last.then_inc(down_done, 1)
                    last.then_inc(unit_used, 1)


_INS = ["x", "mem", "g_mix_pre", "w_in", "conv_w", "conv_b", "w_r", "b_r", "w_i", "b_i", "lru_lambda", "b_f",
        "g_mem", "w_mem_kv", "b_gate", "w_pa", "w_pb", "w_pc", "w_o", "g_mix_post", "g_mlp_pre", "w_up",
        "w_down", "g_mlp_post"]


def kernel(**inputs):
    import concourse.bacc as bacc
    from concourse.bass_utils import run_bass_kernel_spmd

    nc = bacc.Bacc("TRN2", target_bir_lowering=False, num_devices=1)
    arrays, args = {}, []
    for name in _INS:
        a = np.ascontiguousarray(inputs[name])
        arrays[f"in_{name}"] = a
        args.append(nc.dram_tensor(f"in_{name}", a.shape, mybir.dt.from_np(a.dtype), kind="ExternalInput").ap())
    args.append(nc.dram_tensor("out_y", (1, T, D), F32, kind="ExternalOutput").ap())
    block_program(nc, *args)
    r = run_bass_kernel_spmd(nc, [arrays], core_ids=[0])
    return r.results[0]["out_y"]
```

```python
from contextlib import ExitStack

import numpy as np
import concourse.bass as bass
from concourse import mybir

F32 = mybir.dt.float32
F32R = mybir.dt.float32r
ALU = mybir.AluOpType
ACT = mybir.ActivationFunctionType
AX = mybir.AxisListType

P = 128
T = 512
NT = T // P
D = 1024
KD = D // P
NM = 256
MT = NM // P
FOX_HEADS = 8
MEM_HEADS = 4
CONV_W = 4
EPS = 1e-6
LRU_C = 8.0
FF = 4 * D
OFF_Q, OFF_K, OFF_V, OFF_MQ = D, 2 * D, 3 * D, 4 * D
OFF_GATE = 5 * D
OFF_F = 8 * D
N_IN = OFF_F + FOX_HEADS
FOX_SCALE = float(D // FOX_HEADS) ** -0.5
MEM_SCALE = float(D // MEM_HEADS) ** -0.5
MASKED = -1e30
BIG = 3e38
F_ROW = P - FOX_HEADS
F_Q = 96
LOG1P_TERMS = (1 / 15, 1 / 13, 1 / 11, 1 / 9, 1 / 7, 1 / 5, 1 / 3)
SLOTS = 4
LATE = 3

PHASES = {
    "mem_k": ((0, 1, 2, 3), 2),
    "mem_v": ((0, 1, 2, 3, 0, 1, 2, 3, 2), 1),
    "mem_att": ((0, 1, 2, 3), 2),
    "lru": ((0, 1, 2), 8),
    "merge_a": ((0, 1, 2, 3), 4),
    "fox": ((0, 1, 2, 0, 1, 2), 4),
    "merge_b": ((0, 1, 2, 3), 4),
    "w_o": ((0, 1, 2, 3, 0, 1, 2, 3), 1),
    "mlp": ((0, 1, 2, 3) * 4, 4),
}


class Units:

    def __init__(self):
        self.base, self.uses, self.first = {}, {}, {}
        n, use, last = 0, [0] * SLOTS, [None] * SLOTS
        for name, (slots, iters) in PHASES.items():
            self.base[name], self.uses[name] = n, list(use)
            self.first[name] = [None if x is None else x - n for x in last]
            for i in range(iters):
                for s, slot in enumerate(slots):
                    use[slot] += 1
                    last[slot] = n
                    n += 1

    def slot(self, phase, s):
        slots = PHASES[phase][0]
        return slots[s % len(slots)]

    def count(self, phase, i, s):
        return i * len(PHASES[phase][0]) + (self.base[phase] + s + 1)

    def loaded(self, phase, i, s):
        slots = PHASES[phase][0]
        s_in, more = s % len(slots), s // len(slots)
        per = slots.count(slots[s_in])
        nth = slots[:s_in].count(slots[s_in]) + 1
        return i * (16 * per) + 16 * (self.uses[phase][slots[s_in]] + more * per + nth)

    def before(self, phase, i, s):
        slots = PHASES[phase][0]
        size = len(slots)
        slot = slots[s % size]
        for back in range(s - 1, -1, -1):
            if slots[back % size] == slot:
                return i * size + (self.base[phase] + back + 1)
        earlier = self.first[phase][slot]
        if isinstance(i, int) and i == 0:
            return None if earlier is None else self.base[phase] + earlier + 1
        wrapped = s - 1
        while slots[wrapped % size] != slot:
            wrapped -= 1
        if earlier is not None:
            wrapped = max(wrapped, earlier)
        return i * size + (self.base[phase] + wrapped + 1)


class From1:

    def __init__(self, n):
        self.n = n

    def __mul__(self, m):
        return self.n * m + (-m)


class Chain:

    def __init__(self, eng, sem):
        self.eng, self.sem, self.n, self.i, self.per = eng, sem, 0, None, 0

    def __call__(self, ins):
        self.n += 1
        ins.then_inc(self.sem, 1)
        self.eng.wait_ge(self.sem, self.n if self.i is None else self.i * self.per + self.n)

    def enter(self, i, per, first=0):
        self.n -= per * first
        self.i, self.per, self.start = i, per, self.n

    def leave(self, end):
        assert self.n - self.start == self.per, (self.n - self.start, self.per)
        self.n = self.start + self.per * end
        self.i = None


def block_program(nc, x, mem, g_mix_pre, w_in, conv_w, conv_b, w_r, b_r, w_i, b_i, lru_lambda,
                  b_f, g_mem, w_mem_kv, b_gate, w_pa, w_pb, w_pc, w_o, g_mix_post, g_mlp_pre,
                  w_up, w_down, g_mlp_post, out):
    ctx = ExitStack()
    units = Units()
    KB = 1024
    with ctx:
        ctx.enter_context(nc.allow_non_contiguous_dma("small parameter columns"))
        base = -(-nc.sbuf_base // 32) * 32
        ctx.enter_context(nc.sbuf_tensor("arena", [P, 207 * 256], F32))

        def at(name, kib, shape, dt=F32):
            return nc.alloc_sbuf_tensor_at(name, [P] + shape, dt, offset=base + int(kib * KB))

        def sem(name):
            return ctx.enter_context(nc.semaphore(name))

        RING, RAW, UT, Y0, Y1, E, MG, TMP, CONST = 0, 32, 48, 80, 112, 144, 168, 184, 204
        ring = at("ring", RING, [SLOTS, 2, D], F32R)
        raw = at("raw", RAW, [SLOTS, D])
        uT = at("uT", UT, [2, KD, T], F32R)
        yc = at("yc", Y0, [2, KD, T], F32R)
        ya = at("ya", Y1, [2, KD, T], F32R)
        yb = at("yb", Y0, [2, KD, T], F32R)
        mgT = at("mgT", Y1, [2, KD, T], F32R)
        merged = at("merged", MG, [KD, T])
        x_in = at("x_in", MG, [NT, D])
        mem_in = at("mem_in", TMP, [MT, D])
        square_out = at("square_out", TMP + 8, [D])
        square_out3 = at("square_out3", Y0 + 8, [D])
        g_mem_all = at("g_mem_all", Y0, [D])
        g_mix_all = at("g_mix_all", Y0 + 4, [D])
        memT = at("memT", Y1, [2, KD, NM], F32R)
        mem_k = at("mem_k", Y1 + 16, [2, KD, NM], F32R)
        mem_v = at("mem_v", E, [2, MT, D], F32R)
        f_z = at("f_z", MG, [T])
        f_e = at("f_e", MG + 2, [T])
        f_s = at("f_s", MG + 4, [T])
        f_y = at("f_y", MG + 6, [T])
        f_p = at("f_p", MG + 8, [T])
        f_ones = at("f_ones", MG + 10, [T])
        f_m = at("f_m", TMP + 16, [T])
        f_neg_c = at("f_neg_c", MG + 12, [T])
        f_c = at("f_c", MG + 14, [T])
        mq = at("mq", Y1, [4, 2, T], F32R)
        mem_pT = [at("mem_pT0", E + 16, [2, MT, T], F32R), at("mem_pT1", TMP + 8, [2, MT, T], F32R)]
        mem_p = at("mem_p", TMP, [2, NT, NM])
        xcT = at("xcT", E, [2, T], F32R)
        w_ri = at("w_ri", E + 4, [2, 2, P], F32R)
        z_pad = at("z_pad", TMP, [T + 8])
        xc = at("xc", TMP + 2.5, [T])
        l_r = at("l_r", TMP + 4.5, [T])
        l_i = at("l_i", TMP + 6.5, [T])
        l_t = at("l_t", TMP + 8.5, [T])
        l_a = at("l_a", TMP + 10.5, [T])
        l_m = at("l_m", TMP + 12.5, [T])
        l_h = at("l_h", TMP + 14.5, [T])
        w_ri_raw = at("w_ri_raw", TMP + 16.5, [2, P])
        gate = at("gate", E + 12, [2, T])
        prod = at("prod", E + 16, [2, T])
        qk = at("qk", Y1, [4, 2, T], F32R)
        v_h = at("v_h", Y1 + 16, [2, 2, NT, P], F32R)
        ROW = [P * t * (t + 1) // 2 for t in range(NT + 1)]
        TURNS = ((0,), (1, 3), (2,))
        TURN_START = (0, NT * P, 2 * NT * P, ROW[NT])
        TURN_BANK = ((6, 7, 0), (4, 5, 7))
        fox_pT = at("fox_pT", E, [2, 2, ROW[NT]], F32R)
        fox_p = at("fox_p", TMP, [2, ROW[NT]])
        v_f = at("v_f", TMP + 10, [T])
        c_all = at("c_all", TMP + 12, [2, T])
        h1 = at("h1", TMP, [NT, D])
        g_post_all = at("g_post_all", E, [D])
        g_pre2_all = at("g_pre2_all", E + 4, [D])
        g_post2_all = at("g_post2_all", E + 8, [D])
        normed = at("normed", E + 12, [2, D])
        square_out2 = at("square_out2", E + 20, [D])
        square_out4 = at("square_out4", Y0 + 16, [D])
        u2 = at("u2", Y0, [NT, D])
        u2T = at("u2T", UT, [2, KD, T], F32R)
        actT = at("actT", Y0, [2, KD, T], F32R)
        relu = at("relu", E + 12, [2, T])
        relu2 = at("relu2", E + 16, [2, T])
        down_sum = at("down_sum", MG, [NT, D])
        ident = at("ident", CONST, [P])
        identR = at("identR", CONST + 0.5, [P], F32R)
        mask = at("mask", CONST + 1, [P])
        maskR = at("maskR", CONST + 1.5, [P], F32R)
        col = at("col", CONST + 2, [27, 8])
        stat = at("stat", CONST + 2.875, [4, 8])
        f_col = at("f_col", TMP + 18, [8])
        CW, CB, BR, BI, LAM, BG, NQ, SP = 0, 4, 5, 6, 7, 8, 11, 15
        rows = at("rows", CONST + 3, [8, 4])

        ps = ctx.enter_context(nc.psum_tensor("ps", [P, 8, T], F32))
        c_dram = nc.dram_tensor("c_scratch", [2, FOX_HEADS, T], F32, kind="Internal").ap()

        slot_loaded = [sem(f"slot_loaded{s}") for s in range(SLOTS)]
        hi_done, lo_done, unit_used = sem("hi_done"), sem("lo_done"), sem("unit_used")
        act_link, dve_link, pool_link = sem("act_link"), sem("dve_link"), sem("pool_link")
        mem_landed = [sem(f"mem_landed{t}") for t in range(MT)]
        x_landed = [sem(f"x_landed{t}") for t in range(NT)]
        g_mem_landed, g_mix_landed = sem("g_mem_landed"), sem("g_mix_landed")
        cols_landed, consts_ready = sem("cols_landed"), sem("consts_ready")
        consts_rounded = sem("consts_rounded")
        norm_sum, norm_var, norm_std = sem("norm_sum"), sem("norm_var"), sem("norm_std")
        dve_sum = sem("dve_sum")
        normed_ready, turned, turned_hi, turned_lo = (
            sem("normed_ready"), sem("turned"), sem("turned_hi"), sem("turned_lo"))
        mem_k_hi, mem_k_lo = sem("mem_k_hi"), sem("mem_k_lo")
        mem_v_done, mem_v_hi, mem_v_lo = sem("mem_v_done"), sem("mem_v_hi"), sem("mem_v_lo")
        f_read, f_exp, f_sum, f_inv, f_soft, f_c_ready = (
            sem("f_read"), sem("f_exp"), sem("f_sum"), sem("f_inv"), sem("f_soft"), sem("f_c_ready"))
        c_stored, c_cols_landed = sem("c_stored"), sem("c_cols_landed")
        lam_exp = sem("lam_exp")
        mq_hi, mq_lo = sem("mq_hi"), sem("mq_lo")
        ms_done, ms_max, ms_exp, ms_p, z_zeroed = sem("ms_done"), sem("ms_max"), sem("ms_exp"), sem("ms_p"), sem("z_zeroed")
        mt_done, mt_hi, mt_lo = sem("mt_done"), sem("mt_hi"), sem("mt_lo")
        yc_done, yc_hi, yc_lo = sem("yc_done"), sem("yc_hi"), sem("yc_lo")
        wri_landed, wri_hi, wri_lo = sem("wri_landed"), sem("wri_hi"), sem("wri_lo")
        z_copied, xc_ready, xc_hi, xc_lo = (
            sem("z_copied"), sem("xc_ready"), sem("xc_hi"), sem("xc_lo"))
        ri_done, lru_r, lru_tanh, lru_i, lru_sqrt, lru_x, lru_h, ya_lo = (
            sem("ri_done"), sem("lru_r"), sem("lru_tanh"), sem("lru_i"), sem("lru_sqrt"),
            sem("lru_x"), sem("lru_h"), sem("ya_lo"))
        ya_hi = sem("ya_hi")
        gate_ready, merged_done = sem("gate_ready"), sem("merged_done")
        BEFORE = {"c": 0, "a": KD, "b": 2 * KD}
        mg_hi, mg_lo = sem("mg_hi"), sem("mg_lo")
        qk_hi, qk_lo = sem("qk_hi"), sem("qk_lo")
        v_copied, vt_done, vt_hi, vt_lo = (
            sem("v_copied"), sem("vt_done"), sem("vt_hi"), sem("vt_lo"))
        fs_done, fs_read, fs_min, fs_exp, fs_p = (
            sem("fs_done"), sem("fs_read"), sem("fs_min"), sem("fs_exp"), sem("fs_p"))
        ft_done, ft_hi, ft_lo = sem("ft_done"), sem("ft_hi"), sem("ft_lo")
        yb_done, yb_hi, yb_lo = sem("yb_done"), sem("yb_hi"), sem("yb_lo")
        c_landed = [sem("c_landed_a"), sem("c_landed_b")]
        gains2_landed, x2_landed = sem("gains2_landed"), sem("x2_landed")
        wo_done = sem("wo_done")
        n2_ready, n4_ready, h1_last, y_last = sem("n2_ready"), sem("n4_ready"), sem("h1_last"), sem("y_last")
        n2_sum, n2_var, n2_std, h1_ready, n3_sum, n3_var, n3_std, u2_ready = (
            sem("n2_sum"), sem("n2_var"), sem("n2_std"), sem("h1_ready"), sem("n3_sum"),
            sem("n3_var"), sem("n3_std"), sem("u2_ready"))
        u2_turned, u2_hi, pair_free = sem("u2_turned"), sem("u2_hi"), sem("pair_free")
        sums_zeroed = sem("sums_zeroed")
        up_relu, up_sq, up_hi, act_ready, down_done = (
            sem("up_relu"), sem("up_sq"), sem("up_hi"), sem("act_ready"),
            sem("down_done"))
        n4_in, n4_sum, n4_var, n4_std, y_ready, stored = (
            sem("n4_in"), sem("n4_sum"), sem("n4_var"), sem("n4_std"), sem("y_ready"), sem("stored"))

        block = ctx.enter_context(nc.Block())

        MEM_ORDER = "q0 q1 q2 s0 q3 q4 s1 q5 t0 q6 o0 t1 q7 s2 o1 s3 t2 l0 t3 o2 l1 o3".split()
        MEM_ORDER_EVAC = "q0 q1 q2 q3 s0 q4 q5 s1 t0 q6 o0 t1 q7 f0 s2 o1 s3 t2 t3 o2 w0 o3".split()
        MS_BANK, MO_BANK = (2, 4, 2, 4), (2, 0, 2, 6)

        NORM_ORDER = "a0 a1 b0 a2 b1 a3 c0 b2 c1 w1 w2 b3 c2 c3".split()

        w_in_v = w_in.rearrange("o (k p) n -> p (o k) n", p=P)
        w_kv_v = w_mem_kv.rearrange("o (k p) n -> p (o k) n", p=P)
        w_up_v = w_up.rearrange("o (k p) n -> p (o k) n", p=P)
        proj_v = {"a": w_pa.rearrange("o (k p) n -> p (o k) n", p=P),
                  "b": w_pb.rearrange("o (k p) n -> p (o k) n", p=P),
                  "c": w_pc.rearrange("o (k p) n -> p (o k) n", p=P)}
        w_o_v = w_o.rearrange("o (k p) n -> p (o k) n", p=P)
        w_down_v = w_down.rearrange("o (k p) n -> p (o k) n", p=P)
        x_v = x.rearrange("o (t p) d -> p (o t) d", p=P)
        out_v = out.rearrange("o (t p) d -> p (o t) d", p=P)
        GATE_OFF = {"a": OFF_GATE, "b": OFF_GATE + D, "c": OFF_GATE + 2 * D}

        @block.sync
        def _(sp):
            def cols(view, start):
                return view[:, :, bass.ds(start, P)]

            def load(phase, i, s, src):
                slot = units.slot(phase, s)
                used = units.before(phase, i, s)
                if used is not None:
                    sp.wait_ge(lo_done, used)
                dst = raw[:, slot]
                if len(src.shape) == 3 and src.shape[1] == KD:
                    dst = dst.rearrange("p (k n) -> p k n", k=KD)
                    return sp.dma_start(dst, src).then_inc(slot_loaded[slot], 16)
                return sp.dma_start(dst, src).then_inc(slot_loaded[slot], 16)

            mem_rows = mem.rearrange("o (t p) d -> p (o t) d", p=P)
            for t in range(MT):
                sp.dma_start(mem_in[:, t], mem_rows[:, t]).then_inc(mem_landed[t], 16)
            sp.dma_start(g_mem_all[:], g_mem.partition_broadcast(P)[:, 0]).then_inc(g_mem_landed, 16)
            for m in range(KD):
                load("mem_k", m // 4, m % 4, cols(w_kv_v, m * P))
                if m >= 3 and m < 3 + NT:
                    sp.dma_start(x_in[:, m - 3], x_v[:, m - 3]).then_inc(x_landed[m - 3], 16)
            for k in range(KD):
                load("mem_v", 0, k, w_kv_v[:, k, D:2 * D])
            load("mem_v", 0, KD, cols(w_in_v, N_IN - P))
            with sp.Fori(0, 2) as i:
                for s in range(4):
                    load("mem_att", i, s, cols(w_in_v, i * (4 * P) + (OFF_MQ + s * P)))
            def lru_loads(i):
                load("lru", i, 0, cols(w_in_v, i * P))
                load("lru", i, 1, cols(w_in_v, i * P + GATE_OFF["c"]))
                load("lru", i, 2, cols(proj_v["c"], i * P))

            wri_v = [w.rearrange("o h i j -> i (o h) j") for w in (w_r, w_i)]
            lru_loads(0)
            sp.wait_ge(f_soft, 1)
            for g in range(2):
                sp.dma_start(w_ri_raw[:, g], wri_v[g][:, 0]).then_inc(wri_landed, 16)
            with sp.Fori(1, KD) as i:
                lru_loads(i)
                sp.wait_ge(wri_lo, i)
                for g in range(2):
                    sp.dma_start(w_ri_raw[:, g], wri_v[g][:, bass.ds(i, 1)]).then_inc(wri_landed, 16)

            def merge_loads(phase, b):
                with sp.Fori(1, KD // 2 + 1) as n:
                    i = From1(n)
                    for s in range(2):
                        load(phase, i, s, cols(w_in_v, i * (2 * P) + (GATE_OFF[b] + s * P)))
                    for s in range(2):
                        load(phase, i, 2 + s, cols(proj_v[b], i * (2 * P) + s * P))

            merge_loads("merge_a", "a")
            with sp.Fori(0, FOX_HEADS // 2) as i:
                for s, off in enumerate((OFF_Q, OFF_K, OFF_Q + P, OFF_K + P, OFF_V, OFF_V + P)):
                    load("fox", i, s, cols(w_in_v, i * (2 * P) + off))
            merge_loads("merge_b", "b")
            for k in range(KD):
                load("w_o", 0, k, w_o_v[:, k])
            with sp.Fori(1, 5) as n:
                i = From1(n)
                for s in range(8):
                    load("mlp", i, s, cols(w_up_v, i * D + s * P))
                for s in range(8):
                    load("mlp", i, 8 + s, w_down_v[:, bass.ds(i * KD + s, 1)])
            for t in range(NT):
                sp.wait_ge(*((y_ready, t + 1) if t < NT - 1 else (y_last, 1)))
                sp.dma_start(out_v[:, t], down_sum[:, t]).then_inc(stored, 16)
            sp.wait_ge(stored, 16 * NT)

        @block.gpsimd
        def _(pool):
            link = Chain(pool, pool_link)
            link(nc.gpsimd.memset(ident[:], 0.0))
            link(nc.gpsimd.memset(mask[:], 0.0))
            nc.gpsimd.affine_select(out=ident[:], in_=ident[:], compare_op=ALU.not_equal, fill=1.0,
                                    base=0, pattern=[[-1, P]], channel_multiplier=1).then_inc(consts_ready, 1)
            nc.gpsimd.affine_select(out=mask[:], in_=mask[:], compare_op=ALU.is_ge, fill=MASKED,
                                    base=0, pattern=[[-1, P]], channel_multiplier=1).then_inc(consts_ready, 1)
            pool.dma_start(g_mix_all[:], g_mix_pre.partition_broadcast(P)[:, 0]).then_inc(g_mix_landed, 16)
            link(nc.gpsimd.memset(f_col[:], 0.0))
            for w in range(CONV_W):
                pool.dma_start(col[:, CW + w], conv_w[0, w].rearrange("(j p) -> p j", p=P)).then_inc(cols_landed, 16)
            pool.dma_start(col[:, CB], conv_b[0].rearrange("(j p) -> p j", p=P)).then_inc(cols_landed, 16)
            pool.dma_start(col[:, BR], b_r[0].rearrange("j p -> p j")).then_inc(cols_landed, 16)
            pool.dma_start(col[:, BI], b_i[0].rearrange("j p -> p j")).then_inc(cols_landed, 16)
            pool.dma_start(col[:, LAM], lru_lambda[0].rearrange("(j p) -> p j", p=P)).then_inc(cols_landed, 16)
            for b in range(3):
                pool.dma_start(col[:, BG + b], b_gate[0, b].rearrange("(j p) -> p j", p=P)).then_inc(cols_landed, 16)
            pool.dma_start(f_col[F_ROW:P, 0:1], b_f.rearrange("o h -> h o")).then_inc(cols_landed, 16)
            q = slice(F_Q, P)
            G = nc.gpsimd
            pool.wait_ge(f_exp, 1)
            G.tensor_scalar(f_s[q], f_e[q], 2.0, 1.0, ALU.add, ALU.mult).then_inc(f_sum, 1)
            pool.wait_ge(f_inv, 1)
            link(G.tensor_tensor(f_s[q], f_e[q], f_y[q], ALU.mult))
            link(G.tensor_tensor(f_y[q], f_s[q], f_s[q], ALU.mult))
            link(G.tensor_scalar(f_p[q], f_y[q], LOG1P_TERMS[0], 1.0, ALU.mult, ALU.mult))
            for term in LOG1P_TERMS[1:]:
                link(G.tensor_scalar(f_p[q], f_p[q], term, 1.0, ALU.add, ALU.mult))
                link(G.tensor_tensor(f_p[q], f_p[q], f_y[q], ALU.mult))
            link(G.tensor_scalar(f_p[q], f_p[q], 1.0, 2.0, ALU.add, ALU.mult))
            link(G.tensor_tensor(f_p[q], f_p[q], f_s[q], ALU.mult))
            G.tensor_tensor(f_z[q], f_m[q], f_p[q], ALU.add).then_inc(f_soft, 1)
            pool.wait_ge(f_c_ready, 1)
            pool.dma_start(c_dram[0], f_neg_c[F_ROW:P, :]).then_inc(c_stored, 16)
            pool.dma_start(c_dram[1], f_c[F_ROW:P, :]).then_inc(c_stored, 16)
            pool.wait_ge(c_stored, 32)
            for t in range(NT):
                pool.dma_start(col[:, NQ + t], c_dram[0, :, t * P:(t + 1) * P].rearrange("h p -> p h")).then_inc(c_cols_landed, 16)
            pool.wait_ge(merged_done, 2 * KD)
            for n in range(2):
                pool.dma_start(c_all[:, n], c_dram[1, n:n + 1].partition_broadcast(P)[:, 0]).then_inc(c_landed[n], 16)
            with pool.Fori(0, FOX_HEADS // 2 - 1) as i:
                for n in range(2):
                    pool.wait_ge(fs_min, i * 8 + 4 * (n + 1))
                    pool.dma_start(c_all[:, n], c_dram[1, bass.ds(i * 2 + (n + 2), 1)].partition_broadcast(P)[:, 0]).then_inc(c_landed[n], 16)
            pool.wait_ge(yb_lo, FOX_HEADS)
            for g, dst in ((g_mix_post, g_post_all), (g_mlp_pre, g_pre2_all), (g_mlp_post, g_post2_all)):
                pool.dma_start(dst[:], g.partition_broadcast(P)[:, 0]).then_inc(gains2_landed, 16)
            pool.dma_start(h1[:], x_v).then_inc(x2_landed, 16)
            pool.wait_ge(mg_lo, KD)
            nc.gpsimd.memset(down_sum[:], 0.0).then_inc(sums_zeroed, 1)
            pool.wait_ge(x2_landed, 16)
            for t in range(NT - 1):
                pool.wait_ge(n2_ready, t + 1)
                G.tensor_tensor(h1[:, t], h1[:, t], normed[:, t % 2], ALU.add).then_inc(h1_ready, 1)
            for t in range(NT - 1):
                pool.wait_ge(n4_ready, t + 1)
                G.tensor_tensor(down_sum[:, t], down_sum[:, t], h1[:, t], ALU.add).then_inc(y_ready, 1)

        @block.scalar
        def _(act):
            A = nc.scalar.activation

            def split(phase, i, s):
                slot = units.slot(phase, s)
                act.wait_ge(slot_loaded[slot], units.loaded(phase, i, s))
                used = units.before(phase, i, s)
                if used is not None:
                    act.wait_ge(unit_used, used)
                A(ring[:, slot, 0], raw[:, slot], ACT.Copy).then_inc(hi_done, 1)

            def evac(ready, value, dst, src, done):
                act.wait_ge(ready, value)
                A(dst, src, ACT.Copy).then_inc(done, 1)

            nc.scalar.preload_act_table(ACT.Sqrt)
            act.wait_ge(mem_landed[0], 16)
            A(square_out[:], mem_in[:, 0], ACT.Square, accum_out=stat[:, 0, 0:1]).then_inc(norm_sum, 1)
            for t in range(MT):
                act.wait_ge(norm_var, t + 1)
                A(stat[:, 2, t:t + 1], stat[:, 1, t:t + 1], ACT.Sqrt).then_inc(norm_std, 1)
            for t in range(MT):
                split("mem_k", 0, t)
                evac(turned, t + 1, memT[:, 0, :, t * P:(t + 1) * P],
                     ps[:, 2 * t:2 * t + 2].rearrange("p b (k n) -> p (b k) n", n=P), turned_hi)
            for m in range(KD):
                split("mem_k", 0, m + 2)
                evac(unit_used, units.count("mem_k", 0, m), mem_k[:, 0, m], ps[:, 4 + m % 4, 0:NM], mem_k_hi)
                if 2 <= m < 2 + NT:
                    t = m - 2
                    act.wait_ge(x_landed[t], 16)
                    act.wait_ge(norm_sum, MT - 1 + t)
                    A(square_out[:], x_in[:, t], ACT.Square, accum_out=stat[:, 0, MT + t:MT + t + 1]).then_inc(norm_sum, 1)
                    act.wait_ge(norm_var, MT + t + 1)
                    A(stat[:, 2, MT + t:MT + t + 1], stat[:, 1, MT + t:MT + t + 1], ACT.Sqrt).then_inc(norm_std, 1)

            def x_turned(t):
                evac(turned, MT + t + 1, uT[:, 0, :, t * P:(t + 1) * P],
                     ps[:, 2 * (t % 2):2 * (t % 2) + 2].rearrange("p b (k n) -> p (b k) n", n=P), turned_hi)

            for s in range(KD + 1):
                if s == 0:
                    x_turned(0)
                split("mem_v", 0, s + 2)
                if s == 0:
                    x_turned(1)
                if s == 3:
                    x_turned(2)
                if s == 5:
                    x_turned(3)
                if s == KD - 1:
                    for j in range(MT):
                        evac(*((mem_v_done, 1) if j == 0 else (unit_used, units.count("mem_v", 0, KD - 1))), mem_v[:, 0, j],
                             ps[:, 4 + 2 * j:6 + 2 * j].rearrange("p b n -> p (b n)"), mem_v_hi)
            act.wait_ge(cols_landed, 16 * 12)
            A(col[:, SP + 1], col[:, LAM], ACT.Abs).then_inc(act_link, 1)
            act.wait_ge(act_link, 1)
            A(col[:, SP + 2], col[:, SP + 1], ACT.Exp, scale=-1.0).then_inc(lam_exp, 1)
            q = slice(F_Q, P)
            act.wait_ge(unit_used, units.count("mem_v", 0, KD))
            A(f_z[q], ps[q, 0], ACT.Identity, bias=f_col[q, 0:1]).then_inc(f_read, 1)
            act.wait_ge(f_read, 1)
            A(f_m[q], f_z[q], ACT.Relu, scale=-1.0)
            A(f_e[q], f_z[q], ACT.Abs).then_inc(act_link, 1)
            act.wait_ge(act_link, 2)
            A(f_e[q], f_e[q], ACT.Exp, scale=-1.0).then_inc(f_exp, 1)

            def query(s):
                split("mem_att", s // 4, s % 4 + 2)
                evac(unit_used, units.count("mem_att", 0, s), mq[:, s % 4, 0], ps[:, s % 2], mq_hi)

            def mem_exp(n):
                for t in range(NT):
                    if t % 2 == 0:
                        act.wait_ge(ms_max, 2 * n + t // 2 + 1)
                    A(mem_p[:, n % 2, t], ps[:, MS_BANK[n] + t // 2, (t % 2) * NM:(t % 2 + 1) * NM], ACT.Exp,
                      bias=rows[:, 4 * (n % 2) + 1, t:t + 1], scale=MEM_SCALE,
                      accum_out=rows[:, 4 * (n % 2) + 2, t:t + 1]).then_inc(ms_exp, 1)

            def mem_turned(n):
                for j in range(MT):
                    evac(mt_done, 2 * n + j + 1, mem_pT[n % 2][:, 0, j], ps[:, 6 + j], mt_hi)

            def mem_out(n):
                for f in range(2):
                    evac(yc_done, 2 * n + f + 1, yc[:, 0, 2 * n + f], ps[:, MO_BANK[n] + f], yc_hi)

            for step in MEM_ORDER_EVAC:
                if step[0] == "w":
                    split("lru", 0, 2)
                elif step[0] != "f":
                    {"q": query, "s": mem_exp, "t": mem_turned, "o": mem_out}[step[0]](int(step[1]))

            def lru_out(i):
                evac(lru_h, i + 1, ya[:, 0, bass.ds(i, 1)], l_h[:].rearrange("p (o t) -> p o t", o=1), ya_hi)

            def lru(i, first):
                one = bass.ds(i, 1)
                nc.scalar.preload_act_table(ACT.Sigmoid)
                act.wait_ge(unit_used, units.count("lru", i, 0))
                A(z_pad[:, CONV_W - 1:CONV_W - 1 + T], ps[:, 0], ACT.Copy).then_inc(z_copied, 1)
                act.wait_ge(wri_landed, i * 32 + 32)
                A(w_ri[:, 0], w_ri_raw[:], ACT.Copy).then_inc(wri_hi, 1)
                if not first:
                    lru_out(i - 1)
                split("lru", i, 3)
                act.wait_ge(xc_ready, i + 1)
                A(xcT[:, 0], xc[:], ACT.Copy).then_inc(xc_hi, 1)
                act.wait_ge(unit_used, units.count("lru", i, 1))
                A(gate[:, 0], ps[:, 1], ACT.Sigmoid, bias=col[:, BG + 2, one]).then_inc(gate_ready, 1)
                split("lru", i, 4)
                act.wait_ge(ri_done, i * 2 + 1)
                A(l_r[:], ps[:, 2], ACT.Sigmoid, bias=col[:, BR, one]).then_inc(lru_r, 1)
                act.wait_ge(lru_r, i + 1)
                A(l_t[:], l_r[:], ACT.Tanh, scale=col[:, SP, one]).then_inc(lru_tanh, 1)
                act.wait_ge(ri_done, i * 2 + 2)
                A(l_i[:], ps[:, 3], ACT.Sigmoid, bias=col[:, BI, one]).then_inc(lru_i, 1)
                split("lru", i, 5)
                act.wait_ge(lru_tanh, i + 1)
                A(l_r[:], l_t[:], ACT.Sqrt, scale=4.0).then_inc(lru_sqrt, 1)

            lru(0, True)
            with act.Fori(1, KD) as i:
                lru(i, False)
            lru_out(KD - 1)

            def merge(phase, b, banks, last):
                def body(i, first):
                    nc.scalar.preload_act_table(ACT.Sigmoid)
                    for s in range(2):
                        if not (first and s == 0):
                            split(phase, i, s + 2)
                        act.wait_ge(unit_used, units.count(phase, i, s))
                        act.wait_ge(merged_done, i * 2 + BEFORE[b])
                        A(gate[:, s], ps[:, banks[s]], ACT.Sigmoid,
                          bias=col[:, BG + "abc".index(b), bass.ds(i * 2 + s, 1)]).then_inc(gate_ready, 1)
                    for s in range(2):
                        split(phase, i, s + 4)
                        if last:
                            one = bass.ds(i * 2 + s, 1)
                            evac(merged_done, i * 2 + (BEFORE[b] + s + 1), mgT[:, 0, one], merged[:, one], mg_hi)

                body(0, not last)
                with act.Fori(1, KD // 2) as i:
                    body(i, False)

            merge("merge_a", "a", (5, 6, 7, 4), False)

            act.wait_ge(c_cols_landed, 16 * NT)
            with act.Fori(0, FOX_HEADS // 2) as i:
                def scores(n):
                    for t in range(NT):
                        act.wait_ge(fs_done, i * 8 + 4 * n + t + 1)
                        A(fox_p[:, n, ROW[t]:ROW[t + 1]], ps[:, 2 + t, 0:(t + 1) * P], ACT.Identity,
                          bias=col[:, NQ + t, bass.ds(i * 2 + n, 1)], scale=-FOX_SCALE).then_inc(fs_read, 1)

                def exps(n):
                    for t in range(NT):
                        act.wait_ge(fs_min, i * 8 + 4 * n + t + 1)
                        p = fox_p[:, n, ROW[t]:ROW[t + 1]]
                        A(p, p, ACT.Exp, bias=rows[:, 4 * n, t:t + 1], scale=-1.0,
                          accum_out=rows[:, 4 * n + 2, t:t + 1]).then_inc(fs_exp, 1)

                def turned_p(n):
                    for g in range(3):
                        c = slice(TURN_START[g], TURN_START[g + 1])
                        evac(ft_done, i * 6 + 3 * n + g + 1, fox_pT[:, n, 0, c],
                             ps[:, TURN_BANK[n][g], 0:c.stop - c.start], ft_hi)

                def value(n, bank):
                    act.wait_ge(unit_used, units.count("fox", i, 4 + n))
                    A(v_f[:], ps[:, bank], ACT.Copy).then_inc(v_copied, 1)

                for s in range(4):
                    split("fox", i, s + 2)
                    evac(unit_used, units.count("fox", i, s), qk[:, s, 0], ps[:, s % 2], qk_hi)
                scores(0)
                exps(0)
                split("fox", i, 6)
                value(0, 0)
                scores(1)
                turned_p(0)
                evac(vt_done, i * 2 + 1, v_h[:, 0, 0], ps[:, 1].rearrange("p (j n) -> p j n", n=P), vt_hi)
                exps(1)
                split("fox", i, 7)
                value(1, 2)
                turned_p(1)
                evac(vt_done, i * 2 + 2, v_h[:, 1, 0], ps[:, 1].rearrange("p (j n) -> p j n", n=P), vt_hi)
                evac(yb_done, i * 2 + 1, yb[:, 0, bass.ds(i * 2, 1)], ps[:, 3:4], yb_hi)
                evac(yb_done, i * 2 + 2, yb[:, 0, bass.ds(i * 2 + 1, 1)], ps[:, 6:7], yb_hi)

            merge("merge_b", "b", (4, 5, 6, 7), True)

            for s in range(KD - 1):
                split("w_o", 0, s + 2)
            def norm_after(t):
                act.wait_ge(*((wo_done, t + 1) if t < NT - 1 else (unit_used, units.count("w_o", 0, KD - 1))))
                A(square_out2[:], ps[:, 2 * t:2 * t + 2].rearrange("p b n -> p (b n)"), ACT.Square,
                  accum_out=stat[:, 0, t:t + 1]).then_inc(n2_sum, 1)
                act.wait_ge(n2_var, t + 1)
                A(stat[:, 2, t:t + 1], stat[:, 1, t:t + 1], ACT.Sqrt).then_inc(n2_std, 1)

            def norm_before(t):
                act.wait_ge(*((h1_ready, t + 1) if t < NT - 1 else (h1_last, 1)))
                A(square_out4[:], h1[:, t], ACT.Square, accum_out=stat[:, 0, 4 + t:5 + t]).then_inc(n3_sum, 1)
                act.wait_ge(n3_var, t + 1)
                A(stat[:, 2, 4 + t:5 + t], stat[:, 1, 4 + t:5 + t], ACT.Sqrt).then_inc(n3_std, 1)

            def u2_turn(t):
                evac(u2_turned, t + 1, u2T[:, 0, :, t * P:(t + 1) * P],
                     ps[:, 2 * t:2 * t + 2].rearrange("p b (k n) -> p (b k) n", n=P), u2_hi)

            for step in NORM_ORDER:
                {"a": norm_after, "b": norm_before, "c": u2_turn,
                 "w": lambda s: split("mlp", 0, s)}[step[0]](int(step[1]))

            def mlp(i, first, final):
                for s in range(8):
                    if not (first and s == 0):
                        split("mlp", i, s + 2)
                    act.wait_ge(unit_used, units.count("mlp", i, s))
                    A(relu[:, s % 2], ps[:, s], ACT.Relu).then_inc(up_relu, 1)
                    evac(up_sq, i * 8 + s + 1, actT[:, 0, s], relu2[:, s % 2], up_hi)
                for s in range(8, 16):
                    if not (final and s >= 14):
                        split("mlp", i, s + 2)

            mlp(0, True, False)
            with act.Fori(1, 3) as i:
                mlp(i, False, False)
            mlp(3, False, True)
            for t in range(NT):
                act.wait_ge(n4_in, t + 1)
                if t:
                    act.wait_ge(n4_sum, t)
                A(square_out2[:], down_sum[:, t], ACT.Square, accum_out=stat[:, 0, t:t + 1]).then_inc(n4_sum, 1)
                act.wait_ge(n4_var, t + 1)
                A(stat[:, 2, t:t + 1], stat[:, 1, t:t + 1], ACT.Sqrt).then_inc(n4_std, 1)

        @block.vector
        def _(dve):
            V = nc.vector
            link = Chain(dve, dve_link)

            def split(phase, i, s):
                slot = units.slot(phase, s)
                dve.wait_ge(hi_done, units.count(phase, i, s))
                V.tensor_tensor(ring[:, slot, 1], raw[:, slot], ring[:, slot, 0].bitcast(F32),
                                ALU.subtract).then_inc(lo_done, 1)

            def evac(hi_sem, value, dst, src, hi, done):
                dve.wait_ge(hi_sem, value)
                V.tensor_tensor(dst, src, hi.bitcast(F32), ALU.subtract).then_inc(done, 1)

            def log1p(e, s, y, p):
                link(V.tensor_scalar_add(s, e, 2.0))
                link(V.reciprocal(y, s))
                link(V.tensor_tensor(s, e, y, ALU.mult))
                link(V.tensor_tensor(y, s, s, ALU.mult))
                link(V.tensor_scalar(p, y, LOG1P_TERMS[0], None, ALU.mult))
                for term in LOG1P_TERMS[1:]:
                    link(V.scalar_tensor_tensor(out=p, in0=p, scalar=term, in1=y, op0=ALU.add, op1=ALU.mult))
                link(V.scalar_tensor_tensor(out=p, in0=p, scalar=1.0, in1=s, op0=ALU.add, op1=ALU.mult))
                link(V.tensor_scalar(p, p, 2.0, None, ALU.mult))

            def variance(sums, value, lo, hi, done):
                dve.wait_ge(sums, value)
                V.tensor_scalar(stat[:, 1, lo:hi], stat[:, 0, lo:hi], 1.0 / D, EPS, ALU.mult, ALU.add).then_inc(done, 1)

            def rstd(stds, value, lo, hi):
                dve.wait_ge(stds, value)
                link(V.reciprocal(stat[:, 3, lo:hi], stat[:, 2, lo:hi]))

            variance(norm_sum, 1, 0, 1, norm_var)
            dve.wait_ge(mem_landed[1], 16)
            V.tensor_tensor_reduce(out=square_out3[:], in0=mem_in[:, 1], in1=mem_in[:, 1], scale=1.0, scalar=0.0,
                                   op0=ALU.mult, op1=ALU.add, accum_out=stat[:, 0, 1:2]).then_inc(dve_sum, 1)
            variance(dve_sum, 1, 1, 2, norm_var)
            dve.wait_ge(g_mem_landed, 16)
            for t in range(MT):
                rstd(norm_std, t + 1, t, t + 1)
                V.scalar_tensor_tensor(out=mem_in[:, t], in0=mem_in[:, t], scalar=stat[:, 3, t:t + 1],
                                       in1=g_mem_all[:], op0=ALU.mult, op1=ALU.mult).then_inc(normed_ready, 1)

            def turned_to(dst, n, t, bank):
                evac(turned_hi, n + 1, dst[:, 1, :, t * P:(t + 1) * P],
                     ps[:, bank:bank + 2].rearrange("p b (k n) -> p (b k) n", n=P),
                     dst[:, 0, :, t * P:(t + 1) * P], turned_lo)

            for t in range(MT):
                split("mem_k", 0, t)
                turned_to(memT, t, t, 2 * t)
            dve.wait_ge(consts_ready, 2)
            V.tensor_copy(identR[:], ident[:]).then_inc(consts_rounded, 1)
            V.tensor_copy(maskR[:], mask[:]).then_inc(consts_rounded, 1)
            for m in range(KD):
                split("mem_k", 0, m + 2)
                evac(mem_k_hi, m + 1, mem_k[:, 1, m], ps[:, 4 + m % 4, 0:NM], mem_k[:, 0, m], mem_k_lo)
                if 2 <= m < 2 + NT:
                    t = m - 2
                    variance(norm_sum, MT + t, MT + t, MT + t + 1, norm_var)
                    rstd(norm_std, MT + t + 1, MT + t, MT + t + 1)
                    if t == 0:
                        dve.wait_ge(g_mix_landed, 16)
                    V.scalar_tensor_tensor(out=x_in[:, t], in0=x_in[:, t], scalar=stat[:, 3, MT + t:MT + t + 1],
                                           in1=g_mix_all[:], op0=ALU.mult, op1=ALU.mult).then_inc(normed_ready, 1)
            for s in range(KD + 1):
                if s == 0:
                    turned_to(uT, MT, 0, 0)
                split("mem_v", 0, s + 2)
                if s == 0:
                    turned_to(uT, MT + 1, 1, 2)
                if s == 3:
                    turned_to(uT, MT + 2, 2, 0)
                if s == 5:
                    turned_to(uT, MT + 3, 3, 2)
                if s == KD - 1:
                    for j in range(MT):
                        evac(mem_v_hi, j + 1, mem_v[:, 1, j],
                             ps[:, 4 + 2 * j:6 + 2 * j].rearrange("p b n -> p (b n)"), mem_v[:, 0, j], mem_v_lo)
            dve.wait_ge(lam_exp, 1)
            log1p(col[:, SP + 2], col[:, SP + 3], col[:, SP + 4], col[:, SP + 5])
            link(V.tensor_scalar(col[:, SP + 6], col[:, LAM], -1.0, 0.0, ALU.mult, ALU.max))
            link(V.tensor_tensor(col[:, SP + 6], col[:, SP + 6], col[:, SP + 5], ALU.add))
            link(V.tensor_scalar(col[:, SP], col[:, SP + 6], LRU_C / 2, None, ALU.mult))
            q = slice(F_Q, P)
            V.memset(f_ones[q], 1.0)
            dve.wait_ge(f_sum, 1)
            V.reciprocal(f_y[q], f_s[q]).then_inc(f_inv, 1)

            def query(s):
                split("mem_att", s // 4, s % 4 + 2)
                evac(mq_hi, s + 1, mq[:, s % 4, 1], ps[:, s % 2], mq[:, s % 4, 0], mq_lo)

            def mem_max(n):
                dve.wait_ge(ms_done, n + 1)
                r = 4 * (n % 2)
                for h in range(2):
                    c = slice(2 * h, 2 * h + 2)
                    link(V.reduce_max(rows[:, r, c], ps[:, MS_BANK[n] + h].rearrange("p (t m) -> p t m", m=NM), axis=AX.X))
                    V.tensor_scalar(rows[:, r + 1, c], rows[:, r, c], -MEM_SCALE, None, ALU.mult).then_inc(ms_max, 1)

            def mem_norm(n):
                r = 4 * (n % 2)
                for h in range(2):
                    dve.wait_ge(ms_exp, 4 * n + 2 * h + 2)
                    link(V.reciprocal(rows[:, r + 3, 2 * h:2 * h + 2], rows[:, r + 2, 2 * h:2 * h + 2]))
                    for t in (2 * h, 2 * h + 1):
                        V.tensor_scalar(mem_p[:, n % 2, t], mem_p[:, n % 2, t], rows[:, r + 3, t:t + 1], None,
                                        ALU.mult).then_inc(ms_p, 1)

            def mem_softmax(n):
                mem_max(n)
                mem_norm(n)

            def mem_turned(n):
                for j in range(MT):
                    evac(mt_hi, 2 * n + j + 1, mem_pT[n % 2][:, 1, j], ps[:, 6 + j], mem_pT[n % 2][:, 0, j], mt_lo)

            def mem_out(n):
                for f in range(2):
                    evac(yc_hi, 2 * n + f + 1, yc[:, 1, 2 * n + f], ps[:, MO_BANK[n] + f], yc[:, 0, 2 * n + f], yc_lo)

            def forget_sums(_):
                dve.wait_ge(f_soft, 1)
                link(V.tensor_tensor_scan(f_neg_c[q], f_ones[q], f_z[q], 0.0, ALU.mult, ALU.add))
                V.tensor_scalar(f_c[q], f_neg_c[q], -1.0, None, ALU.mult).then_inc(f_c_ready, 1)

            for step in MEM_ORDER_EVAC:
                {"w": lambda _: split("lru", 0, 2), "q": query, "s": mem_softmax, "t": mem_turned, "o": mem_out, "f": forget_sums}[step[0]](int(step[1]))
            link(V.memset(z_pad[:, 0:CONV_W - 1], 0.0))
            def lru_out(i):
                one = bass.ds(i, 1)
                evac(ya_hi, i + 1, ya[:, 1, one], l_h[:].rearrange("p (o t) -> p o t", o=1), ya[:, 0, one], ya_lo)

            def lru(i, first):
                one = bass.ds(i, 1)
                dve.wait_ge(z_copied, i + 1)
                link(V.tensor_scalar(xc[:], z_pad[:, 0:T], col[:, CW, one], col[:, CB, one], ALU.mult, ALU.add))
                for w in range(1, CONV_W):
                    ins = V.scalar_tensor_tensor(out=xc[:], in0=z_pad[:, w:w + T], scalar=col[:, CW + w, one],
                                                 in1=xc[:], op0=ALU.mult, op1=ALU.add)
                    if w < CONV_W - 1:
                        link(ins)
                    else:
                        ins.then_inc(xc_ready, 1)
                dve.wait_ge(wri_hi, i + 1)
                V.tensor_tensor(w_ri[:, 1], w_ri_raw[:], w_ri[:, 0].bitcast(F32), ALU.subtract).then_inc(wri_lo, 1)
                evac(xc_hi, i + 1, xcT[:, 1], xc[:], xcT[:, 0], xc_lo)
                if not first:
                    lru_out(i - 1)
                split("lru", i, 3)
                split("lru", i, 4)
                if first:
                    dve.wait_ge(c_stored, 32)
                dve.wait_ge(gate_ready, i + 1)
                dve.wait_ge(unit_used, units.count("lru", i, 2))
                V.tensor_tensor(merged[:, one], gate[:, 0:1], ps[:, 4:5], ALU.mult).then_inc(merged_done, 1)
                dve.wait_ge(lru_tanh, i + 1)
                link(V.tensor_scalar_add(l_a[:], l_t[:], 1.0))
                link(V.reciprocal(l_m[:], l_a[:]))
                V.tensor_scalar(l_a[:], l_m[:], 2.0, -1.0, ALU.mult, ALU.add)
                dve.wait_ge(lru_i, i + 1)
                link(V.tensor_tensor(l_i[:], l_i[:], xc[:], ALU.mult))
                split("lru", i, 5)
                link(V.tensor_tensor(l_i[:], l_i[:], l_m[:], ALU.mult))
                dve.wait_ge(lru_sqrt, i + 1)
                link(V.tensor_tensor(l_i[:], l_i[:], l_r[:], ALU.mult))
                V.tensor_tensor_scan(l_h[:], l_a[:], l_i[:], 0.0, ALU.mult, ALU.add).then_inc(lru_h, 1)

            lru(0, True)
            with dve.Fori(1, KD) as i:
                link.enter(i, 8, 1)
                lru(i, False)
            link.leave(KD)
            lru_out(KD - 1)

            def merge(phase, b, banks, last):
                def body(i, first):
                    if not first:
                        split(phase, i, 2)
                    split(phase, i, 3)
                    for s in range(2):
                        one = bass.ds(i * 2 + s, 1)
                        split(phase, i, s + 4)
                        dve.wait_ge(gate_ready, i * 2 + (BEFORE[b] + s + 1))
                        dve.wait_ge(unit_used, units.count(phase, i, 2 + s))
                        link(V.tensor_tensor(prod[:, s], gate[:, s], ps[:, banks[2 + s]], ALU.mult))
                        V.tensor_tensor(merged[:, one], merged[:, one], prod[:, s:s + 1], ALU.add).then_inc(merged_done, 1)
                        if last:
                            evac(mg_hi, i * 2 + s + 1, mgT[:, 1, one], merged[:, one], mgT[:, 0, one], mg_lo)

                body(0, not last)
                with dve.Fori(1, KD // 2) as i:
                    link.enter(i, 2, 1)
                    body(i, False)
                link.leave(KD // 2)

            merge("merge_a", "a", (5, 6, 7, 4), False)

            with dve.Fori(0, FOX_HEADS // 2) as i:
                link.enter(i, 2)

                def mins(n):
                    dve.wait_ge(c_landed[n], i * 16 + 16)
                    for t in range(NT):
                        dve.wait_ge(fs_read, i * 8 + 4 * n + t + 1)
                        V.memset(rows[:, 4 * n + 1, t:t + 1], 0.0)
                        p = fox_p[:, n, ROW[t]:ROW[t + 1]]
                        V.tensor_tensor_reduce(out=p, in0=p, in1=c_all[:, n, 0:(t + 1) * P], scale=1.0, scalar=BIG,
                                               op0=ALU.add, op1=ALU.min,
                                               accum_out=rows[:, 4 * n, t:t + 1]).then_inc(fs_min, 1)

                def norm(n):
                    dve.wait_ge(fs_exp, i * 8 + 4 * n + 4)
                    link(V.reciprocal(rows[:, 4 * n + 3], rows[:, 4 * n + 2]))
                    for t in range(NT):
                        p = fox_p[:, n, ROW[t]:ROW[t + 1]]
                        V.tensor_scalar(p, p, rows[:, 4 * n + 3, t:t + 1], None, ALU.mult).then_inc(fs_p, 1)

                def turned_p(n):
                    for g in range(3):
                        c = slice(TURN_START[g], TURN_START[g + 1])
                        evac(ft_hi, i * 6 + 3 * n + g + 1, fox_pT[:, n, 1, c],
                             ps[:, TURN_BANK[n][g], 0:c.stop - c.start], fox_pT[:, n, 0, c], ft_lo)

                def value(n, bank):
                    evac(vt_hi, i * 2 + n + 1, v_h[:, n, 1], ps[:, bank].rearrange("p (j n) -> p j n", n=P),
                         v_h[:, n, 0], vt_lo)

                def out_b(n, bank):
                    one = bass.ds(i * 2 + n, 1)
                    evac(yb_hi, i * 2 + n + 1, yb[:, 1, one], ps[:, bank:bank + 1], yb[:, 0, one], yb_lo)

                for s in range(4):
                    split("fox", i, s + 2)
                    evac(qk_hi, i * 4 + s + 1, qk[:, s, 1], ps[:, s % 2], qk[:, s, 0], qk_lo)
                mins(0)
                norm(0)
                split("fox", i, 6)
                mins(1)
                turned_p(0)
                value(0, 1)
                norm(1)
                split("fox", i, 7)
                turned_p(1)
                value(1, 1)
                out_b(0, 3)
                out_b(1, 6)
            link.leave(FOX_HEADS // 2)

            merge("merge_b", "b", (4, 5, 6, 7), True)

            for s in range(KD - 1):
                split("w_o", 0, s + 2)
            dve.wait_ge(gains2_landed, 48)
            def norm_after(t):
                variance(n2_sum, t + 1, t, t + 1, n2_var)
                rstd(n2_std, t + 1, t, t + 1)
                if t >= 2:
                    dve.wait_ge(h1_ready, t - 1)
                V.scalar_tensor_tensor(out=normed[:, t % 2], in0=ps[:, 2 * t:2 * t + 2].rearrange("p b n -> p (b n)"),
                                       scalar=stat[:, 3, t:t + 1], in1=g_post_all[:],
                                       op0=ALU.mult, op1=ALU.mult).then_inc(n2_ready, 1)
                if t == NT - 1:
                    dve.wait_ge(n2_ready, NT)
                    V.tensor_tensor(h1[:, t], h1[:, t], normed[:, t % 2], ALU.add).then_inc(h1_last, 1)

            def norm_before(t):
                variance(n3_sum, t + 1, 4 + t, 5 + t, n3_var)
                rstd(n3_std, t + 1, 4 + t, 5 + t)
                V.scalar_tensor_tensor(out=u2[:, t], in0=h1[:, t], scalar=stat[:, 3, 4 + t:5 + t],
                                       in1=g_pre2_all[:], op0=ALU.mult, op1=ALU.mult).then_inc(u2_ready, 1)

            def u2_turn(t):
                evac(u2_hi, t + 1, u2T[:, 1, :, t * P:(t + 1) * P],
                     ps[:, 2 * t:2 * t + 2].rearrange("p b (k n) -> p (b k) n", n=P),
                     u2T[:, 0, :, t * P:(t + 1) * P], pair_free)

            for step in NORM_ORDER:
                {"a": norm_after, "b": norm_before, "c": u2_turn,
                 "w": lambda s: split("mlp", 0, s)}[step[0]](int(step[1]))

            def mlp(i, first, final):
                for s in range(8):
                    if not (first and s == 0):
                        split("mlp", i, s + 2)
                    dve.wait_ge(up_relu, i * 8 + s + 1)
                    V.scalar_tensor_tensor(out=relu2[:, s % 2], in0=ps[:, s], scalar=0.0, in1=relu[:, s % 2],
                                           op0=ALU.max, op1=ALU.mult).then_inc(up_sq, 1)
                    evac(up_hi, i * 8 + s + 1, actT[:, 1, s], relu2[:, s % 2], actT[:, 0, s], act_ready)
                for s in range(8, 15):
                    if not (final and s == 14):
                        split("mlp", i, s + 2)
                for t in range(NT):
                    if t == NT - 1 and not final:
                        split("mlp", i, 17)
                    if t < NT - 1:
                        dve.wait_ge(down_done, i * (NT - 1) + t + 1)
                    else:
                        dve.wait_ge(unit_used, units.count("mlp", i, 15))
                    V.tensor_tensor(down_sum[:, t], down_sum[:, t],
                                    ps[:, 2 * t:2 * t + 2].rearrange("p b n -> p (b n)"),
                                    ALU.add).then_inc(n4_in if final else pair_free, 1)
                    if final:
                        variance(n4_sum, t + 1, t, t + 1, n4_var)
                        rstd(n4_std, t + 1, t, t + 1)
                        V.scalar_tensor_tensor(out=down_sum[:, t], in0=down_sum[:, t], scalar=stat[:, 3, t:t + 1],
                                               in1=g_post2_all[:], op0=ALU.mult, op1=ALU.mult).then_inc(n4_ready, 1)
                        if t == NT - 1:
                            dve.wait_ge(n4_ready, NT)
                            V.tensor_tensor(down_sum[:, t], down_sum[:, t], h1[:, t], ALU.add).then_inc(y_last, 1)

            dve.wait_ge(sums_zeroed, 1)
            mlp(0, True, False)
            with dve.Fori(1, 3) as i:
                mlp(i, False, False)
            mlp(3, False, True)

        @block.tensor
        def _(pe):
            def product(dst, lhs, rhs, start, stop):
                nc.tensor.matmul(dst, lhs(0), rhs(0), start=start, stop=False)
                nc.tensor.matmul(dst, lhs(0), rhs(1), start=False, stop=False)
                return nc.tensor.matmul(dst, lhs(1), rhs(0), start=False, stop=stop)

            def unit_ready(phase, i, s):
                pe.wait_ge(lo_done, units.count(phase, i, s))

            def columns(phase, i, s, dst, moving, before=None, used=True):
                unit_ready(phase, i, s)
                slot = units.slot(phase, s)
                for k in range(KD):
                    if before is not None:
                        before(k)
                    last = product(dst, lambda h: ring[:, slot, h, k * P:(k + 1) * P],
                                   lambda h: moving(h, k), k == 0, k == KD - 1)
                if used:
                    last.then_inc(unit_used, 1)

            def turn(t, src, bank):
                for k in range(KD):
                    last = nc.tensor.transpose(ps[:, bank + k // 4, (k % 4) * P:(k % 4 + 1) * P],
                                               src[:, k * P:(k + 1) * P], ident[:])
                return last

            from_u = lambda h, k: uT[:, h, k]

            pe.wait_ge(consts_ready, 2)
            for t in range(MT):
                pe.wait_ge(normed_ready, t + 1)
                turn(t, mem_in[:, t], 2 * t).then_inc(turned, 1)
            pe.wait_ge(turned_lo, MT)
            with pe.Fori(0, 2) as i:
                for s in range(4):
                    columns("mem_k", i, s, ps[:, 4 + s, 0:NM], lambda h, k: memT[:, h, k])

            def turn_x(t):
                pe.wait_ge(normed_ready, MT + t + 1)
                if t >= 2:
                    pe.wait_ge(turned_lo, MT + t - 1)
                turn(t, x_in[:, t], 2 * (t % 2)).then_inc(turned, 1)

            turn_x(0)
            turn_x(1)
            pe.wait_ge(mem_k_lo, KD)
            for k in range(KD):
                unit_ready("mem_v", 0, k)
                slot = units.slot("mem_v", k)
                for j in range(MT):
                    for h in range(2):
                        last = product(ps[:, 4 + 2 * j + h], lambda w: memT[:, w, k, j * P:(j + 1) * P],
                                       lambda w: ring[:, slot, w, h * T:(h + 1) * T], k == 0, k == KD - 1)
                    if k == KD - 1 and j == 0:
                        last.then_inc(mem_v_done, 1)
                last.then_inc(unit_used, 1)
                if k == 3:
                    turn_x(2)
                if k == 5:
                    turn_x(3)
            pe.wait_ge(turned_lo, MT + NT)
            columns("mem_v", 0, KD, ps[:, 0], from_u)

            pe.wait_ge(mem_v_lo, MT)
            pe.wait_ge(f_read, 1)

            def query(s):
                if s >= 2:
                    pe.wait_ge(mq_lo, s - 1)
                columns("mem_att", 0, s, ps[:, s % 2], from_u)

            def mem_scores(n):
                pe.wait_ge(mq_lo, 2 * n + 2)
                if n == 2:
                    pe.wait_ge(yc_lo, 2)
                if n == 3:
                    pe.wait_ge(ms_exp, 8)
                for t in range(NT):
                    dst = ps[:, MS_BANK[n] + t // 2, (t % 2) * NM:(t % 2 + 1) * NM]
                    for d in range(2):
                        last = product(dst, lambda w: mq[:, 2 * (n % 2) + d, w, t * P:(t + 1) * P],
                                       lambda w: mem_k[:, w, 2 * n + d], d == 0, d == 1)
                last.then_inc(ms_done, 1)

            def mem_turn(n):
                pe.wait_ge(ms_p, 4 * n + 4)
                for j in range(MT):
                    if n:
                        pe.wait_ge(mt_lo, 2 * n - 1 + j)
                    for t in range(NT):
                        last = nc.tensor.transpose(ps[:, 6 + j, t * P:(t + 1) * P],
                                                   mem_p[:, n % 2, t, j * P:(j + 1) * P], ident[:])
                    last.then_inc(mt_done, 1)

            def mem_outputs(n):
                pe.wait_ge(mt_lo, 2 * n + 2)
                if n == 1:
                    pe.wait_ge(mq_lo, 8)
                for f in range(2):
                    for j in range(MT):
                        last = product(ps[:, MO_BANK[n] + f],
                                       lambda w: mem_v[:, w, j, n * NM + f * P:n * NM + (f + 1) * P],
                                       lambda w: mem_pT[n % 2][:, w, j], j == 0, j == MT - 1)
                    last.then_inc(yc_done, 1)

            def lru_in(s, i=0):
                columns("lru", i, s, ps[:, s], from_u)

            def lru_rest(i):
                if not (isinstance(i, int) and i == 0):
                    pe.wait_ge(merged_done, i)
                columns("lru", i, 2, ps[:, 4], lambda h, k: yc[:, h, k],
                        (lambda k: pe.wait_ge(yc_lo, k + 1)) if isinstance(i, int) else None)
                pe.wait_ge(xc_lo, i + 1)
                pe.wait_ge(wri_lo, i + 1)
                for n in range(2):
                    product(ps[:, 2 + n], lambda w: w_ri[:, w, n], lambda w: xcT[:, w], True, True).then_inc(ri_done, 1)

            for step in MEM_ORDER:
                if step == "l0":
                    pe.wait_ge(yc_lo, 4)
                {"q": query, "s": mem_scores, "t": mem_turn, "o": mem_outputs, "l": lru_in}[step[0]](int(step[1]))
            lru_rest(0)
            with pe.Fori(1, KD) as i:
                lru_in(0, i)
                lru_in(1, i)
                lru_rest(i)

            def merge(phase, b, banks, y, y_ready, y_count):
                with pe.Fori(0, KD // 2) as i:
                    for s in range(2):
                        pe.wait_ge(gate_ready, i * 2 + BEFORE[b])
                        columns(phase, i, s, ps[:, banks[s]], from_u)
                    pe.wait_ge(y_ready, y_count)
                    for s in range(2):
                        pe.wait_ge(merged_done, i * 2 + BEFORE[b])
                        columns(phase, i, 2 + s, ps[:, banks[2 + s]], lambda h, k: y[:, h, k])

            merge("merge_a", "a", (5, 6, 7, 4), ya, ya_lo, KD)

            pe.wait_ge(consts_rounded, 2)
            with pe.Fori(0, FOX_HEADS // 2) as i:
                def project(s, bank):
                    columns("fox", i, s, ps[:, bank], from_u)

                def scores(n):
                    for t in range(NT):
                        if n:
                            pe.wait_ge(fs_read, i * 8 + t + 1)
                        dst = ps[:, 2 + t, 0:(t + 1) * P]
                        product(dst, lambda w: qk[:, 2 * n, w, t * P:(t + 1) * P],
                                lambda w: qk[:, 2 * n + 1, w, 0:(t + 1) * P], True, False)
                        nc.tensor.matmul(ps[:, 2 + t, t * P:(t + 1) * P], identR[:], maskR[:],
                                         start=False, stop=True).then_inc(fs_done, 1)

                def turn_v(n, bank):
                    pe.wait_ge(v_copied, i * 2 + n + 1)
                    for j in range(NT):
                        last = nc.tensor.transpose(ps[:, bank, j * P:(j + 1) * P], v_f[:, j * P:(j + 1) * P], ident[:])
                    last.then_inc(vt_done, 1)

                def turn_p(n):
                    pe.wait_ge(fs_p, i * 8 + 4 * n + 4)
                    for g, keys in enumerate(TURNS):
                        if n == 0 and g == 2:
                            pe.wait_ge(v_copied, i * 2 + 1)
                        if n == 1 and g == 2:
                            pe.wait_ge(ft_lo, i * 6 + 2)
                        at_col = 0
                        for j in keys:
                            for t in range(j, NT):
                                last = nc.tensor.transpose(ps[:, TURN_BANK[n][g], at_col:at_col + P],
                                                           fox_p[:, n, ROW[t] + j * P:ROW[t] + (j + 1) * P], ident[:])
                                at_col += P
                        last.then_inc(ft_done, 1)

                def outputs(n, bank):
                    pe.wait_ge(vt_lo, i * 2 + n + 1)
                    for g, keys in enumerate(TURNS):
                        pe.wait_ge(ft_lo, i * 6 + 3 * n + g + 1)
                        at_col = TURN_START[g]
                        for j in keys:
                            c = slice(at_col, at_col + (NT - j) * P)
                            last = product(ps[:, bank, j * P:T], lambda w: v_h[:, n, w, j],
                                           lambda w: fox_pT[:, n, w, c], g == 0, g == len(TURNS) - 1)
                            at_col = c.stop
                    last.then_inc(yb_done, 1)

                project(0, 0)
                project(1, 1)
                pe.wait_ge(qk_lo, i * 4 + 1)
                project(2, 0)
                pe.wait_ge(qk_lo, i * 4 + 2)
                project(3, 1)
                scores(0)
                pe.wait_ge(qk_lo, i * 4 + 3)
                project(4, 0)
                pe.wait_ge(qk_lo, i * 4 + 4)
                scores(1)
                turn_p(0)
                turn_v(0, 1)
                pe.wait_ge(fs_read, i * 8 + 5)
                project(5, 2)
                turn_p(1)
                pe.wait_ge(vt_lo, i * 2 + 1)
                turn_v(1, 1)
                outputs(0, 3)
                outputs(1, 6)

            merge("merge_b", "b", (4, 5, 6, 7), yb, yb_lo, FOX_HEADS)

            def rows_units(phase, i, s0, left, n_k, tile_done, before_unit, before_tile):
                def tile(k, t):
                    slot = units.slot(phase, s0 + k)
                    if k == 0:
                        before_tile(t)
                    for h in range(2):
                        last = product(ps[:, 2 * t + h], lambda w: left(w, k, t),
                                       lambda w: ring[:, slot, w, h * T:(h + 1) * T], k == 0, k == n_k - 1)
                    return last

                for k in range(n_k - LATE):
                    before_unit(k)
                    unit_ready(phase, i, s0 + k)
                    for t in range(NT):
                        last = tile(k, t)
                    last.then_inc(unit_used, 1)
                for t in range(NT):
                    for k in range(n_k - LATE, n_k):
                        if t == 0:
                            before_unit(k)
                            unit_ready(phase, i, s0 + k)
                        last = tile(k, t)
                        if t == NT - 1:
                            last.then_inc(unit_used, 1)
                    if t < NT - 1:
                        last.then_inc(tile_done, 1)

            def bank_evacuated(t):
                if t == 2:
                    pe.wait_ge(gate_ready, 3 * KD)
                if t == 3:
                    pe.wait_ge(mg_lo, KD)

            rows_units("w_o", 0, 0, lambda w, k, t: mgT[:, w, k, t * P:(t + 1) * P], KD, wo_done,
                       lambda k: pe.wait_ge(mg_lo, k + 1), bank_evacuated)
            def up(i, s, c=slice(0, T), used=True):
                columns("mlp", i, s, ps[:, s, c], lambda h, k: u2T[:, h, k, c], used=used)

            def down(i):
                rows_units("mlp", i, 8, lambda w, k, t: actT[:, w, k, t * P:(t + 1) * P], 8, down_done,
                           lambda k: pe.wait_ge(act_ready, i * 8 + k + 1),
                           lambda t: pe.wait_ge(act_ready, i * 8 + 2 * t + 2))

            def turn_u2(t):
                pe.wait_ge(u2_ready, t + 1)
                turn(t, u2[:, t], 2 * t).then_inc(u2_turned, 1)

            HALF = (slice(0, T // 2), slice(T // 2, T))
            turn_u2(0)
            turn_u2(1)
            pe.wait_ge(pair_free, 2)
            up(0, 0, HALF[0], used=False)
            turn_u2(2)
            up(0, 1, HALF[0], used=False)
            turn_u2(3)
            up(0, 2, HALF[0], used=False)
            pe.wait_ge(pair_free, NT)
            for s in range(3):
                up(0, s, HALF[1])
            for s in range(3, 8):
                up(0, s)
            down(0)
            with pe.Fori(1, 4) as i:
                for s in range(8):
                    pe.wait_ge(pair_free, i * 4 + s // 2 + 1)
                    up(i, s)
                down(i)


_INS = ["x", "mem", "g_mix_pre", "w_in", "conv_w", "conv_b", "w_r", "b_r", "w_i", "b_i", "lru_lambda", "b_f",
        "g_mem", "w_mem_kv", "b_gate", "w_pa", "w_pb", "w_pc", "w_o", "g_mix_post", "g_mlp_pre", "w_up",
        "w_down", "g_mlp_post"]


def kernel(**inputs):
    import concourse.bacc as bacc
    from concourse.bass_utils import run_bass_kernel_spmd

    nc = bacc.Bacc("TRN2", target_bir_lowering=False, num_devices=1)
    arrays, args = {}, []
    for name in _INS:
        a = np.ascontiguousarray(inputs[name])
        arrays[f"in_{name}"] = a
        args.append(nc.dram_tensor(f"in_{name}", a.shape, mybir.dt.from_np(a.dtype), kind="ExternalInput").ap())
    args.append(nc.dram_tensor("out_y", (1, T, D), F32, kind="ExternalOutput").ap())
    block_program(nc, *args)
    r = run_bass_kernel_spmd(nc, [arrays], core_ids=[0])
    return r.results[0]["out_y"]
```

```python
from contextlib import ExitStack

import numpy as np
import concourse.bass as bass
from concourse import mybir

F32 = mybir.dt.float32
F32R = mybir.dt.float32r
ALU = mybir.AluOpType
ACT = mybir.ActivationFunctionType
AX = mybir.AxisListType

P = 128
T = 512
NT = T // P
D = 1024
KD = D // P
NM = 256
MT = NM // P
FOX_HEADS = 8
MEM_HEADS = 4
CONV_W = 4
EPS = 1e-6
LRU_C = 8.0
OFF_Q, OFF_K, OFF_V, OFF_MQ = D, 2 * D, 3 * D, 4 * D
OFF_GATE = 5 * D
OFF_F = 8 * D
N_IN = OFF_F + FOX_HEADS
FOX_SCALE = float(D // FOX_HEADS) ** -0.5
MEM_SCALE = float(D // MEM_HEADS) ** -0.5
MASKED = -1e30
BIG = 3e38
F_ROW = P - FOX_HEADS
F_Q = 96
LOG1P_TERMS = (1 / 15, 1 / 13, 1 / 11, 1 / 9, 1 / 7, 1 / 5, 1 / 3)
SLOTS = 4
LATE_O, LATE_DOWN = 4, 3

PHASES = {
    "mem_k": ((0, 1, 2, 3), 2),
    "mem_v": ((0, 1, 2, 3, 0, 1, 2, 3, 2), 1),
    "mem_att": ((0, 1, 2, 3), 2),
    "lru": ((0, 1, 2), 8),
    "merge_a": ((0, 1, 2, 3), 4),
    "fox": ((0, 1, 0, 1, 2, 3), 4),
    "merge_b": ((0, 1, 2, 3), 4),
    "w_o": ((0, 1, 2, 3, 0, 1, 2, 3), 1),
    "mlp": ((0, 1, 2, 3) * 4, 4),
}


class Units:

    def __init__(self):
        self.base, self.uses, self.first = {}, {}, {}
        n, use, last = 0, [0] * SLOTS, [None] * SLOTS
        for name, (slots, iters) in PHASES.items():
            self.base[name], self.uses[name] = n, list(use)
            self.first[name] = [None if x is None else x - n for x in last]
            for i in range(iters):
                for s, slot in enumerate(slots):
                    use[slot] += 1
                    last[slot] = n
                    n += 1

    def slot(self, phase, s):
        slots = PHASES[phase][0]
        return slots[s % len(slots)]

    def count(self, phase, i, s):
        return i * len(PHASES[phase][0]) + (self.base[phase] + s + 1)

    def loaded(self, phase, i, s):
        slots = PHASES[phase][0]
        s_in, more = s % len(slots), s // len(slots)
        per = slots.count(slots[s_in])
        nth = slots[:s_in].count(slots[s_in]) + 1
        return i * (16 * per) + 16 * (self.uses[phase][slots[s_in]] + more * per + nth)

    def before(self, phase, i, s):
        slots = PHASES[phase][0]
        size = len(slots)
        slot = slots[s % size]
        for back in range(s - 1, -1, -1):
            if slots[back % size] == slot:
                return i * size + (self.base[phase] + back + 1)
        earlier = self.first[phase][slot]
        if isinstance(i, int) and i == 0:
            return None if earlier is None else self.base[phase] + earlier + 1
        wrapped = s - 1
        while slots[wrapped % size] != slot:
            wrapped -= 1
        if earlier is not None:
            wrapped = max(wrapped, earlier)
        return i * size + (self.base[phase] + wrapped + 1)


class From1:

    def __init__(self, n):
        self.n = n

    def __mul__(self, m):
        return self.n * m + (-m)


class Chain:

    def __init__(self, eng, sem):
        self.eng, self.sem, self.n, self.i, self.per = eng, sem, 0, None, 0

    def __call__(self, ins):
        self.n += 1
        ins.then_inc(self.sem, 1)
        self.eng.wait_ge(self.sem, self.n if self.i is None else self.i * self.per + self.n)

    def enter(self, i, per, first=0):
        self.n -= per * first
        self.i, self.per, self.start = i, per, self.n

    def leave(self, end):
        assert self.n - self.start == self.per, (self.n - self.start, self.per)
        self.n = self.start + self.per * end
        self.i = None


def block_program(nc, x, mem, g_mix_pre, w_in, conv_w, conv_b, w_r, b_r, w_i, b_i, lru_lambda,
                  b_f, g_mem, w_mem_kv, b_gate, w_pa, w_pb, w_pc, w_o, g_mix_post, g_mlp_pre,
                  w_up, w_down, g_mlp_post, out):
    ctx = ExitStack()
    units = Units()
    KB = 1024
    with ctx:
        ctx.enter_context(nc.allow_non_contiguous_dma("small parameter columns"))
        base = -(-nc.sbuf_base // 32) * 32
        ctx.enter_context(nc.sbuf_tensor("arena", [P, 207 * 256], F32))

        def at(name, kib, shape, dt=F32):
            return nc.alloc_sbuf_tensor_at(name, [P] + shape, dt, offset=base + int(kib * KB))

        def sem(name):
            return ctx.enter_context(nc.semaphore(name))

        RING, RAW, UT, Y0, Y1, E, MG, TMP, CONST = 0, 32, 48, 80, 112, 144, 168, 184, 204
        ring = at("ring", RING, [SLOTS, 2, D], F32R)
        raw = at("raw", RAW, [SLOTS, D])
        uT = at("uT", UT, [2, KD, T], F32R)
        yc = at("yc", Y0, [2, KD, T], F32R)
        ya = at("ya", Y1, [2, KD, T], F32R)
        yb = at("yb", Y0, [2, KD, T], F32R)
        mgT = at("mgT", Y1, [2, KD, T], F32R)
        merged = at("merged", MG, [KD, T])
        x_in = at("x_in", MG, [NT, D])
        mem_in = at("mem_in", TMP, [MT, D])
        squares = at("squares", TMP + 8, [D])
        squares_v = at("squares_v", Y0 + 8, [D])
        g_mem_all = at("g_mem_all", Y0, [D])
        g_mix_all = at("g_mix_all", Y0 + 4, [D])
        memT = at("memT", Y1, [2, KD, NM], F32R)
        mem_k = at("mem_k", Y1 + 16, [2, KD, NM], F32R)
        mem_v = at("mem_v", E, [2, MT, D], F32R)
        f_z = at("f_z", MG, [T])
        f_exp_abs = at("f_exp_abs", MG + 2, [T])
        f_ratio = at("f_ratio", MG + 4, [T])
        f_work = at("f_work", MG + 6, [T])
        f_poly = at("f_poly", MG + 8, [T])
        f_ones = at("f_ones", MG + 10, [T])
        f_relu = at("f_relu", TMP + 16, [T])
        f_neg_c = at("f_neg_c", MG + 12, [T])
        f_c = at("f_c", MG + 14, [T])
        mqT = at("mqT", Y1, [4, 2, T], F32R)
        mem_pT = [at("mem_pT0", E + 16, [2, MT, T], F32R), at("mem_pT1", TMP + 8, [2, MT, T], F32R)]
        mem_p = at("mem_p", TMP, [2, NT, NM])
        xcT = at("xcT", E, [2, T], F32R)
        w_ri = at("w_ri", E + 4, [2, 2, P], F32R)
        z_pad = at("z_pad", TMP, [T + 8])
        xc = at("xc", TMP + 2.5, [T])
        lru_r_sq = at("lru_r_sq", TMP + 4.5, [T])
        lru_in_x = at("lru_in_x", TMP + 6.5, [T])
        lru_t = at("lru_t", TMP + 8.5, [T])
        lru_a = at("lru_a", TMP + 10.5, [T])
        lru_v = at("lru_v", TMP + 12.5, [T])
        lru_hT = at("lru_hT", TMP + 14.5, [T])
        w_ri_raw = at("w_ri_raw", TMP + 16.5, [2, P])
        gate = at("gate", E + 12, [2, T])
        prod = at("prod", E + 16, [2, T])
        qkT = at("qkT", Y1, [4, 2, T], F32R)
        v_fox = at("v_fox", Y1 + 16, [2, NT, 2, P], F32R)
        ROW = [P * t * (t + 1) // 2 for t in range(NT + 1)]
        TURNS = ((0,), (1, 3), (2,))
        TURN_START = (0, NT * P, 2 * NT * P, ROW[NT])
        TURN_BANK = ((0, 1, 6), (4, 5, 0))
        fox_pT = at("fox_pT", E, [2, 2, ROW[NT]], F32R)
        fox_p = at("fox_p", TMP, [2, ROW[NT]])
        c_all = at("c_all", TMP + 12, [2, T])
        h1 = at("h1", TMP, [NT, D])
        g_post_all = at("g_post_all", E, [D])
        g_pre2_all = at("g_pre2_all", E + 4, [D])
        g_post2_all = at("g_post2_all", E + 8, [D])
        normed = at("normed", E + 12, [2, D])
        squares_wo = at("squares_wo", E + 20, [D])
        squares_h1 = at("squares_h1", Y0 + 16, [D])
        u2 = at("u2", Y0, [NT, D])
        u2T = at("u2T", UT, [2, KD, T], F32R)
        actT = at("actT", Y0, [2, KD, T], F32R)
        relu = at("relu", E + 12, [2, T])
        relu2 = at("relu2", E + 16, [2, T])
        down_sum = at("down_sum", MG, [NT, D])
        ident = at("ident", CONST, [P])
        identR = at("identR", CONST + 0.5, [P], F32R)
        mask = at("mask", CONST + 1, [P])
        maskR = at("maskR", CONST + 1.5, [P], F32R)
        col = at("col", CONST + 2, [27, 8])
        stat = at("stat", CONST + 2.875, [4, 8])
        f_col = at("f_col", TMP + 18, [8])
        CW, CB, BR, BI, LAM, BG, NQ, SP = 0, 4, 5, 6, 7, 8, 11, 15
        rows = at("rows", CONST + 3, [8, 4])

        ps = ctx.enter_context(nc.psum_tensor("ps", [P, 8, T], F32))
        c_dram = nc.dram_tensor("c_scratch", [2, FOX_HEADS, T], F32, kind="Internal").ap()

        slot_loaded = [sem(f"slot_loaded{s}") for s in range(SLOTS)]
        hi_done, lo_done, unit_used = sem("hi_done"), sem("lo_done"), sem("unit_used")
        act_link, dve_link, pool_link = sem("act_link"), sem("dve_link"), sem("pool_link")
        mem_landed = [sem(f"mem_landed{t}") for t in range(MT)]
        x_landed = [sem(f"x_landed{t}") for t in range(NT)]
        g_mem_landed, g_mix_landed = sem("g_mem_landed"), sem("g_mix_landed")
        cols_landed, consts_ready = sem("cols_landed"), sem("consts_ready")
        consts_rounded = sem("consts_rounded")
        norm_sum, norm_var, norm_std = sem("norm_sum"), sem("norm_var"), sem("norm_std")
        dve_sum = sem("dve_sum")
        normed_ready, turned, turned_hi, turned_lo = (
            sem("normed_ready"), sem("turned"), sem("turned_hi"), sem("turned_lo"))
        mem_k_hi, mem_k_lo = sem("mem_k_hi"), sem("mem_k_lo")
        mem_v_done, mem_v_hi, mem_v_lo = sem("mem_v_done"), sem("mem_v_hi"), sem("mem_v_lo")
        f_read, f_exp, f_sum, f_inv, f_soft, f_c_ready = (
            sem("f_read"), sem("f_exp"), sem("f_sum"), sem("f_inv"), sem("f_soft"), sem("f_c_ready"))
        c_stored, c_cols_landed = sem("c_stored"), sem("c_cols_landed")
        lam_exp = sem("lam_exp")
        mq_hi, mq_lo = sem("mq_hi"), sem("mq_lo")
        ms_done, ms_max, ms_exp, ms_p = sem("ms_done"), sem("ms_max"), sem("ms_exp"), sem("ms_p")
        mt_done, mt_hi, mt_lo = sem("mt_done"), sem("mt_hi"), sem("mt_lo")
        yc_done, yc_hi, yc_lo = sem("yc_done"), sem("yc_hi"), sem("yc_lo")
        wri_landed, wri_hi, wri_lo = sem("wri_landed"), sem("wri_hi"), sem("wri_lo")
        z_copied, xc_ready, xc_hi, xc_lo = (
            sem("z_copied"), sem("xc_ready"), sem("xc_hi"), sem("xc_lo"))
        ri_done, lru_r, lru_tanh, lru_i, lru_sqrt, lru_h, ya_lo = (
            sem("ri_done"), sem("lru_r"), sem("lru_tanh"), sem("lru_i"), sem("lru_sqrt"),
            sem("lru_h"), sem("ya_lo"))
        ya_hi = sem("ya_hi")
        gate_ready, merged_done = sem("gate_ready"), sem("merged_done")
        BEFORE = {"c": 0, "a": KD, "b": 2 * KD}
        mg_hi, mg_lo = sem("mg_hi"), sem("mg_lo")
        qk_hi, qk_lo = sem("qk_hi"), sem("qk_lo")
        v_done, v_hi, v_lo = sem("v_done"), sem("v_hi"), sem("v_lo")
        fs_done, fs_read, fs_min, fs_exp, fs_p = (
            sem("fs_done"), sem("fs_read"), sem("fs_min"), sem("fs_exp"), sem("fs_p"))
        ft_done, ft_hi, ft_lo = sem("ft_done"), sem("ft_hi"), sem("ft_lo")
        yb_done, yb_hi, yb_lo = sem("yb_done"), sem("yb_hi"), sem("yb_lo")
        c_landed = [sem("c_landed_a"), sem("c_landed_b")]
        gains2_landed, x2_landed = sem("gains2_landed"), sem("x2_landed")
        wo_done = sem("wo_done")
        n2_ready, n4_ready, h1_last, y_last = sem("n2_ready"), sem("n4_ready"), sem("h1_last"), sem("y_last")
        n2_sum, n2_var, n2_std, h1_ready, n3_sum, n3_var, n3_std, u2_ready = (
            sem("n2_sum"), sem("n2_var"), sem("n2_std"), sem("h1_ready"), sem("n3_sum"),
            sem("n3_var"), sem("n3_std"), sem("u2_ready"))
        u2_turned, u2_hi, pair_free = sem("u2_turned"), sem("u2_hi"), sem("pair_free")
        sums_zeroed = sem("sums_zeroed")
        up_relu, up_sq, up_hi, act_ready, down_done = (
            sem("up_relu"), sem("up_sq"), sem("up_hi"), sem("act_ready"),
            sem("down_done"))
        n4_in, n4_sum, n4_var, n4_std, y_ready, stored = (
            sem("n4_in"), sem("n4_sum"), sem("n4_var"), sem("n4_std"), sem("y_ready"), sem("stored"))

        block = ctx.enter_context(nc.Block())

        MEM_ORDER = "q0 q1 q2 s0 q3 q4 s1 q5 t0 q6 o0 t1 q7 s2 o1 s3 t2 l0 t3 o2 l1 o3".split()
        MEM_ORDER_EVAC = "q0 q1 q2 q3 s0 q4 q5 s1 t0 q6 o0 t1 q7 f0 s2 o1 s3 t2 t3 z0 o2 w0 o3".split()
        MS_BANK, MO_BANK = (2, 4, 2, 4), (2, 0, 2, 6)

        NORM_ORDER = "a0 a1 b0 a2 b1 w0 c0 c1 w1 a3 b2 w2 b3 w3 c2 c3".split()

        w_in_v = w_in.rearrange("o (k p) n -> p (o k) n", p=P)
        w_kv_v = w_mem_kv.rearrange("o (k p) n -> p (o k) n", p=P)
        w_up_v = w_up.rearrange("o (k p) n -> p (o k) n", p=P)
        proj_v = {"a": w_pa.rearrange("o (k p) n -> p (o k) n", p=P),
                  "b": w_pb.rearrange("o (k p) n -> p (o k) n", p=P),
                  "c": w_pc.rearrange("o (k p) n -> p (o k) n", p=P)}
        w_o_v = w_o.rearrange("o (k p) n -> p (o k) n", p=P)
        w_down_v = w_down.rearrange("o (k p) n -> p (o k) n", p=P)
        x_v = x.rearrange("o (t p) d -> p (o t) d", p=P)
        out_v = out.rearrange("o (t p) d -> p (o t) d", p=P)
        GATE_OFF = {"a": OFF_GATE, "b": OFF_GATE + D, "c": OFF_GATE + 2 * D}

        @block.sync
        def _(sp):
            def cols(view, start):
                return view[:, :, bass.ds(start, P)]

            def load(phase, i, s, src):
                slot = units.slot(phase, s)
                used = units.before(phase, i, s)
                if used is not None:
                    sp.wait_ge(lo_done, used)
                dst = raw[:, slot]
                if len(src.shape) == 3 and src.shape[1] == KD:
                    dst = dst.rearrange("p (k n) -> p k n", k=KD)
                sp.dma_start(dst, src).then_inc(slot_loaded[slot], 16)

            mem_rows = mem.rearrange("o (t p) d -> p (o t) d", p=P)
            for t in range(MT):
                sp.dma_start(mem_in[:, t], mem_rows[:, t]).then_inc(mem_landed[t], 16)
            sp.dma_start(g_mem_all[:], g_mem.partition_broadcast(P)[:, 0]).then_inc(g_mem_landed, 16)
            for m in range(KD):
                load("mem_k", m // 4, m % 4, cols(w_kv_v, m * P))
                if m >= 3 and m < 3 + NT:
                    sp.dma_start(x_in[:, m - 3], x_v[:, m - 3]).then_inc(x_landed[m - 3], 16)
            for k in range(KD):
                load("mem_v", 0, k, w_kv_v[:, k, D:2 * D])
            load("mem_v", 0, KD, cols(w_in_v, N_IN - P))
            with sp.Fori(0, 2) as i:
                for s in range(4):
                    load("mem_att", i, s, cols(w_in_v, i * (4 * P) + (OFF_MQ + s * P)))
            def lru_loads(i):
                load("lru", i, 0, cols(w_in_v, i * P))
                load("lru", i, 1, cols(w_in_v, i * P + GATE_OFF["c"]))
                load("lru", i, 2, cols(proj_v["c"], i * P))

            wri_v = [w.rearrange("o h i j -> i (o h) j") for w in (w_r, w_i)]
            lru_loads(0)
            sp.wait_ge(f_soft, 1)
            for g in range(2):
                sp.dma_start(w_ri_raw[:, g], wri_v[g][:, 0]).then_inc(wri_landed, 16)
            with sp.Fori(1, KD) as i:
                lru_loads(i)
                sp.wait_ge(wri_lo, i)
                for g in range(2):
                    sp.dma_start(w_ri_raw[:, g], wri_v[g][:, bass.ds(i, 1)]).then_inc(wri_landed, 16)

            def merge_loads(phase, b):
                with sp.Fori(1, KD // 2 + 1) as n:
                    i = From1(n)
                    for s in range(2):
                        load(phase, i, s, cols(w_in_v, i * (2 * P) + (GATE_OFF[b] + s * P)))
                    for s in range(2):
                        load(phase, i, 2 + s, cols(proj_v[b], i * (2 * P) + s * P))

            merge_loads("merge_a", "a")
            with sp.Fori(0, FOX_HEADS // 2) as i:
                for s, off in enumerate((OFF_Q, OFF_K, OFF_Q + P, OFF_K + P, OFF_V, OFF_V + P)):
                    load("fox", i, s, cols(w_in_v, i * (2 * P) + off))
            merge_loads("merge_b", "b")
            for k in range(KD):
                load("w_o", 0, k, w_o_v[:, k])
            with sp.Fori(1, 5) as n:
                i = From1(n)
                for s in range(8):
                    load("mlp", i, s, cols(w_up_v, i * D + s * P))
                for s in range(8):
                    load("mlp", i, 8 + s, w_down_v[:, bass.ds(i * KD + s, 1)])
            for t in range(NT):
                if t < NT - 1:
                    sp.wait_ge(y_ready, t + 1)
                    sp.dma_start(out_v[:, t], down_sum[:, t]).then_inc(stored, 16)
                else:
                    for h in range(2):
                        sp.wait_ge(*((y_ready, NT) if h == 0 else (y_last, 1)))
                        sp.dma_start(out_v[:, t, h * T:(h + 1) * T], down_sum[:, t, h * T:(h + 1) * T]).then_inc(stored, 16)
            sp.wait_ge(stored, 16 * (NT + 1))

        @block.gpsimd
        def _(pool):
            link = Chain(pool, pool_link)
            link(nc.gpsimd.memset(ident[:], 0.0))
            link(nc.gpsimd.memset(mask[:], 0.0))
            nc.gpsimd.affine_select(out=ident[:], in_=ident[:], compare_op=ALU.not_equal, fill=1.0,
                                    base=0, pattern=[[-1, P]], channel_multiplier=1).then_inc(consts_ready, 1)
            nc.gpsimd.affine_select(out=mask[:], in_=mask[:], compare_op=ALU.is_ge, fill=MASKED,
                                    base=0, pattern=[[-1, P]], channel_multiplier=1).then_inc(consts_ready, 1)
            pool.dma_start(g_mix_all[:], g_mix_pre.partition_broadcast(P)[:, 0]).then_inc(g_mix_landed, 16)
            link(nc.gpsimd.memset(f_col[:], 0.0))
            for w in range(CONV_W):
                pool.dma_start(col[:, CW + w], conv_w[0, w].rearrange("(j p) -> p j", p=P)).then_inc(cols_landed, 16)
            pool.dma_start(col[:, CB], conv_b[0].rearrange("(j p) -> p j", p=P)).then_inc(cols_landed, 16)
            pool.dma_start(col[:, BR], b_r[0].rearrange("j p -> p j")).then_inc(cols_landed, 16)
            pool.dma_start(col[:, BI], b_i[0].rearrange("j p -> p j")).then_inc(cols_landed, 16)
            pool.dma_start(col[:, LAM], lru_lambda[0].rearrange("(j p) -> p j", p=P)).then_inc(cols_landed, 16)
            for b in range(3):
                pool.dma_start(col[:, BG + b], b_gate[0, b].rearrange("(j p) -> p j", p=P)).then_inc(cols_landed, 16)
            pool.dma_start(f_col[F_ROW:P, 0:1], b_f.rearrange("o h -> h o")).then_inc(cols_landed, 16)
            q = slice(F_Q, P)
            G = nc.gpsimd
            pool.wait_ge(f_exp, 1)
            G.tensor_scalar(f_ratio[q], f_exp_abs[q], 2.0, 1.0, ALU.add, ALU.mult).then_inc(f_sum, 1)
            pool.wait_ge(f_inv, 1)
            link(G.tensor_tensor(f_ratio[q], f_exp_abs[q], f_work[q], ALU.mult))
            link(G.tensor_tensor(f_work[q], f_ratio[q], f_ratio[q], ALU.mult))
            link(G.tensor_scalar(f_poly[q], f_work[q], LOG1P_TERMS[0], 1.0, ALU.mult, ALU.mult))
            for term in LOG1P_TERMS[1:]:
                link(G.tensor_scalar(f_poly[q], f_poly[q], term, 1.0, ALU.add, ALU.mult))
                link(G.tensor_tensor(f_poly[q], f_poly[q], f_work[q], ALU.mult))
            link(G.tensor_scalar(f_poly[q], f_poly[q], 1.0, 2.0, ALU.add, ALU.mult))
            link(G.tensor_tensor(f_poly[q], f_poly[q], f_ratio[q], ALU.mult))
            G.tensor_tensor(f_z[q], f_relu[q], f_poly[q], ALU.add).then_inc(f_soft, 1)
            pool.wait_ge(f_c_ready, 1)
            pool.dma_start(c_dram[0], f_neg_c[F_ROW:P, :]).then_inc(c_stored, 16)
            pool.dma_start(c_dram[1], f_c[F_ROW:P, :]).then_inc(c_stored, 16)
            pool.wait_ge(c_stored, 32)
            for t in range(NT):
                pool.dma_start(col[:, NQ + t], c_dram[0, :, t * P:(t + 1) * P].rearrange("h p -> p h")).then_inc(c_cols_landed, 16)
            pool.wait_ge(merged_done, 2 * KD)
            for n in range(2):
                pool.dma_start(c_all[:, n], c_dram[1, n:n + 1].partition_broadcast(P)[:, 0]).then_inc(c_landed[n], 16)
            with pool.Fori(0, FOX_HEADS // 2 - 1) as i:
                for n in range(2):
                    pool.wait_ge(fs_min, i * 8 + 4 * (n + 1))
                    pool.dma_start(c_all[:, n], c_dram[1, bass.ds(i * 2 + (n + 2), 1)].partition_broadcast(P)[:, 0]).then_inc(c_landed[n], 16)
            pool.wait_ge(yb_lo, FOX_HEADS)
            for g, dst in ((g_mix_post, g_post_all), (g_mlp_pre, g_pre2_all), (g_mlp_post, g_post2_all)):
                pool.dma_start(dst[:], g.partition_broadcast(P)[:, 0]).then_inc(gains2_landed, 16)
            pool.dma_start(h1[:], x_v).then_inc(x2_landed, 16)
            pool.wait_ge(mg_lo, KD)
            nc.gpsimd.memset(down_sum[:], 0.0).then_inc(sums_zeroed, 1)
            pool.wait_ge(x2_landed, 16)
            for t in range(NT - 1):
                pool.wait_ge(n2_ready, t + 1)
                G.tensor_tensor(h1[:, t], h1[:, t], normed[:, t % 2], ALU.add).then_inc(h1_ready, 1)
            for t in range(NT):
                c = slice(0, D if t < NT - 1 else T)
                pool.wait_ge(n4_ready, t + 1)
                G.tensor_tensor(down_sum[:, t, c], down_sum[:, t, c], h1[:, t, c], ALU.add).then_inc(y_ready, 1)

        @block.scalar
        def _(act):
            A = nc.scalar.activation

            def split(phase, i, s):
                slot = units.slot(phase, s)
                act.wait_ge(slot_loaded[slot], units.loaded(phase, i, s))
                used = units.before(phase, i, s)
                if used is not None:
                    act.wait_ge(unit_used, used)
                A(ring[:, slot, 0], raw[:, slot], ACT.Copy).then_inc(hi_done, 1)

            def evac(ready, value, dst, src, done):
                act.wait_ge(ready, value)
                A(dst, src, ACT.Copy).then_inc(done, 1)

            nc.scalar.preload_act_table(ACT.Sqrt)
            act.wait_ge(mem_landed[0], 16)
            A(squares[:], mem_in[:, 0], ACT.Square, accum_out=stat[:, 0, 0:1]).then_inc(norm_sum, 1)
            for t in range(MT):
                act.wait_ge(norm_var, t + 1)
                A(stat[:, 2, t:t + 1], stat[:, 1, t:t + 1], ACT.Sqrt).then_inc(norm_std, 1)
            for t in range(MT):
                split("mem_k", 0, t)
                evac(turned, t + 1, memT[:, 0, :, t * P:(t + 1) * P],
                     ps[:, 2 * t:2 * t + 2].rearrange("p b (k n) -> p (b k) n", n=P), turned_hi)
            for m in range(KD):
                split("mem_k", 0, m + 2)
                evac(unit_used, units.count("mem_k", 0, m), mem_k[:, 0, m], ps[:, 4 + m % 4, 0:NM], mem_k_hi)
                if 2 <= m < 2 + NT:
                    t = m - 2
                    act.wait_ge(x_landed[t], 16)
                    act.wait_ge(norm_sum, MT - 1 + t)
                    A(squares[:], x_in[:, t], ACT.Square, accum_out=stat[:, 0, MT + t:MT + t + 1]).then_inc(norm_sum, 1)
                    act.wait_ge(norm_var, MT + t + 1)
                    A(stat[:, 2, MT + t:MT + t + 1], stat[:, 1, MT + t:MT + t + 1], ACT.Sqrt).then_inc(norm_std, 1)

            def x_turned(t):
                evac(turned, MT + t + 1, uT[:, 0, :, t * P:(t + 1) * P],
                     ps[:, 2 * (t % 2):2 * (t % 2) + 2].rearrange("p b (k n) -> p (b k) n", n=P), turned_hi)

            for s in range(KD + 1):
                if s == 0:
                    x_turned(0)
                split("mem_v", 0, s + 2)
                if s == 0:
                    x_turned(1)
                if s == 3:
                    x_turned(2)
                if s == 5:
                    x_turned(3)
                if s == KD - 1:
                    for j in range(MT):
                        evac(*((mem_v_done, 1) if j == 0 else (unit_used, units.count("mem_v", 0, KD - 1))), mem_v[:, 0, j],
                             ps[:, 4 + 2 * j:6 + 2 * j].rearrange("p b n -> p (b n)"), mem_v_hi)
            act.wait_ge(cols_landed, 16 * 12)
            A(col[:, SP + 1], col[:, LAM], ACT.Abs).then_inc(act_link, 1)
            act.wait_ge(act_link, 1)
            A(col[:, SP + 2], col[:, SP + 1], ACT.Exp, scale=-1.0).then_inc(lam_exp, 1)
            q = slice(F_Q, P)
            act.wait_ge(unit_used, units.count("mem_v", 0, KD))
            A(f_z[q], ps[q, 0], ACT.Identity, bias=f_col[q, 0:1]).then_inc(f_read, 1)
            act.wait_ge(f_read, 1)
            A(f_relu[q], f_z[q], ACT.Relu, scale=-1.0)
            A(f_exp_abs[q], f_z[q], ACT.Abs).then_inc(act_link, 1)
            act.wait_ge(act_link, 2)
            A(f_exp_abs[q], f_exp_abs[q], ACT.Exp, scale=-1.0).then_inc(f_exp, 1)

            def query(s):
                split("mem_att", s // 4, s % 4 + 2)
                evac(unit_used, units.count("mem_att", 0, s), mqT[:, s % 4, 0], ps[:, s % 2], mq_hi)

            def mem_exp(n):
                for t in range(NT):
                    if t % 2 == 0:
                        act.wait_ge(ms_max, 2 * n + t // 2 + 1)
                    A(mem_p[:, n % 2, t], ps[:, MS_BANK[n] + t // 2, (t % 2) * NM:(t % 2 + 1) * NM], ACT.Exp,
                      bias=rows[:, 4 * (n % 2) + 1, t:t + 1], scale=MEM_SCALE,
                      accum_out=rows[:, 4 * (n % 2) + 2, t:t + 1]).then_inc(ms_exp, 1)

            def mem_turned(n):
                for j in range(MT):
                    evac(mt_done, 2 * n + j + 1, mem_pT[n % 2][:, 0, j], ps[:, 6 + j], mt_hi)

            def mem_out(n):
                for f in range(2):
                    evac(yc_done, 2 * n + f + 1, yc[:, 0, 2 * n + f], ps[:, MO_BANK[n] + f], yc_hi)

            def lru_column(i):
                nc.scalar.preload_act_table(ACT.Sigmoid)
                act.wait_ge(unit_used, units.count("lru", i, 0))
                A(z_pad[:, CONV_W - 1:CONV_W - 1 + T], ps[:, 0], ACT.Copy).then_inc(z_copied, 1)

            for step in MEM_ORDER_EVAC:
                if step[0] != "f":
                    {"w": lambda _: split("lru", 0, 2), "z": lru_column, "q": query, "s": mem_exp,
                     "t": mem_turned, "o": mem_out}[step[0]](int(step[1]))

            def lru_out(i):
                evac(lru_h, i + 1, ya[:, 0, bass.ds(i, 1)], lru_hT[:].rearrange("p (o t) -> p o t", o=1), ya_hi)

            def lru(i, first):
                one = bass.ds(i, 1)
                if not first:
                    lru_column(i)
                act.wait_ge(wri_landed, i * 32 + 32)
                A(w_ri[:, 0], w_ri_raw[:], ACT.Copy).then_inc(wri_hi, 1)
                if not first:
                    lru_out(i - 1)
                split("lru", i, 3)
                act.wait_ge(xc_ready, i + 1)
                A(xcT[:, 0], xc[:], ACT.Copy).then_inc(xc_hi, 1)
                act.wait_ge(unit_used, units.count("lru", i, 1))
                A(gate[:, 0], ps[:, 1], ACT.Sigmoid, bias=col[:, BG + 2, one]).then_inc(gate_ready, 1)
                split("lru", i, 4)
                act.wait_ge(ri_done, i * 2 + 1)
                A(lru_r_sq[:], ps[:, 2], ACT.Sigmoid, bias=col[:, BR, one]).then_inc(lru_r, 1)
                act.wait_ge(lru_r, i + 1)
                A(lru_t[:], lru_r_sq[:], ACT.Tanh, scale=col[:, SP, one]).then_inc(lru_tanh, 1)
                act.wait_ge(ri_done, i * 2 + 2)
                A(lru_in_x[:], ps[:, 3], ACT.Sigmoid, bias=col[:, BI, one]).then_inc(lru_i, 1)
                split("lru", i, 5)
                act.wait_ge(lru_tanh, i + 1)
                A(lru_r_sq[:], lru_t[:], ACT.Sqrt, scale=4.0).then_inc(lru_sqrt, 1)

            lru(0, True)
            with act.Fori(1, KD) as i:
                lru(i, False)
            lru_out(KD - 1)

            def merge(phase, b, banks, last):
                def body(i, first):
                    nc.scalar.preload_act_table(ACT.Sigmoid)
                    for s in range(2):
                        if not (first and s == 0):
                            split(phase, i, s + 2)
                        act.wait_ge(unit_used, units.count(phase, i, s))
                        act.wait_ge(merged_done, i * 2 + BEFORE[b])
                        A(gate[:, s], ps[:, banks[s]], ACT.Sigmoid,
                          bias=col[:, BG + "abc".index(b), bass.ds(i * 2 + s, 1)]).then_inc(gate_ready, 1)
                    for s in range(2):
                        split(phase, i, s + 4)
                        if last:
                            one = bass.ds(i * 2 + s, 1)
                            evac(merged_done, i * 2 + (BEFORE[b] + s + 1), mgT[:, 0, one], merged[:, one], mg_hi)

                body(0, not last)
                with act.Fori(1, KD // 2) as i:
                    body(i, False)

            merge("merge_a", "a", (5, 6, 7, 4), False)

            act.wait_ge(c_cols_landed, 16 * NT)
            with act.Fori(0, FOX_HEADS // 2) as i:
                def scores(n):
                    for t in range(NT):
                        act.wait_ge(fs_done, i * 8 + 4 * n + t + 1)
                        A(fox_p[:, n, ROW[t]:ROW[t + 1]], ps[:, 2 + t, 0:(t + 1) * P], ACT.Identity,
                          bias=col[:, NQ + t, bass.ds(i * 2 + n, 1)], scale=-FOX_SCALE).then_inc(fs_read, 1)

                def exps(n):
                    for t in range(NT):
                        act.wait_ge(fs_min, i * 8 + 4 * n + t + 1)
                        p = fox_p[:, n, ROW[t]:ROW[t + 1]]
                        A(p, p, ACT.Exp, bias=rows[:, 4 * n, t:t + 1], scale=-1.0,
                          accum_out=rows[:, 4 * n + 2, t:t + 1]).then_inc(fs_exp, 1)

                def turned_p(n):
                    for g in range(3):
                        c = slice(TURN_START[g], TURN_START[g + 1])
                        evac(ft_done, i * 6 + 3 * n + g + 1, fox_pT[:, n, 0, c],
                             ps[:, TURN_BANK[n][g], 0:c.stop - c.start], ft_hi)

                def project(s):
                    evac(unit_used, units.count("fox", i, s), qkT[:, s, 0], ps[:, s % 2], qk_hi)

                def values(g, ready, value):
                    evac(ready, value, v_fox[:, 0, 2 * g:2 * g + 2].rearrange("p j a n -> p (j a n)"), ps[:, 6 + g], v_hi)

                def out_b(n, bank):
                    evac(yb_done, i * 2 + n + 1, yb[:, 0, bass.ds(i * 2 + n, 1)], ps[:, bank:bank + 1], yb_hi)

                project(0)
                split("fox", i, 2)
                project(1)
                split("fox", i, 3)
                split("fox", i, 4)
                project(2)
                split("fox", i, 5)
                scores(0)
                exps(0)
                project(3)
                split("fox", i, 6)
                values(0, v_done, i + 1)
                scores(1)
                turned_p(0)
                exps(1)
                split("fox", i, 7)
                values(1, unit_used, units.count("fox", i, 5))
                turned_p(1)
                out_b(0, 3)
                out_b(1, 2)

            merge("merge_b", "b", (4, 5, 6, 7), True)

            for s in range(KD - 2):
                split("w_o", 0, s + 2)
            nc.scalar.preload_act_table(ACT.Sqrt)
            def norm_after(t):
                act.wait_ge(*((wo_done, t + 1) if t < NT - 1 else (unit_used, units.count("w_o", 0, KD - 1))))
                A(squares_wo[:], ps[:, 2 * t:2 * t + 2].rearrange("p b n -> p (b n)"), ACT.Square,
                  accum_out=stat[:, 0, t:t + 1]).then_inc(n2_sum, 1)
                act.wait_ge(n2_var, t + 1)
                A(stat[:, 2, t:t + 1], stat[:, 1, t:t + 1], ACT.Sqrt).then_inc(n2_std, 1)

            def norm_before(t):
                act.wait_ge(*((h1_ready, t + 1) if t < NT - 1 else (h1_last, 1)))
                A(squares_h1[:], h1[:, t], ACT.Square, accum_out=stat[:, 0, 4 + t:5 + t]).then_inc(n3_sum, 1)
                act.wait_ge(n3_var, t + 1)
                A(stat[:, 2, 4 + t:5 + t], stat[:, 1, 4 + t:5 + t], ACT.Sqrt).then_inc(n3_std, 1)

            def u2_turn(t):
                evac(u2_turned, t + 1, u2T[:, 0, :, t * P:(t + 1) * P],
                     ps[:, 2 * t:2 * t + 2].rearrange("p b (k n) -> p (b k) n", n=P), u2_hi)

            for step in NORM_ORDER:
                {"a": norm_after, "b": norm_before, "c": u2_turn,
                 "w": lambda s: split("mlp", 0, s)}[step[0]](int(step[1]))

            def mlp(i, first, final):
                for s in range(8):
                    if not (first and s < 2):
                        split("mlp", i, s + 2)
                    act.wait_ge(unit_used, units.count("mlp", i, s))
                    A(relu[:, s % 2], ps[:, s], ACT.Relu).then_inc(up_relu, 1)
                    evac(up_sq, i * 8 + s + 1, actT[:, 0, s], relu2[:, s % 2], up_hi)
                for s in range(8, 16):
                    if not (final and s >= 14):
                        split("mlp", i, s + 2)

            mlp(0, True, False)
            with act.Fori(1, 3) as i:
                mlp(i, False, False)
            mlp(3, False, True)
            for t in range(NT):
                act.wait_ge(n4_in, t + 1)
                if t:
                    act.wait_ge(n4_sum, t)
                if t < NT - 1:
                    A(squares_wo[:], down_sum[:, t], ACT.Square, accum_out=stat[:, 0, t:t + 1]).then_inc(n4_sum, 1)
                else:
                    A(squares_wo[:, 0:T], down_sum[:, t, 0:T], ACT.Square, accum_out=stat[:, 0, t:t + 1]).then_inc(n4_sum, 1)
                    act.wait_ge(n4_in, NT + 1)
                    A(squares_wo[:, T:D], down_sum[:, t, T:D], ACT.Square,
                      accum_out=stat[:, 0, NT:NT + 1]).then_inc(n4_sum, 1)
                act.wait_ge(n4_var, t + 1)
                A(stat[:, 2, t:t + 1], stat[:, 1, t:t + 1], ACT.Sqrt).then_inc(n4_std, 1)

        @block.vector
        def _(dve):
            V = nc.vector
            link = Chain(dve, dve_link)

            def split(phase, i, s):
                slot = units.slot(phase, s)
                dve.wait_ge(hi_done, units.count(phase, i, s))
                V.tensor_tensor(ring[:, slot, 1], raw[:, slot], ring[:, slot, 0].bitcast(F32),
                                ALU.subtract).then_inc(lo_done, 1)

            def evac(hi_sem, value, dst, src, hi, done):
                dve.wait_ge(hi_sem, value)
                V.tensor_tensor(dst, src, hi.bitcast(F32), ALU.subtract).then_inc(done, 1)

            def log1p(e, s, y, p):
                link(V.tensor_scalar_add(s, e, 2.0))
                link(V.reciprocal(y, s))
                link(V.tensor_tensor(s, e, y, ALU.mult))
                link(V.tensor_tensor(y, s, s, ALU.mult))
                link(V.tensor_scalar(p, y, LOG1P_TERMS[0], None, ALU.mult))
                for term in LOG1P_TERMS[1:]:
                    link(V.scalar_tensor_tensor(out=p, in0=p, scalar=term, in1=y, op0=ALU.add, op1=ALU.mult))
                link(V.scalar_tensor_tensor(out=p, in0=p, scalar=1.0, in1=s, op0=ALU.add, op1=ALU.mult))
                link(V.tensor_scalar(p, p, 2.0, None, ALU.mult))

            def variance(sums, value, lo, hi, done):
                dve.wait_ge(sums, value)
                V.tensor_scalar(stat[:, 1, lo:hi], stat[:, 0, lo:hi], 1.0 / D, EPS, ALU.mult, ALU.add).then_inc(done, 1)

            def rstd(stds, value, lo, hi):
                dve.wait_ge(stds, value)
                link(V.reciprocal(stat[:, 3, lo:hi], stat[:, 2, lo:hi]))

            variance(norm_sum, 1, 0, 1, norm_var)
            dve.wait_ge(mem_landed[1], 16)
            V.tensor_tensor_reduce(out=squares_v[:], in0=mem_in[:, 1], in1=mem_in[:, 1], scale=1.0, scalar=0.0,
                                   op0=ALU.mult, op1=ALU.add, accum_out=stat[:, 0, 1:2]).then_inc(dve_sum, 1)
            variance(dve_sum, 1, 1, 2, norm_var)
            dve.wait_ge(g_mem_landed, 16)
            for t in range(MT):
                rstd(norm_std, t + 1, t, t + 1)
                V.scalar_tensor_tensor(out=mem_in[:, t], in0=mem_in[:, t], scalar=stat[:, 3, t:t + 1],
                                       in1=g_mem_all[:], op0=ALU.mult, op1=ALU.mult).then_inc(normed_ready, 1)

            def turned_to(dst, n, t, bank):
                evac(turned_hi, n + 1, dst[:, 1, :, t * P:(t + 1) * P],
                     ps[:, bank:bank + 2].rearrange("p b (k n) -> p (b k) n", n=P),
                     dst[:, 0, :, t * P:(t + 1) * P], turned_lo)

            for t in range(MT):
                split("mem_k", 0, t)
                turned_to(memT, t, t, 2 * t)
            dve.wait_ge(consts_ready, 2)
            V.tensor_copy(identR[:], ident[:]).then_inc(consts_rounded, 1)
            V.tensor_copy(maskR[:], mask[:]).then_inc(consts_rounded, 1)
            for m in range(KD):
                split("mem_k", 0, m + 2)
                evac(mem_k_hi, m + 1, mem_k[:, 1, m], ps[:, 4 + m % 4, 0:NM], mem_k[:, 0, m], mem_k_lo)
                if 2 <= m < 2 + NT:
                    t = m - 2
                    variance(norm_sum, MT + t, MT + t, MT + t + 1, norm_var)
                    rstd(norm_std, MT + t + 1, MT + t, MT + t + 1)
                    if t == 0:
                        dve.wait_ge(g_mix_landed, 16)
                    V.scalar_tensor_tensor(out=x_in[:, t], in0=x_in[:, t], scalar=stat[:, 3, MT + t:MT + t + 1],
                                           in1=g_mix_all[:], op0=ALU.mult, op1=ALU.mult).then_inc(normed_ready, 1)
            for s in range(KD + 1):
                if s == 0:
                    turned_to(uT, MT, 0, 0)
                split("mem_v", 0, s + 2)
                if s == 0:
                    turned_to(uT, MT + 1, 1, 2)
                if s == 3:
                    turned_to(uT, MT + 2, 2, 0)
                if s == 5:
                    turned_to(uT, MT + 3, 3, 2)
                if s == KD - 1:
                    for j in range(MT):
                        evac(mem_v_hi, j + 1, mem_v[:, 1, j],
                             ps[:, 4 + 2 * j:6 + 2 * j].rearrange("p b n -> p (b n)"), mem_v[:, 0, j], mem_v_lo)
            dve.wait_ge(lam_exp, 1)
            log1p(col[:, SP + 2], col[:, SP + 3], col[:, SP + 4], col[:, SP + 5])
            link(V.tensor_scalar(col[:, SP + 6], col[:, LAM], -1.0, 0.0, ALU.mult, ALU.max))
            link(V.tensor_tensor(col[:, SP + 6], col[:, SP + 6], col[:, SP + 5], ALU.add))
            link(V.tensor_scalar(col[:, SP], col[:, SP + 6], LRU_C / 2, None, ALU.mult))
            q = slice(F_Q, P)
            V.memset(f_ones[q], 1.0)
            dve.wait_ge(f_sum, 1)
            V.reciprocal(f_work[q], f_ratio[q]).then_inc(f_inv, 1)

            def query(s):
                split("mem_att", s // 4, s % 4 + 2)
                evac(mq_hi, s + 1, mqT[:, s % 4, 1], ps[:, s % 2], mqT[:, s % 4, 0], mq_lo)

            def mem_max(n):
                dve.wait_ge(ms_done, n + 1)
                r = 4 * (n % 2)
                for h in range(2):
                    c = slice(2 * h, 2 * h + 2)
                    link(V.reduce_max(rows[:, r, c], ps[:, MS_BANK[n] + h].rearrange("p (t m) -> p t m", m=NM), axis=AX.X))
                    V.tensor_scalar(rows[:, r + 1, c], rows[:, r, c], -MEM_SCALE, None, ALU.mult).then_inc(ms_max, 1)

            def mem_norm(n):
                r = 4 * (n % 2)
                for h in range(2):
                    dve.wait_ge(ms_exp, 4 * n + 2 * h + 2)
                    link(V.reciprocal(rows[:, r + 3, 2 * h:2 * h + 2], rows[:, r + 2, 2 * h:2 * h + 2]))
                    for t in (2 * h, 2 * h + 1):
                        V.tensor_scalar(mem_p[:, n % 2, t], mem_p[:, n % 2, t], rows[:, r + 3, t:t + 1], None,
                                        ALU.mult).then_inc(ms_p, 1)

            def mem_softmax(n):
                mem_max(n)
                mem_norm(n)

            def mem_turned(n):
                for j in range(MT):
                    evac(mt_hi, 2 * n + j + 1, mem_pT[n % 2][:, 1, j], ps[:, 6 + j], mem_pT[n % 2][:, 0, j], mt_lo)

            def mem_out(n):
                for f in range(2):
                    evac(yc_hi, 2 * n + f + 1, yc[:, 1, 2 * n + f], ps[:, MO_BANK[n] + f], yc[:, 0, 2 * n + f], yc_lo)

            def forget_sums(_):
                dve.wait_ge(f_soft, 1)
                link(V.tensor_tensor_scan(f_neg_c[q], f_ones[q], f_z[q], 0.0, ALU.mult, ALU.add))
                V.tensor_scalar(f_c[q], f_neg_c[q], -1.0, None, ALU.mult).then_inc(f_c_ready, 1)

            def convolution(i):
                one = bass.ds(i, 1)
                dve.wait_ge(z_copied, i + 1)
                link(V.tensor_scalar(xc[:], z_pad[:, 0:T], col[:, CW, one], col[:, CB, one], ALU.mult, ALU.add))
                for w in range(1, CONV_W):
                    ins = V.scalar_tensor_tensor(out=xc[:], in0=z_pad[:, w:w + T], scalar=col[:, CW + w, one],
                                                 in1=xc[:], op0=ALU.mult, op1=ALU.add)
                    if w < CONV_W - 1:
                        link(ins)
                    else:
                        ins.then_inc(xc_ready, 1)

            def first_convolution(i):
                link(V.memset(z_pad[:, 0:CONV_W - 1], 0.0))
                convolution(i)

            for step in MEM_ORDER_EVAC:
                {"w": lambda _: split("lru", 0, 2), "z": first_convolution, "q": query, "s": mem_softmax,
                 "t": mem_turned, "o": mem_out, "f": forget_sums}[step[0]](int(step[1]))

            def lru_out(i):
                one = bass.ds(i, 1)
                evac(ya_hi, i + 1, ya[:, 1, one], lru_hT[:].rearrange("p (o t) -> p o t", o=1), ya[:, 0, one], ya_lo)

            def lru(i, first):
                one = bass.ds(i, 1)
                if not first:
                    convolution(i)
                dve.wait_ge(wri_hi, i + 1)
                V.tensor_tensor(w_ri[:, 1], w_ri_raw[:], w_ri[:, 0].bitcast(F32), ALU.subtract).then_inc(wri_lo, 1)
                evac(xc_hi, i + 1, xcT[:, 1], xc[:], xcT[:, 0], xc_lo)
                if not first:
                    lru_out(i - 1)
                split("lru", i, 3)
                split("lru", i, 4)
                if first:
                    dve.wait_ge(c_stored, 32)
                dve.wait_ge(gate_ready, i + 1)
                dve.wait_ge(unit_used, units.count("lru", i, 2))
                V.tensor_tensor(merged[:, one], gate[:, 0:1], ps[:, 4:5], ALU.mult).then_inc(merged_done, 1)
                dve.wait_ge(lru_tanh, i + 1)
                link(V.tensor_scalar_add(lru_a[:], lru_t[:], 1.0))
                link(V.reciprocal(lru_v[:], lru_a[:]))
                V.tensor_scalar(lru_a[:], lru_v[:], 2.0, -1.0, ALU.mult, ALU.add)
                dve.wait_ge(lru_i, i + 1)
                link(V.tensor_tensor(lru_in_x[:], lru_in_x[:], xc[:], ALU.mult))
                split("lru", i, 5)
                link(V.tensor_tensor(lru_in_x[:], lru_in_x[:], lru_v[:], ALU.mult))
                dve.wait_ge(lru_sqrt, i + 1)
                link(V.tensor_tensor(lru_in_x[:], lru_in_x[:], lru_r_sq[:], ALU.mult))
                V.tensor_tensor_scan(lru_hT[:], lru_a[:], lru_in_x[:], 0.0, ALU.mult, ALU.add).then_inc(lru_h, 1)

            lru(0, True)
            with dve.Fori(1, KD) as i:
                link.enter(i, 8, 1)
                lru(i, False)
            link.leave(KD)
            lru_out(KD - 1)

            def merge(phase, b, banks, last):
                def body(i, first):
                    if not first:
                        split(phase, i, 2)
                    split(phase, i, 3)
                    for s in range(2):
                        one = bass.ds(i * 2 + s, 1)
                        split(phase, i, s + 4)
                        dve.wait_ge(gate_ready, i * 2 + (BEFORE[b] + s + 1))
                        dve.wait_ge(unit_used, units.count(phase, i, 2 + s))
                        link(V.tensor_tensor(prod[:, s], gate[:, s], ps[:, banks[2 + s]], ALU.mult))
                        V.tensor_tensor(merged[:, one], merged[:, one], prod[:, s:s + 1], ALU.add).then_inc(merged_done, 1)
                        if last:
                            evac(mg_hi, i * 2 + s + 1, mgT[:, 1, one], merged[:, one], mgT[:, 0, one], mg_lo)

                body(0, not last)
                with dve.Fori(1, KD // 2) as i:
                    link.enter(i, 2, 1)
                    body(i, False)
                link.leave(KD // 2)

            merge("merge_a", "a", (5, 6, 7, 4), False)

            with dve.Fori(0, FOX_HEADS // 2) as i:
                link.enter(i, 2)

                def mins(n):
                    dve.wait_ge(c_landed[n], i * 16 + 16)
                    for t in range(NT):
                        dve.wait_ge(fs_read, i * 8 + 4 * n + t + 1)
                        V.memset(rows[:, 4 * n + 1, t:t + 1], 0.0)
                        p = fox_p[:, n, ROW[t]:ROW[t + 1]]
                        V.tensor_tensor_reduce(out=p, in0=p, in1=c_all[:, n, 0:(t + 1) * P], scale=1.0, scalar=BIG,
                                               op0=ALU.add, op1=ALU.min,
                                               accum_out=rows[:, 4 * n, t:t + 1]).then_inc(fs_min, 1)

                def norm(n):
                    dve.wait_ge(fs_exp, i * 8 + 4 * n + 4)
                    link(V.reciprocal(rows[:, 4 * n + 3], rows[:, 4 * n + 2]))
                    for t in range(NT):
                        p = fox_p[:, n, ROW[t]:ROW[t + 1]]
                        V.tensor_scalar(p, p, rows[:, 4 * n + 3, t:t + 1], None, ALU.mult).then_inc(fs_p, 1)

                def turned_p(n):
                    for g in range(3):
                        c = slice(TURN_START[g], TURN_START[g + 1])
                        evac(ft_hi, i * 6 + 3 * n + g + 1, fox_pT[:, n, 1, c],
                             ps[:, TURN_BANK[n][g], 0:c.stop - c.start], fox_pT[:, n, 0, c], ft_lo)

                def project(s):
                    evac(qk_hi, i * 4 + s + 1, qkT[:, s, 1], ps[:, s % 2], qkT[:, s, 0], qk_lo)

                def values(g):
                    both = [v_fox[:, w, 2 * g:2 * g + 2].rearrange("p j a n -> p (j a n)") for w in range(2)]
                    evac(v_hi, i * 2 + g + 1, both[1], ps[:, 6 + g], both[0], v_lo)

                def out_b(n, bank):
                    one = bass.ds(i * 2 + n, 1)
                    evac(yb_hi, i * 2 + n + 1, yb[:, 1, one], ps[:, bank:bank + 1], yb[:, 0, one], yb_lo)

                project(0)
                split("fox", i, 2)
                project(1)
                split("fox", i, 3)
                split("fox", i, 4)
                project(2)
                split("fox", i, 5)
                mins(0)
                norm(0)
                project(3)
                split("fox", i, 6)
                values(0)
                mins(1)
                turned_p(0)
                norm(1)
                split("fox", i, 7)
                values(1)
                turned_p(1)
                out_b(0, 3)
                out_b(1, 2)
            link.leave(FOX_HEADS // 2)

            merge("merge_b", "b", (4, 5, 6, 7), True)

            for s in range(KD - 2):
                split("w_o", 0, s + 2)
            dve.wait_ge(gains2_landed, 48)
            def norm_after(t):
                variance(n2_sum, t + 1, t, t + 1, n2_var)
                rstd(n2_std, t + 1, t, t + 1)
                if t >= 2:
                    dve.wait_ge(h1_ready, t - 1)
                V.scalar_tensor_tensor(out=normed[:, t % 2], in0=ps[:, 2 * t:2 * t + 2].rearrange("p b n -> p (b n)"),
                                       scalar=stat[:, 3, t:t + 1], in1=g_post_all[:],
                                       op0=ALU.mult, op1=ALU.mult).then_inc(n2_ready, 1)
                if t == NT - 1:
                    dve.wait_ge(n2_ready, NT)
                    V.tensor_tensor(h1[:, t], h1[:, t], normed[:, t % 2], ALU.add).then_inc(h1_last, 1)

            def norm_before(t):
                variance(n3_sum, t + 1, 4 + t, 5 + t, n3_var)
                rstd(n3_std, t + 1, 4 + t, 5 + t)
                V.scalar_tensor_tensor(out=u2[:, t], in0=h1[:, t], scalar=stat[:, 3, 4 + t:5 + t],
                                       in1=g_pre2_all[:], op0=ALU.mult, op1=ALU.mult).then_inc(u2_ready, 1)

            def u2_turn(t):
                evac(u2_hi, t + 1, u2T[:, 1, :, t * P:(t + 1) * P],
                     ps[:, 2 * t:2 * t + 2].rearrange("p b (k n) -> p (b k) n", n=P),
                     u2T[:, 0, :, t * P:(t + 1) * P], pair_free)

            for step in NORM_ORDER:
                {"a": norm_after, "b": norm_before, "c": u2_turn,
                 "w": lambda s: split("mlp", 0, s)}[step[0]](int(step[1]))

            def mlp(i, first, final):
                for s in range(8):
                    if not (first and s < 2):
                        split("mlp", i, s + 2)
                    dve.wait_ge(up_relu, i * 8 + s + 1)
                    V.scalar_tensor_tensor(out=relu2[:, s % 2], in0=ps[:, s], scalar=0.0, in1=relu[:, s % 2],
                                           op0=ALU.max, op1=ALU.mult).then_inc(up_sq, 1)
                    evac(up_hi, i * 8 + s + 1, actT[:, 1, s], relu2[:, s % 2], actT[:, 0, s], act_ready)
                for s in range(8, 15):
                    if not (final and s == 14):
                        split("mlp", i, s + 2)
                def add_down(t, c, done):
                    V.tensor_tensor(down_sum[:, t, c], down_sum[:, t, c],
                                    ps[:, 2 * t:2 * t + 2].rearrange("p b n -> p (b n)")[:, c], ALU.add).then_inc(done, 1)

                def scale(t, c, done):
                    V.scalar_tensor_tensor(out=down_sum[:, t, c], in0=down_sum[:, t, c], scalar=stat[:, 3, t:t + 1],
                                           in1=g_post2_all[:, c], op0=ALU.mult, op1=ALU.mult).then_inc(done, 1)

                every, first_half, second_half = slice(0, D), slice(0, T), slice(T, D)
                for t in range(NT if not final else NT - 1):
                    if t == NT - 1:
                        split("mlp", i, 17)
                        dve.wait_ge(unit_used, units.count("mlp", i, 15))
                    else:
                        dve.wait_ge(down_done, i * (NT - 1) + t + 1)
                    add_down(t, every, n4_in if final else pair_free)
                    if final:
                        if t == NT - 2:
                            dve.wait_ge(down_done, i * (NT - 1) + NT)
                            add_down(NT - 1, first_half, n4_in)
                        variance(n4_sum, t + 1, t, t + 1, n4_var)
                        rstd(n4_std, t + 1, t, t + 1)
                        if t == NT - 2:
                            dve.wait_ge(unit_used, units.count("mlp", i, 15))
                            add_down(NT - 1, second_half, n4_in)
                        scale(t, every, n4_ready)
                if final:
                    t = NT - 1
                    dve.wait_ge(n4_sum, NT)
                    link(V.tensor_scalar(stat[:, 1, t:t + 1], stat[:, 0, t:t + 1], 1.0 / D, EPS, ALU.mult, ALU.add))
                    dve.wait_ge(n4_sum, NT + 1)
                    V.scalar_tensor_tensor(out=stat[:, 1, t:t + 1], in0=stat[:, 0, NT:NT + 1], scalar=1.0 / D,
                                           in1=stat[:, 1, t:t + 1], op0=ALU.mult, op1=ALU.add).then_inc(n4_var, 1)
                    rstd(n4_std, NT, t, t + 1)
                    scale(t, first_half, n4_ready)
                    scale(t, second_half, n4_ready)
                    dve.wait_ge(n4_ready, NT + 1)
                    V.tensor_tensor(down_sum[:, t, second_half], down_sum[:, t, second_half], h1[:, t, second_half],
                                    ALU.add).then_inc(y_last, 1)

            dve.wait_ge(sums_zeroed, 1)
            mlp(0, True, False)
            with dve.Fori(1, 3) as i:
                mlp(i, False, False)
            mlp(3, False, True)

        @block.tensor
        def _(pe):
            def product(dst, lhs, rhs, start, stop):
                nc.tensor.matmul(dst, lhs(0), rhs(0), start=start, stop=False)
                nc.tensor.matmul(dst, lhs(0), rhs(1), start=False, stop=False)
                return nc.tensor.matmul(dst, lhs(1), rhs(0), start=False, stop=stop)

            def unit_ready(phase, i, s):
                pe.wait_ge(lo_done, units.count(phase, i, s))

            def columns(phase, i, s, dst, moving, before=None, used=True):
                unit_ready(phase, i, s)
                slot = units.slot(phase, s)
                for k in range(KD):
                    if before is not None:
                        before(k)
                    last = product(dst, lambda h: ring[:, slot, h, k * P:(k + 1) * P],
                                   lambda h: moving(h, k), k == 0, k == KD - 1)
                if used:
                    last.then_inc(unit_used, 1)

            def turn(t, src, bank):
                for k in range(KD):
                    last = nc.tensor.transpose(ps[:, bank + k // 4, (k % 4) * P:(k % 4 + 1) * P],
                                               src[:, k * P:(k + 1) * P], ident[:])
                return last

            from_u = lambda h, k: uT[:, h, k]

            pe.wait_ge(consts_ready, 2)
            for t in range(MT):
                pe.wait_ge(normed_ready, t + 1)
                turn(t, mem_in[:, t], 2 * t).then_inc(turned, 1)
            pe.wait_ge(turned_lo, MT)
            with pe.Fori(0, 2) as i:
                for s in range(4):
                    columns("mem_k", i, s, ps[:, 4 + s, 0:NM], lambda h, k: memT[:, h, k])

            def turn_x(t):
                pe.wait_ge(normed_ready, MT + t + 1)
                if t >= 2:
                    pe.wait_ge(turned_lo, MT + t - 1)
                turn(t, x_in[:, t], 2 * (t % 2)).then_inc(turned, 1)

            turn_x(0)
            turn_x(1)
            pe.wait_ge(mem_k_lo, KD)
            for k in range(KD):
                unit_ready("mem_v", 0, k)
                slot = units.slot("mem_v", k)
                for j in range(MT):
                    for h in range(2):
                        last = product(ps[:, 4 + 2 * j + h], lambda w: memT[:, w, k, j * P:(j + 1) * P],
                                       lambda w: ring[:, slot, w, h * T:(h + 1) * T], k == 0, k == KD - 1)
                    if k == KD - 1 and j == 0:
                        last.then_inc(mem_v_done, 1)
                last.then_inc(unit_used, 1)
                if k == 3:
                    turn_x(2)
                if k == 5:
                    turn_x(3)
            pe.wait_ge(turned_lo, MT + NT)
            columns("mem_v", 0, KD, ps[:, 0], from_u)

            pe.wait_ge(mem_v_lo, MT)
            pe.wait_ge(f_read, 1)

            def query(s):
                if s >= 2:
                    pe.wait_ge(mq_lo, s - 1)
                columns("mem_att", 0, s, ps[:, s % 2], from_u)

            def mem_scores(n):
                pe.wait_ge(mq_lo, 2 * n + 2)
                if n == 2:
                    pe.wait_ge(yc_lo, 2)
                if n == 3:
                    pe.wait_ge(ms_exp, 8)
                for t in range(NT):
                    dst = ps[:, MS_BANK[n] + t // 2, (t % 2) * NM:(t % 2 + 1) * NM]
                    for d in range(2):
                        last = product(dst, lambda w: mqT[:, 2 * (n % 2) + d, w, t * P:(t + 1) * P],
                                       lambda w: mem_k[:, w, 2 * n + d], d == 0, d == 1)
                last.then_inc(ms_done, 1)

            def mem_turn(n):
                pe.wait_ge(ms_p, 4 * n + 4)
                for j in range(MT):
                    if n:
                        pe.wait_ge(mt_lo, 2 * n - 1 + j)
                    for t in range(NT):
                        last = nc.tensor.transpose(ps[:, 6 + j, t * P:(t + 1) * P],
                                                   mem_p[:, n % 2, t, j * P:(j + 1) * P], ident[:])
                    last.then_inc(mt_done, 1)

            def mem_outputs(n):
                pe.wait_ge(mt_lo, 2 * n + 2)
                if n == 1:
                    pe.wait_ge(mq_lo, 8)
                for f in range(2):
                    for j in range(MT):
                        last = product(ps[:, MO_BANK[n] + f],
                                       lambda w: mem_v[:, w, j, n * NM + f * P:n * NM + (f + 1) * P],
                                       lambda w: mem_pT[n % 2][:, w, j], j == 0, j == MT - 1)
                    last.then_inc(yc_done, 1)

            def lru_in(s, i=0):
                columns("lru", i, s, ps[:, s], from_u)

            def lru_rest(i):
                if not (isinstance(i, int) and i == 0):
                    pe.wait_ge(merged_done, i)
                columns("lru", i, 2, ps[:, 4], lambda h, k: yc[:, h, k],
                        (lambda k: pe.wait_ge(yc_lo, k + 1)) if isinstance(i, int) else None)
                pe.wait_ge(xc_lo, i + 1)
                pe.wait_ge(wri_lo, i + 1)
                for n in range(2):
                    product(ps[:, 2 + n], lambda w: w_ri[:, w, n], lambda w: xcT[:, w], True, True).then_inc(ri_done, 1)

            for step in MEM_ORDER:
                if step == "l0":
                    pe.wait_ge(yc_lo, 4)
                {"q": query, "s": mem_scores, "t": mem_turn, "o": mem_outputs, "l": lru_in}[step[0]](int(step[1]))
            lru_rest(0)
            with pe.Fori(1, KD) as i:
                lru_in(0, i)
                lru_in(1, i)
                lru_rest(i)

            def merge(phase, b, banks, y, y_ready, y_count):
                with pe.Fori(0, KD // 2) as i:
                    for s in range(2):
                        pe.wait_ge(gate_ready, i * 2 + BEFORE[b])
                        columns(phase, i, s, ps[:, banks[s]], from_u)
                    pe.wait_ge(y_ready, y_count)
                    for s in range(2):
                        pe.wait_ge(merged_done, i * 2 + BEFORE[b])
                        columns(phase, i, 2 + s, ps[:, banks[2 + s]], lambda h, k: y[:, h, k])

            merge("merge_a", "a", (5, 6, 7, 4), ya, ya_lo, KD)

            pe.wait_ge(consts_rounded, 2)
            with pe.Fori(0, FOX_HEADS // 2) as i:
                def project(s, bank):
                    columns("fox", i, s, ps[:, bank], from_u)

                def scores(n):
                    for t in range(NT):
                        if n:
                            pe.wait_ge(fs_read, i * 8 + t + 1)
                        dst = ps[:, 2 + t, 0:(t + 1) * P]
                        product(dst, lambda w: qkT[:, 2 * n, w, t * P:(t + 1) * P],
                                lambda w: qkT[:, 2 * n + 1, w, 0:(t + 1) * P], True, False)
                        nc.tensor.matmul(ps[:, 2 + t, t * P:(t + 1) * P], identR[:], maskR[:],
                                         start=False, stop=True).then_inc(fs_done, 1)

                def values(g):
                    unit_ready("fox", i, 5)
                    slot = units.slot("fox", 4)
                    for h in range(2):
                        dst = ps[:, 6 + g, h * 2 * P:(h + 1) * 2 * P].rearrange("p (a n) -> p a n", a=2)
                        t = 2 * g + h
                        for k in range(KD):
                            last = product(dst, lambda w: uT[:, w, k, t * P:(t + 1) * P],
                                           lambda w: ring[:, slot:slot + 2, w, k * P:(k + 1) * P], k == 0, k == KD - 1)
                    if g == 0:
                        last.then_inc(v_done, 1)
                    else:
                        last.then_inc(unit_used, 2)

                def turn_p(n):
                    pe.wait_ge(fs_p, i * 8 + 4 * n + 4)
                    for g, keys in enumerate(TURNS):
                        if n == 0 and g == 2:
                            pe.wait_ge(v_lo, i * 2 + 1)
                        if n == 1 and g == 2:
                            pe.wait_ge(ft_lo, i * 6 + 1)
                        at_col = 0
                        for j in keys:
                            for t in range(j, NT):
                                last = nc.tensor.transpose(ps[:, TURN_BANK[n][g], at_col:at_col + P],
                                                           fox_p[:, n, ROW[t] + j * P:ROW[t] + (j + 1) * P], ident[:])
                                at_col += P
                        last.then_inc(ft_done, 1)

                def outputs(n, bank):
                    pe.wait_ge(v_lo, i * 2 + 2)
                    for g, keys in enumerate(TURNS):
                        pe.wait_ge(ft_lo, i * 6 + 3 * n + g + 1)
                        at_col = TURN_START[g]
                        for j in keys:
                            c = slice(at_col, at_col + (NT - j) * P)
                            last = product(ps[:, bank, j * P:T], lambda w: v_fox[:, w, j, n],
                                           lambda w: fox_pT[:, n, w, c], g == 0, g == len(TURNS) - 1)
                            at_col = c.stop
                    last.then_inc(yb_done, 1)

                project(0, 0)
                project(1, 1)
                pe.wait_ge(qk_lo, i * 4 + 1)
                project(2, 0)
                pe.wait_ge(qk_lo, i * 4 + 2)
                scores(0)
                project(3, 1)
                values(0)
                pe.wait_ge(qk_lo, i * 4 + 4)
                scores(1)
                turn_p(0)
                values(1)
                turn_p(1)
                outputs(0, 3)
                outputs(1, 2)

            merge("merge_b", "b", (4, 5, 6, 7), yb, yb_lo, FOX_HEADS)

            def rows_units(phase, i, s0, left, n_k, late, tile_done, before_unit, before_tile, between=None,
                           halves=False):
                def tile(k, t, banks=(0, 1)):
                    slot = units.slot(phase, s0 + k)
                    if k == 0:
                        before_tile(t)
                    for h in banks:
                        last = product(ps[:, 2 * t + h], lambda w: left(w, k, t),
                                       lambda w: ring[:, slot, w, h * T:(h + 1) * T], k == 0, k == n_k - 1)
                    return last

                for k in range(n_k - late):
                    before_unit(k)
                    unit_ready(phase, i, s0 + k)
                    for t in range(NT):
                        last = tile(k, t)
                    last.then_inc(unit_used, 1)
                for t in range(NT - 1 if halves else NT):
                    for k in range(n_k - late, n_k):
                        if between is not None:
                            between(t, k)
                        if t == 0:
                            before_unit(k)
                            unit_ready(phase, i, s0 + k)
                        last = tile(k, t)
                        if t == NT - 1:
                            last.then_inc(unit_used, 1)
                    if t < NT - 1:
                        last.then_inc(tile_done, 1)
                if halves:
                    for h in range(2):
                        for k in range(n_k - late, n_k):
                            last = tile(k, NT - 1, (h,))
                            if h == 1:
                                last.then_inc(unit_used, 1)
                        if h == 0:
                            last.then_inc(tile_done, 1)

            def turn_u2(t):
                pe.wait_ge(u2_ready, t + 1)
                turn(t, u2[:, t], 2 * t).then_inc(u2_turned, 1)

            def bank_evacuated(t):
                if t == 2:
                    pe.wait_ge(gate_ready, 3 * KD)
                if t == 3:
                    pe.wait_ge(mg_lo, KD)

            rows_units("w_o", 0, 0, lambda w, k, t: mgT[:, w, k, t * P:(t + 1) * P], KD, LATE_O,
                       wo_done, lambda k: pe.wait_ge(mg_lo, k + 1), bank_evacuated,
                       lambda t, k: turn_u2(k - (KD - 2)) if t == NT - 1 and k >= KD - 2 else None)
            def up(i, s, c=slice(0, T), used=True):
                columns("mlp", i, s, ps[:, s, c], lambda h, k: u2T[:, h, k, c], used=used)

            def down(i, halves=False):
                rows_units("mlp", i, 8, lambda w, k, t: actT[:, w, k, t * P:(t + 1) * P], 8, LATE_DOWN, down_done,
                           lambda k: pe.wait_ge(act_ready, i * 8 + k + 1),
                           lambda t: pe.wait_ge(act_ready, i * 8 + 2 * t + 2), halves=halves)

            HALF = (slice(0, T // 2), slice(T // 2, T))
            pe.wait_ge(pair_free, 2)
            up(0, 0, HALF[0], used=False)
            up(0, 1, HALF[0], used=False)
            turn_u2(2)
            up(0, 2, HALF[0], used=False)
            turn_u2(3)
            up(0, 3, HALF[0], used=False)
            pe.wait_ge(pair_free, NT)
            for s in range(4):
                up(0, s, HALF[1])
            for s in range(4, 8):
                up(0, s)
            down(0)
            def whole(i, final):
                for s in range(8):
                    pe.wait_ge(pair_free, i * 4 + s // 2 + 1)
                    up(i, s)
                down(i, halves=final)

            with pe.Fori(1, 3) as i:
                whole(i, False)
            whole(3, True)


_INS = ["x", "mem", "g_mix_pre", "w_in", "conv_w", "conv_b", "w_r", "b_r", "w_i", "b_i", "lru_lambda", "b_f",
        "g_mem", "w_mem_kv", "b_gate", "w_pa", "w_pb", "w_pc", "w_o", "g_mix_post", "g_mlp_pre", "w_up",
        "w_down", "g_mlp_post"]


def kernel(**inputs):
    import concourse.bacc as bacc
    from concourse.bass_utils import run_bass_kernel_spmd

    nc = bacc.Bacc("TRN2", target_bir_lowering=False, num_devices=1)
    arrays, args = {}, []
    for name in _INS:
        a = np.ascontiguousarray(inputs[name])
        arrays[f"in_{name}"] = a
        args.append(nc.dram_tensor(f"in_{name}", a.shape, mybir.dt.from_np(a.dtype), kind="ExternalInput").ap())
    args.append(nc.dram_tensor("out_y", (1, T, D), F32, kind="ExternalOutput").ap())
    block_program(nc, *args)
    r = run_bass_kernel_spmd(nc, [arrays], core_ids=[0])
    return r.results[0]["out_y"]
```
